# Optimizing a Trainium2 kernel written in Bass

```python
import jax
import jax.numpy as jnp
from jax import lax
import numpy as np

D_MODEL = 1024
BATCH = 1
SEQ = 512
DEPTH = 1

POOL_WINDOWS = (2, 4, 8, 16)
POOL_GROUPS = 4
POOL_GROUP_W = 128
POOL_W = POOL_GROUPS * POOL_GROUP_W
GLA_HEADS = 4
GLA_DK = 64
GLA_DV = 128
GLA_KEY = GLA_HEADS * GLA_DK
GLA_VAL = GLA_HEADS * GLA_DV
GATE_RANK = 16
GATE_NORMALIZER = 16.0
CHUNK = 64
MIX_W = POOL_W + GLA_VAL
IN_COLS = POOL_W + 2 * GLA_KEY + GLA_VAL + GATE_RANK + GLA_VAL
IN_SPLITS = (POOL_W,
             POOL_W + GLA_KEY,
             POOL_W + 2 * GLA_KEY,
             POOL_W + 2 * GLA_KEY + GLA_VAL,
             POOL_W + 2 * GLA_KEY + GLA_VAL + GATE_RANK)
MEM_LEN = 256
XATTN_HEADS = 4
XATTN_HD = D_MODEL // XATTN_HEADS
N_EXPERTS = 32
TOP_K = 4
D_FF = D_MODEL
SWIGLU_LIMIT = 7.0
SWIGLU_ALPHA = 1.702
MOE_BLOCK = 128
EPS = 1e-6

kernel_name = 'hybrid_pool_gla_xattn_moe_block'

def rms_norm(x, g):
    xf = x.astype(jnp.float32)
    y = xf * lax.rsqrt(jnp.mean(xf * xf, axis=-1, keepdims=True) + EPS)
    return (y * g.astype(jnp.float32)).astype(x.dtype)

def pool_mixer(u, w_pool, pool_scale):
    b, s, _ = u.shape
    uf = u.astype(jnp.float32).reshape(b, s, POOL_GROUPS, POOL_GROUP_W)
    cs = jnp.cumsum(uf, axis=1)
    pos = jnp.arange(s) + 1
    outs = []
    for gi, w in enumerate(POOL_WINDOWS):
        c = cs[:, :, gi]
        lag = jnp.pad(c, ((0, 0), (w, 0), (0, 0)))[:, :s]
        cnt = jnp.minimum(pos, w).astype(jnp.float32)[None, :, None]
        outs.append((c - lag) / cnt - uf[:, :, gi])
    p = jnp.stack(outs, axis=2).astype(u.dtype)
    y = jnp.einsum('bsgc,gcd->bsgd', p, w_pool).reshape(b, s, POOL_W)
    return y * pool_scale

def gla_mixer(q, k, v, g_lr, r, w_gate_up, b_gate_up, gla_norm_g):
    b, s, _ = q.shape
    n = s // CHUNK

    def chunked(a, d):
        return a.reshape(b, n, CHUNK, GLA_HEADS, d).transpose(0, 3, 1, 2, 4).astype(jnp.float32)

    g = jax.nn.log_sigmoid((g_lr @ w_gate_up + b_gate_up).astype(jnp.float32)) / GATE_NORMALIZER
    qc = chunked(q, GLA_DK) * (GLA_DK ** -0.5)
    kc = chunked(k, GLA_DK)
    vc = chunked(v, GLA_DV)
    gc = jnp.cumsum(chunked(g, GLA_DK), axis=3)
    qe = qc * jnp.exp(gc)
    ke = kc * jnp.exp(-gc)
    causal = jnp.tril(jnp.ones((CHUNK, CHUNK), dtype=bool))
    att = jnp.where(causal, jnp.einsum('bhnid,bhnjd->bhnij', qe, ke), 0.0)
    o = jnp.einsum('bhnij,bhnje->bhnie', att, vc)
    g_last = gc[:, :, :, -1]
    d_state = jnp.einsum('bhnjd,bhnje->bhnde',
                         kc * jnp.exp(g_last[:, :, :, None] - gc), vc)

    def step(state, inp):
        dec, ds = inp
        return dec[..., None] * state + ds, state

    init = jnp.zeros((b, GLA_HEADS, GLA_DK, GLA_DV), jnp.float32)
    _, s_prev = lax.scan(step, init,
                         (jnp.exp(g_last).transpose(2, 0, 1, 3),
                          d_state.transpose(2, 0, 1, 3, 4)))
    s_prev = s_prev.transpose(1, 2, 0, 3, 4)
    o = o + jnp.einsum('bhnid,bhnde->bhnie', qe, s_prev)
    o = o.transpose(0, 2, 3, 1, 4).reshape(b, s, GLA_HEADS, GLA_DV)
    o = o * lax.rsqrt(jnp.mean(o * o, axis=-1, keepdims=True) + EPS) * gla_norm_g.astype(jnp.float32)
    rf = jax.nn.silu(r.astype(jnp.float32)).reshape(b, s, GLA_HEADS, GLA_DV)
    return (o * rf).reshape(b, s, GLA_VAL).astype(q.dtype)

def memory_xattn(h, hm, w_xq, w_xk, w_xv, w_xo):
    b, s, _ = h.shape
    m = hm.shape[1]
    q = (h @ w_xq).reshape(b, s, XATTN_HEADS, XATTN_HD)
    k = (hm @ w_xk).reshape(b, m, XATTN_HEADS, XATTN_HD)
    v = (hm @ w_xv).reshape(b, m, XATTN_HEADS, XATTN_HD)
    sc = jnp.einsum('bshd,bmhd->bhsm', q, k).astype(jnp.float32) * (XATTN_HD ** -0.5)
    p = jax.nn.softmax(sc, axis=-1).astype(v.dtype)
    o = jnp.einsum('bhsm,bmhd->bshd', p, v).reshape(b, s, D_MODEL)
    return o @ w_xo

def clamped_swiglu(gu):
    gate = jnp.minimum(gu[..., :D_FF], SWIGLU_LIMIT)
    up = jnp.clip(gu[..., D_FF:], -SWIGLU_LIMIT, SWIGLU_LIMIT)
    return gate * jax.nn.sigmoid(SWIGLU_ALPHA * gate) * (up + 1.0)

def moe(h, w_router, b_router, w_gu, b_gu, w_dn, b_dn):
    b, s, d = h.shape
    n_tok = b * s
    t = h.reshape(n_tok, d)
    logits = (t @ w_router + b_router).astype(jnp.float32)
    top_val, top_idx = lax.top_k(logits, TOP_K)
    gates = jax.nn.softmax(top_val, axis=-1)
    n_assign = n_tok * TOP_K
    e_flat = top_idx.reshape(n_assign)
    tok_flat = jnp.repeat(jnp.arange(n_tok, dtype=jnp.int32), TOP_K)
    g_flat = gates.reshape(n_assign)
    order = jnp.argsort(e_flat)
    e_s = e_flat[order]
    tok_s = tok_flat[order]
    g_s = g_flat[order]
    counts = jnp.bincount(e_flat, length=N_EXPERTS)
    starts = jnp.cumsum(counts) - counts
    pcounts = (counts + MOE_BLOCK - 1) // MOE_BLOCK * MOE_BLOCK
    pends = jnp.cumsum(pcounts)
    pstarts = pends - pcounts
    dest = pstarts[e_s] + jnp.arange(n_assign) - starts[e_s]
    n_blocks = -(-n_assign // MOE_BLOCK) + N_EXPERTS
    n_rows = n_blocks * MOE_BLOCK
    tok_pad = jnp.zeros((n_rows,), jnp.int32).at[dest].set(tok_s)
    g_pad = jnp.zeros((n_rows,), jnp.float32).at[dest].set(g_s)
    blk_e = jnp.minimum(jnp.searchsorted(pends, jnp.arange(n_blocks) * MOE_BLOCK, side='right'),
                        N_EXPERTS - 1)

    def expert_block(args):
        tok_b, g_b, e = args
        xb = t[tok_b]
        a = clamped_swiglu((xb @ w_gu[e] + b_gu[e]).astype(jnp.float32)).astype(t.dtype)
        yb = a @ w_dn[e] + b_dn[e]
        return (yb.astype(jnp.float32) * g_b[:, None]).astype(t.dtype)

    y = lax.map(expert_block, (tok_pad.reshape(n_blocks, MOE_BLOCK),
                               g_pad.reshape(n_blocks, MOE_BLOCK), blk_e))
    out = jnp.zeros((n_tok, d), jnp.float32).at[tok_pad].add(
        y.reshape(n_rows, d).astype(jnp.float32))
    return out.reshape(b, s, d).astype(h.dtype)

def setup_inputs(seed: int = 0) -> dict:
    key = jax.random.key(seed)
    ks = jax.random.split(key, 24)
    L = DEPTH

    def nrm(k, shape, scale):
        return jax.random.normal(k, shape, jnp.float32) * scale

    return {
        'x': nrm(ks[0], (BATCH, SEQ, D_MODEL), 1.0),
        'mem': nrm(ks[1], (BATCH, MEM_LEN, D_MODEL), 1.0),
        'norm_mix_g': 1.0 + nrm(ks[2], (L, D_MODEL), 0.05),
        'w_in': nrm(ks[3], (L, D_MODEL, IN_COLS), D_MODEL ** -0.5),
        'w_pool': nrm(ks[4], (L, POOL_GROUPS, POOL_GROUP_W, POOL_GROUP_W), POOL_GROUP_W ** -0.5),
        'pool_scale': 1.0 + nrm(ks[5], (L, POOL_W), 0.1),
        'w_gate_up': nrm(ks[6], (L, GATE_RANK, GLA_KEY), GATE_RANK ** -0.5),
        'b_gate_up': nrm(ks[7], (L, GLA_KEY), 0.1),
        'gla_norm_g': 1.0 + nrm(ks[8], (L, GLA_DV), 0.05),
        'w_out': nrm(ks[9], (L, MIX_W, D_MODEL), MIX_W ** -0.5),
        'norm_xattn_g': 1.0 + nrm(ks[10], (L, D_MODEL), 0.05),
        'norm_mem_g': 1.0 + nrm(ks[11], (L, D_MODEL), 0.05),
        'w_xq': nrm(ks[12], (L, D_MODEL, D_MODEL), D_MODEL ** -0.5),
        'w_xk': nrm(ks[13], (L, D_MODEL, D_MODEL), D_MODEL ** -0.5),
        'w_xv': nrm(ks[14], (L, D_MODEL, D_MODEL), D_MODEL ** -0.5),
        'w_xo': nrm(ks[15], (L, D_MODEL, D_MODEL), D_MODEL ** -0.5),
        'norm_moe_g': 1.0 + nrm(ks[16], (L, D_MODEL), 0.05),
        'w_router': nrm(ks[17], (L, D_MODEL, N_EXPERTS), D_MODEL ** -0.5),
        'b_router': nrm(ks[18], (L, N_EXPERTS), 0.01),
        'w_gu': nrm(ks[19], (L, N_EXPERTS, D_MODEL, 2 * D_FF), D_MODEL ** -0.5),
        'b_gu': nrm(ks[20], (L, N_EXPERTS, 2 * D_FF), 0.01),
        'w_dn': nrm(ks[21], (L, N_EXPERTS, D_FF, D_MODEL), D_FF ** -0.5),
        'b_dn': nrm(ks[22], (L, N_EXPERTS, D_MODEL), 0.01),
        'norm_final_g': 1.0 + nrm(ks[23], (D_MODEL,), 0.05),
    }

def reference(x, mem, norm_mix_g, w_in, w_pool, pool_scale, w_gate_up, b_gate_up,
              gla_norm_g, w_out, norm_xattn_g, norm_mem_g, w_xq, w_xk, w_xv, w_xo,
              norm_moe_g, w_router, b_router, w_gu, b_gu, w_dn, b_dn, norm_final_g):
    for l in range(DEPTH):
        h = rms_norm(x, norm_mix_g[l])
        z = h @ w_in[l]
        u, q, k, v, g_lr, r = jnp.split(z, IN_SPLITS, axis=-1)
        mix = jnp.concatenate(
            [pool_mixer(u, w_pool[l], pool_scale[l]),
             gla_mixer(q, k, v, g_lr, r, w_gate_up[l], b_gate_up[l], gla_norm_g[l])],
            axis=-1)
        x = x + mix @ w_out[l]
        x = x + memory_xattn(rms_norm(x, norm_xattn_g[l]), rms_norm(mem, norm_mem_g[l]),
                             w_xq[l], w_xk[l], w_xv[l], w_xo[l])
        x = x + moe(rms_norm(x, norm_moe_g[l]), w_router[l], b_router[l],
                    w_gu[l], b_gu[l], w_dn[l], b_dn[l])
    return rms_norm(x, norm_final_g)


_drawn_inputs = setup_inputs


def setup_inputs(seed=0):
    import zlib

    import numpy as np

    out = dict(_drawn_inputs(seed))
    spreads = {}
    factors = {'norm_xattn_g': 3.564, 'b_gu': 8.0, 'b_dn': 8.0}
    for name, (base, spread) in spreads.items():
        noise = np.random.default_rng([zlib.crc32(name.encode()), seed]).standard_normal(out[name].shape)
        drawn = base * np.exp(spread * noise) if base else spread * noise
        out[name] = jnp.asarray(drawn.astype(out[name].dtype))
    for name, factor in factors.items():
        out[name] = (out[name] * factor).astype(out[name].dtype)
    return out
```

```python
from contextlib import ExitStack

import concourse.bass as bass
from concourse import mybir

F32 = mybir.dt.float32
BF16 = mybir.dt.bfloat16
I32 = mybir.dt.int32
U32 = mybir.dt.uint32
ALU = mybir.AluOpType
ACT = mybir.ActivationFunctionType
AX = mybir.AxisListType

P = 128
EPS = 1e-6
WINDOWS = (2, 4, 8, 16)
PAD = 16
GATE_NORMALIZER = 16.0
SWIGLU_LIMIT = 7.0
SWIGLU_ALPHA = 1.702
CHUNK = 64
SUB = 32
NSUB = P // SUB
NCOL = P // SUB


def job_order():
    o = [("xt", t, h) for t in range(4) for h in range(2)]
    o += [("glr",), ("k", 0), ("k", 1), ("q", 0), ("q", 1)]
    o += [("v", t) for t in range(4)]
    o += [("gate", 0), ("gate", 1)]
    o += [("u", g) for g in range(4)]
    o += [("r", h) for h in range(4)]
    o += [("mt", t, h) for t in range(2) for h in range(2)]
    o += [("kd", 0), ("kd", 1)]
    o += [("ds", p, c) for p in range(2) for c in range(2)]
    o += [("K", c) for c in range(4)]
    o += [("att", h) for h in range(4)]
    o += [("pool", g) for g in range(4)]
    o += [("o", h) for h in range(4)]
    o += [("V", m, n) for m in range(2) for n in range(2)]
    o += [("ss", h) for h in range(4)]
    o += [("x1", t, n) for t in range(4) for n in range(2)]
    o += [("h2t", t, h) for t in range(4) for h in range(2)]
    o += [("Q", f) for f in range(8)]
    o += [("sc", h, a) for h in range(4) for a in range(2)]
    o += [("pt", h, m) for h in range(4) for m in range(2)]
    o += [("O", h, c) for h in range(4) for c in range(2)]
    o += [("x2", t, n) for t in range(4) for n in range(2)]
    o += [("h3t", t, h) for t in range(4) for h in range(2)]
    o += [("lg",), ("rank",), ("tab",), ("meta",)]
    return o


ORDER = job_order()
JOB = {name: n for n, name in enumerate(ORDER)}


def decoder_layer(nc, a, out):
    T, D = a["x"].shape[1:]
    M = a["mem"].shape[1]
    E = a["w_gu"].shape[1]
    F = a["w_dn"].shape[2]
    TT, KD, KF, MT = T // P, D // P, F // P, M // P
    TOPK = 4
    assert TT == NSUB
    MAX_EXTRA = T * TOPK // (P + 1)
    NBLK = E + MAX_EXTRA
    NB = NBLK + 1
    GK = 2
    NG = KD // GK
    FQ, DQ = F // NCOL, D // NCOL

    x_d = a["x"].rearrange("o (t p) d -> p (o t) d", p=P)
    mem_d = a["mem"].rearrange("o (t p) d -> p (o t) d", p=P)
    out_d = out.rearrange("o (t p) d -> p (o t) d", p=P)
    w_in_d = a["w_in"].rearrange("o (k p) n -> p (o k) n", p=P)
    wsq = {n: a[n].rearrange("o (k p) n -> p (o k) n", p=P) for n in ("w_out", "w_xq", "w_xk", "w_xv", "w_xo")}
    h3_d = nc.dram_tensor("h3_rows", (T, D), F32).ap()
    acc_d = nc.dram_tensor("acc_rows", (T * NCOL, DQ), F32).ap()
    acc_tok = acc_d.rearrange("(t p j) d -> p t (j d)", p=P, j=NCOL)
    h3_tok = h3_d.rearrange("(t p) d -> p t d", p=P)

    with ExitStack() as ctx:
        def sb(name, shape, dt=F32):
            return ctx.enter_context(nc.sbuf_tensor(name, shape, dt))

        def sem(name):
            return ctx.enter_context(nc.semaphore(name))

        W = sb("weights", [P, 3 * 8192])
        x_sb = sb("x_sb", [P, TT, D])
        nrm = sb("nrm", [P, 4096])
        hT = sb("hT", [P, KD, T])
        mixT = sb("mixT", [P, KD, T])
        qreg = sb("qreg", [P, 4096])
        KT = sb("KT", [P, KD, M])
        V = sb("V", [P, MT, D])
        pool_s = sb("pool_s", [P, 2, PAD + T])
        gbc = sb("gbc", [P, D])

        ident = sb("ident", [P, P])
        ones = sb("ones", [P, P])
        causal = sb("causal", [P, P])
        before = sb("before", [P, P], BF16)
        ones_b = sb("ones_b", [P, P], BF16)
        w_pool = sb("w_pool_sb", [P, 4, P])
        w_gate = sb("w_gate_sb", [16, 256])
        w_rt = sb("w_router_sb", [P, KD, E])
        b_rt = sb("b_router_sb", [P, E])
        cols = sb("cols", [P, 8])
        stat = sb("stat", [P, 3, 24])
        inv_cnt = sb("inv_cnt", [P, PAD])
        eps_c = sb("eps_c", [P, 1])
        pool_end = sb("pool_end", [1, 2])
        soft = sb("soft", [P, 4, 16])
        sel = sb("sel", [P, SUB], BF16)
        ctl = sb("ctl", [1, 2, 64], I32)
        cur_i = sb("cur_i", [P, 8], I32)
        cur_g = sb("cur_g", [P, 4])

        w_in_cols = a["w_in"].shape[2]
        assert w_in_cols == 2064
        R0, R1, R2 = W[:, 0:8192], W[:, 8192:16384], W[:, 16384:24576]
        w_u = R0[:, 0:4096].rearrange("p (k n) -> p k n", k=KD)
        w_qk = R0[:, 4096:8192].rearrange("p (k n) -> p k n", k=KD)
        w_v = R1[:, 0:4096].rearrange("p (k n) -> p k n", k=KD)
        w_r = R1[:, 4096:8192].rearrange("p (k n) -> p k n", k=KD)
        sq = [R[:, :].rearrange("p (k n) -> p k n", k=KD) for R in (R0, R1, R2)]
        w_xk, w_out, w_xo = sq[0], sq[0], sq[0]
        w_xv = sq[1]
        w_xq = sq[2]
        u_sb = R2[:, 0:2112].rearrange("p (g n) -> p g n", g=4)
        qg = R2[:, 2112:3136].rearrange("p (a n) -> p a n", a=2)
        kg = R2[:, 3136:4160].rearrange("p (a n) -> p a n", a=2)
        sig_r = R2[:, 2112:4160].rearrange("p (h n) -> p h n", h=4)
        gc = R2[:, 4160:5184].rearrange("p (a n) -> p a n", a=2)
        v_sb = R2[:, 5184:7232].rearrange("p (t n) -> p t n", t=4)
        glr = R2[0:16, 7232:7744]
        w_lr = R2[:, 7744:7872].rearrange("p (k n) -> p k n", k=KD)
        qe = qreg[:, 0:1024].rearrange("p (a n) -> p a n", a=2)
        ke = qreg[:, 1024:2048].rearrange("p (a n) -> p a n", a=2)
        kd = qreg[:, 2048:3072].rearrange("p (a n) -> p a n", a=2)
        gtmp = qreg[:, 3072:4096].rearrange("p (a n) -> p a n", a=2)
        kd_tok = qreg[:, 3072:4096].rearrange("p (a t d) -> p a t d", a=2, t=4)
        QT = qreg[:, :].rearrange("p (f n) -> p f n", f=8)
        hflat = hT[:, :, :].rearrange("p k n -> p (k n)")
        att = hflat[:, 0:2048].rearrange("p (h t i) -> p h t i", h=4, t=4)
        S_prev = hflat[:, 2048:4096].rearrange("p (a c e) -> p a c e", a=2, c=8)
        pT = hflat.rearrange("p (h m n) -> p h m n", h=4, m=2)
        nrm_t = nrm[:, :].rearrange("p (t d) -> p t d", t=4)
        hmT = nrm[:, 2048:4096].rearrange("p (k m) -> p k m", k=KD)
        o_sb = nrm[:, 0:2048].rearrange("p (h n) -> p h n", h=4)
        prob = nrm[:, :].rearrange("p (h t m) -> p h t m", h=4, t=4)

        def rt(lo, n):
            return qreg[:, lo:lo + n]
        logits = rt(0, 128).rearrange("p (t e) -> p t e", t=4)
        top8 = rt(128, 32).rearrange("p (t k) -> p t k", t=4)
        idx8 = rt(160, 32).bitcast(U32).rearrange("p (t k) -> p t k", t=4)
        idxf = rt(192, 16).rearrange("p (t k) -> p t k", t=4)
        gate4 = rt(208, 16).rearrange("p (t k) -> p t k", t=4)
        gsum = rt(224, 8)
        oh = rt(256, 512).rearrange("p (k t e) -> p k t e", k=4, t=4)
        maskf = rt(768, 128).rearrange("p (t e) -> p t e", t=4)
        maskb = rt(896, 64).bitcast(BF16).rearrange("p (t e) -> p t e", t=4)
        rank = rt(960, 160).rearrange("p (t e) -> p t e", t=5)
        blk_t = rt(1120, 128).rearrange("p (t e) -> p t e", t=4)
        lvl = rt(1248, 4 * 32).rearrange("p (a e) -> p a e", a=4)
        xend = rt(1376, 32)
        xoff = rt(1408, 32)
        pos16 = rt(1440, 16).rearrange("p (k t) -> p k t", k=4)
        blk16 = rt(1456, 16).rearrange("p (k t) -> p k t", k=4)
        junk = rt(1472, 64)
        onehot_p = rt(1536, 512).rearrange("p (a s) -> p a s", a=4)
        vals = rt(2048, 4 * 2 * NB).rearrange("p (a c b) -> p a c b", a=4, c=2)
        iota_b = rt(2432, NB)
        tokp = rt(2480, 4)
        spread = rt(2496, 512).rearrange("p (s j r) -> p s (j r)", s=4, j=4)
        iota_p = rt(3008, 128)
        gidx = rt(3136, NB)
        tabv = rt(3184, 2 * NB).rearrange("p (c b) -> p c b", c=2)
        meta = rt(3280, 8 * NB).rearrange("p (s c b) -> p s c b", s=4, c=2)
        iota_e = rt(3664, 32)
        ebc = rt(3696, NB)
        row_e = rt(3744, 1)
        pcol = rt(3746, 1)
        jcol = rt(3745, 1)
        nsubf = rt(3780, NB)
        xcmp = rt(3828, 32)
        bias3 = KT[:, 0:6, :].rearrange("p k n -> p (k n)").bitcast(BF16)
        b_all = hflat[:, 0:3072]
        assert NB == 48 and 2 * F + D == 3072
        xg = nrm[:, 0:1024]
        a_sb = nrm[:, 1024:2048].rearrange("p (s n) -> p s n", s=4)
        y_sb = nrm[:, 2048:3072].rearrange("p (s n) -> p s n", s=4)
        up_sb = nrm[:, 3072:4096].rearrange("p (s n) -> p s n", s=4)
        xT = hflat[:, 0:1024].rearrange("p (k n) -> p k n", k=8)
        aT = hflat[:, 1024:2048].rearrange("p (s c n) -> p s c n", s=4, c=2)
        gm_sb = hflat[:, 2048:3072].rearrange("p (s n) -> p s n", s=4)
        sg_sb = hflat[:, 3072:4096].rearrange("p (s n) -> p s n", s=4)
        wg = W[:, 0:16384].rearrange("p (k h n) -> p k h n", k=KD, h=2)
        wd = W[:, 16384:24576].rearrange("p (k n) -> p k n", k=KF)

        PS = [ctx.enter_context(nc.psum_tensor(f"bank{i}", [P, 512], F32)) for i in range(8)]

        bank_full = [sem(f"bank_full{i}") for i in range(8)]
        bank_free = [sem(f"bank_free{i}") for i in range(8)]
        x_in = [sem("x_in0"), sem("x_in1")]
        mem_in, small_in, g_in, consts = sem("mem_in"), sem("small_in"), sem("g_in"), sem("consts")
        w_landed = {n: sem(f"landed_{n}") for n in ("qk", "lr", "v", "u", "r", "w_xk", "w_xv", "w_out", "w_xq", "w_xo")}
        g_used = sem("g_used")
        sq_sum = sem("sq_sum")
        normed = sem("normed")
        gl = sem("gate_logs")
        gd = sem("gate_dve")
        kd_ready, pooled, states, osq_ready, mixed = sem("kd_ready"), sem("pooled"), sem("states"), sem("osq_ready"), sem("mixed")
        sig_ready = sem("sig_ready")
        maxed, exped, prob_ready = sem("maxed"), sem("exped"), sem("prob_ready")
        act_step, dve_step, pool_step = sem("act_step"), sem("dve_step"), sem("pool_step")
        h3_out = sem("h3_out")
        top_ready, gate_exp, mask_ready, vals_ready, vals_used = sem("top_ready"), sem("gate_exp"), sem("mask_ready"), sem("vals_ready"), sem("vals_used")
        tables_ready = sem("tables_ready")
        bias_in, bias_ready = sem("bias_in"), sem("bias_ready")
        gu_in = [sem(f"gu_in{g}") for g in range(NG)]
        dn_in = [sem(f"dn_in{g}") for g in range(NG)]
        gu_used, dn_used = sem("gu_used"), sem("dn_used")
        row_picked, sel_ready, gathered, xt_full, xT_ready = sem("row_picked"), sem("sel_ready"), sem("gathered"), sem("xt_full"), sem("xT_ready")
        gu_full, gate_min, sig_done, a_ready = sem("gu_full"), sem("gate_min"), sem("sig_done"), sem("a_ready")
        at_full, aT_ready, dn_full, y_ready, added = sem("at_full"), sem("aT_ready"), sem("dn_full"), sem("y_ready"), sem("added")
        moe_step = sem("moe_step")
        all_added, final_in, out_done = sem("all_added"), sem("final_in"), sem("out_done")

        block = ctx.enter_context(nc.Block())

        def full(eng, *job):
            n = JOB[job]
            eng.wait_ge(bank_full[n % 8], n // 8 + 1)
            return PS[n % 8]

        def freed(job):
            return bank_free[JOB[job] % 8]

        def evacuated(eng, *job):
            n = JOB[job]
            eng.wait_ge(bank_free[n % 8], n // 8 + 1)

        NORMS = [("x", t) for t in range(TT)] + [("mem", t) for t in range(MT)] + [("x1", t) for t in range(TT)] + \
                [("x2", t) for t in range(TT)] + [("out", t) for t in range(TT)]
        NORM = {n: i for i, n in enumerate(NORMS)}

        G_LOADS = ["norm_mix_g", "norm_mem_g", "norm_xattn_g", "norm_moe_g", "norm_final_g"]

        @block.sync
        def _(sp):
            def load_g(i):
                if i:
                    sp.wait_ge(g_used, i)
                src = a[G_LOADS[i]]
                src = src if i < 4 else src.rearrange("(o d) -> o d", o=1)
                sp.dma_start(gbc[:, :], src.to_broadcast([P, D])).then_inc(g_in, 16)

            sp.dma_start(x_sb[:, 0:2, :], x_d[:, 0:2, :]).then_inc(x_in[0], 16)
            load_g(0)
            sp.dma_start(w_lr, w_in_d[:, :, 1536:1552], allow_slow_non_contiguous=True).then_inc(w_landed["lr"], 16)
            sp.dma_start(x_sb[:, 2:4, :], x_d[:, 2:4, :]).then_inc(x_in[1], 16)
            sp.dma_start(w_qk, w_in_d[:, :, 512:1024]).then_inc(w_landed["qk"], 16)
            sp.dma_start(w_v, w_in_d[:, :, 1024:1536]).then_inc(w_landed["v"], 16)
            sp.dma_start(w_u, w_in_d[:, :, 0:512]).then_inc(w_landed["u"], 16)
            sp.dma_start(w_r, w_in_d[:, :, 1552:2064]).then_inc(w_landed["r"], 16)
            for n in range(4):
                if n % 2:
                    evacuated(sp, "xt", 3, n // 2)
            sp.dma_start(V[:, :, :], mem_d).then_inc(mem_in, 16)
            load_g(1)
            full(sp, "u", 3)
            sp.dma_start(w_xk, wsq["w_xk"]).then_inc(w_landed["w_xk"], 16)
            full(sp, "r", 3)
            sp.dma_start(w_xv, wsq["w_xv"]).then_inc(w_landed["w_xv"], 16)
            load_g(2)
            full(sp, "K", 3)
            sp.dma_start(w_out, wsq["w_out"]).then_inc(w_landed["w_out"], 16)
            sp.wait_ge(mixed, 4)
            evacuated(sp, "pool", 3)
            full(sp, "o", 3)
            sp.dma_start(w_xq, wsq["w_xq"]).then_inc(w_landed["w_xq"], 16)
            load_g(3)
            full(sp, "x1", 3, 1)
            sp.dma_start(w_xo, wsq["w_xo"]).then_inc(w_landed["w_xo"], 16)
            full(sp, "Q", 7)
            for g in range(NG):
                sp.dma_start(wd[:, GK * g:GK * g + GK, :],
                             a["w_dn"][0, 0].rearrange("(k p) n -> p k n", p=P)[:, GK * g:GK * g + GK, :]).then_inc(dn_in[g], 16)
            for g in range(NG // 2, NG):
                sp.dma_start(wg[:, GK * g:GK * g + GK].rearrange("p k h n -> p k (h n)"),
                             a["w_gu"][0, 0].rearrange("(k p) n -> p k n", p=P)[:, GK * g:GK * g + GK, :]).then_inc(gu_in[g], 16)
            full(sp, "x2", 3, 1)
            for g in range(NG // 2):
                sp.dma_start(wg[:, GK * g:GK * g + GK].rearrange("p k h n -> p k (h n)"),
                             a["w_gu"][0, 0].rearrange("(k p) n -> p k n", p=P)[:, GK * g:GK * g + GK, :]).then_inc(gu_in[g], 16)
            sp.wait_ge(tables_ready, 1)
            blocks = sp.value_load(ctl[0:1, 1, 63:64], min_val=E, max_val=NBLK)
            with sp.Fori(1, NBLK) as b:
                with sp.If(b < blocks):
                    e = sp.value_load(ctl[0:1, 1, bass.ds(b, 1)], min_val=0, max_val=E - 1)
                    w_gu_e = a["w_gu"][0, bass.ds(e, 1)].rearrange("o (k p) n -> p (o k) n", p=P)
                    w_dn_e = a["w_dn"][0, bass.ds(e, 1)].rearrange("o (k p) n -> p (o k) n", p=P)
                    for g in range(NG):
                        sp.wait_ge(gu_used, NG * b - NG + g + 1)
                        sp.dma_start(wg[:, GK * g:GK * g + GK].rearrange("p k h n -> p k (h n)"),
                                     w_gu_e[:, GK * g:GK * g + GK, :]).then_inc(gu_in[g], 16)
                    for g in range(NG):
                        sp.wait_ge(dn_used, NG * b - NG + g + 1)
                        sp.dma_start(wd[:, GK * g:GK * g + GK, :],
                                     w_dn_e[:, GK * g:GK * g + GK, :]).then_inc(dn_in[g], 16)
            sp.wait_ge(all_added, 1)
            load_g(4)
            sp.dma_start(x_sb[:, :, :], acc_tok).then_inc(final_in, 16)

        @block.scalar
        def _(act):
            steps = [0]

            def step(ins):
                steps[0] += 1
                ins.then_inc(act_step, 1)
                act.wait_ge(act_step, steps[0])

            act.dma_start(cols[:, 0:4], a["pool_scale"].rearrange("o (g p) -> p (o g)", p=P),
                          allow_slow_non_contiguous=True).then_inc(small_in, 16)
            act.dma_start(cols[:, 4:6], a["b_gate_up"].rearrange("o (g p) -> p (o g)", p=P),
                          allow_slow_non_contiguous=True).then_inc(small_in, 16)
            act.dma_start(cols[:, 6:7], a["gla_norm_g"].rearrange("o p -> p o"),
                          allow_slow_non_contiguous=True).then_inc(small_in, 16)
            act.dma_start(w_gate[:, :], a["w_gate_up"][0]).then_inc(small_in, 16)
            act.dma_start(w_pool[:, :, :], a["w_pool"][0].rearrange("g c d -> c g d")).then_inc(small_in, 16)
            act.dma_start(w_rt[:, :, :], a["w_router"][0].rearrange("(k p) e -> p k e", p=P)).then_inc(small_in, 16)
            act.dma_start(b_rt[:, :], a["b_router"].to_broadcast([P, E])).then_inc(small_in, 16)

            def squares(name, t, src, dst):
                n = NORM[name, t]
                step(act.activation(dst, src, ACT.Square, scale=float(D) ** -0.5, accum_out=stat[:, 0, n:n + 1]))
                act.activation(stat[:, 1, n:n + 1], stat[:, 0, n:n + 1], ACT.Sqrt, bias=eps_c[:, 0:1]).then_inc(sq_sum, 1)

            def copy_bank(job, dst, src=None, **kw):
                ps = full(act, *job)
                act.activation(dst, ps[:, :] if src is None else src(ps), ACT.Copy, **kw).then_inc(freed(job), 1)

            act.wait_ge(consts, 4)
            for t in range(TT):
                act.wait_ge(x_in[t // 2], 16)
                squares("x", t, x_sb[:, t, :], nrm_t[:, t, :])
            for t in range(TT):
                copy_bank(("xt", t, 1), hT[:, 4:8, t * P:t * P + P], lambda ps: ps[:, :].rearrange("p (k n) -> p k n", k=4))
            act.wait_ge(mem_in, 16)
            copy_bank(("glr",), glr, lambda ps: ps[0:16, :])
            for i in range(2):
                evacuated(act, "xt", 1, 0)
                squares("mem", i, V[:, i, :], nrm_t[:, i, :])
            copy_bank(("k", 1), kg[:, 1, :])
            copy_bank(("q", 1), qg[:, 1, :], scale=float(CHUNK) ** -0.5)
            copy_bank(("v", 1), v_sb[:, 1, :])
            copy_bank(("v", 3), v_sb[:, 3, :])
            for p in range(2):
                act.wait_ge(gd, 2 * p + 1)
                step(act.activation(gtmp[:, p, :], gtmp[:, p, :], ACT.Exp, scale=-1.0))
                act.activation(gtmp[:, p, :], gtmp[:, p, :], ACT.Ln, bias=1.0).then_inc(gl, 1)
            for p in range(2):
                act.wait_ge(gd, 4 + p + 1)
                act.activation(qe[:, p, :], gc[:, p, :], ACT.Exp).then_inc(gl, 1)
                act.activation(ke[:, p, :], gc[:, p, :], ACT.Exp, scale=-1.0).then_inc(gl, 1)
                for c in range(8):
                    last = gc[:, p, c * CHUNK + CHUNK - 1:c * CHUNK + CHUNK]
                    act.activation(kd[:, p, c * CHUNK:(c + 1) * CHUNK], gc[:, p, c * CHUNK:(c + 1) * CHUNK], ACT.Exp,
                                   scale=-1.0, bias=last).then_inc(gl, 1)
            for g in (1, 3):
                copy_bank(("u", g), u_sb[:, g, PAD:])
            for h in range(4):
                copy_bank(("r", h), mixT[:, 4 + h, :])
            for h in range(4):
                if h == 0:
                    act.wait_ge(kd_ready, 6)
                evacuated(act, "r", h)
                act.activation(sig_r[:, h, :], mixT[:, 4 + h, :], ACT.Sigmoid).then_inc(sig_ready, 1)
            for t in range(2):
                evacuated(act, "r", 3)
                copy_bank(("mt", t, 1), hmT[:, 4:8, t * P:t * P + P], lambda ps: ps[:, :].rearrange("p (k n) -> p k n", k=4))
            copy_bank(("kd", 1), kd_tok[:, 1, :, :].rearrange("p t d -> p (t d)"))
            for c in range(4):
                copy_bank(("K", c), KT[:, 2 * c:2 * c + 2, :], lambda ps: ps[:, :].rearrange("p (a n) -> p a n", a=2))
            for g in range(4):
                ps = full(act, "pool", g)
                if g == 0:
                    act.wait_ge(small_in, 16 * 7)
                act.activation(mixT[:, g, :], ps[:, :], ACT.Copy, scale=cols[:, g:g + 1]).then_inc(freed(("pool", g)), 1)
            for h in range(4):
                evacuated(act, "o", h)
                if h >= 2:
                    full(act, "ss", h - 2)
                elif h == 0:
                    act.wait_ge(pooled, 4)
                act.activation(pool_s[:, h % 2, 0:T], o_sb[:, h, :], ACT.Square).then_inc(osq_ready, 1)
            for m in range(2):
                copy_bank(("V", m, 1), V[:, m, 512:1024])
            for h in range(4):
                ps = full(act, "ss", h)
                if h:
                    act.wait_ge(mixed, h)
                act.activation(gc[:, 0, :], ps[:, :], ACT.Sqrt, bias=eps_c[:, 0:1]).then_inc(freed(("ss", h)), 1)
            for t in range(TT):
                evacuated(act, "x1", t, 0)
                evacuated(act, "x1", t, 1)
                if t == 0:
                    for m in range(2):
                        evacuated(act, "V", m, 1)
                    full(act, "V", 1, 1)
                    act.wait_ge(mixed, 4)
                squares("x1", t, x_sb[:, t, :], nrm_t[:, t, :])
            for t in range(TT):
                copy_bank(("h2t", t, 1), hT[:, 4:8, t * P:t * P + P], lambda ps: ps[:, :].rearrange("p (k n) -> p k n", k=4))
            for f in range(8):
                copy_bank(("Q", f), QT[:, f, :], scale=float(D // 4) ** -0.5)
            for h in range(4):
                for t in range(4):
                    act.wait_ge(maxed, 4 * h + 2 * (t // 2) + 2)
                    ps = full(act, "sc", h, t // 2)
                    if h == t == 0:
                        evacuated(act, "h2t", 3, 0)
                        evacuated(act, "h2t", 3, 1)
                    act.activation(prob[:, h, t, :], ps[:, (t % 2) * M:(t % 2) * M + M], ACT.Exp,
                                   bias=soft[:, 0, 4 * h + t:4 * h + t + 1],
                                   accum_out=soft[:, 1, 4 * h + t:4 * h + t + 1]).then_inc(exped, 1)
            for h in range(4):
                copy_bank(("pt", h, 1), pT[:, h, 1, :])
                copy_bank(("O", h, 1), mixT[:, 2 * h + 1, :])
            for t in range(TT):
                evacuated(act, "x2", t, 0)
                evacuated(act, "x2", t, 1)
                if t == 0:
                    for h in range(4):
                        for m in range(2):
                            evacuated(act, "pt", h, m)
                squares("x2", t, x_sb[:, t, :], nrm_t[:, t, :])
            act.wait_ge(bias_ready, 2)
            for t in range(TT):
                copy_bank(("h3t", t, 1), hT[:, 4:8, t * P:t * P + P], lambda ps: ps[:, :].rearrange("p (k n) -> p k n", k=4))
            act.wait_ge(top_ready, 1)
            for t in range(TT):
                act.activation(gate4[:, t, :], top8[:, t, 0:4], ACT.Exp, bias=gsum[:, t:t + 1],
                               accum_out=gsum[:, 4 + t:5 + t]).then_inc(gate_exp, 1)

            act.wait_ge(tables_ready, 1)
            blocks = act.value_load(ctl[0:1, 1, 63:64], min_val=E, max_val=NBLK)
            with act.Fori(0, NBLK) as b:
                with act.If(b < blocks):
                    act.wait_ge(xt_full, b + 1)
                    for i in range(2):
                        act.activation(xT[:, 4 * i:4 * i + 4, :], PS[i][:, :].rearrange("p (k n) -> p k n", k=4),
                                       ACT.Copy).then_inc(xT_ready, 1)
                    for i in range(2):
                        act.wait_ge(gate_min, 2 * b + i + 1)
                        act.activation(sg_sb[:, 2 * i:2 * i + 2, :], gm_sb[:, 2 * i:2 * i + 2, :], ACT.Sigmoid,
                                       scale=SWIGLU_ALPHA).then_inc(sig_done, 1)
                    for s in range(NSUB):
                        act.wait_ge(at_full, NSUB * b + s + 1)
                        act.activation(aT[:, s, :, :].rearrange("p c n -> p (c n)"), PS[4 + s][:, 0:256],
                                       ACT.Copy).then_inc(aT_ready, 1)
            for t in range(TT):
                act.wait_ge(final_in, 16)
                squares("out", t, x_sb[:, t, :], nrm_t[:, t, :])
            for t in range(TT):
                act.wait_ge(normed, NORM["out", t] + 1)
                act.dma_start(out_d[:, t, :], nrm_t[:, t, :]).then_inc(out_done, 16)
            act.wait_ge(out_done, 16 * TT)

        @block.tensor
        def _(pe):
            def bank(*job):
                n = JOB[job]
                if n >= 8:
                    pe.wait_ge(bank_free[n % 8], n // 8)
                return PS[n % 8]

            def fills(job):
                return bank_full[JOB[job] % 8]

            def turn(job, src, width=P):
                ps = bank(*job)
                for i in range(4):
                    last = pe.transpose(ps[:, i * P:(i + 1) * P], src(i), ident[:, :])
                last.then_inc(fills(job), 1)

            def product(job, lhsT, rhs, n, width=512, rows=P, finish=True):
                ps = bank(*job)
                for k in range(n):
                    last = pe.matmul(ps[0:rows, 0:width], lhsT(k), rhs(k), start=(k == 0), stop=(k == n - 1))
                return last.then_inc(fills(job), 1)

            pe.wait_ge(consts, 4)
            for t in range(TT):
                pe.wait_ge(normed, NORM["x", t] + 1)
                for h in range(2):
                    turn(("xt", t, h), lambda i: nrm_t[:, t, (4 * h + i) * P:(4 * h + i + 1) * P])
            for t in range(TT):
                for h in range(2):
                    evacuated(pe, "xt", t, h)
            pe.wait_ge(w_landed["lr"], 16)
            product(("glr",), lambda k: w_lr[:, k, :], lambda k: hT[:, k, :], KD, rows=16)
            pe.wait_ge(w_landed["qk"], 16)
            for n in range(2):
                product(("k", n), lambda k: w_qk[:, k, 256 + n * P:256 + (n + 1) * P], lambda k: hT[:, k, :], KD)
            for n in range(2):
                product(("q", n), lambda k: w_qk[:, k, n * P:(n + 1) * P], lambda k: hT[:, k, :], KD)
            pe.wait_ge(w_landed["v"], 16)
            for t in range(TT):
                product(("v", t), lambda k: hT[:, k, t * P:(t + 1) * P], lambda k: w_v[:, k, :], KD)
            evacuated(pe, "glr")
            pe.wait_ge(small_in, 16 * 7)
            for n in range(2):
                product(("gate", n), lambda k: w_gate[:, n * P:(n + 1) * P], lambda k: glr, 1)
            pe.wait_ge(w_landed["u"], 16)
            for g in range(4):
                product(("u", g), lambda k: w_u[:, k, g * P:(g + 1) * P], lambda k: hT[:, k, :], KD)
            pe.wait_ge(w_landed["r"], 16)
            for h in range(4):
                product(("r", h), lambda k: w_r[:, k, h * P:(h + 1) * P], lambda k: hT[:, k, :], KD)
            for t in range(2):
                pe.wait_ge(normed, NORM["mem", t] + 1)
                for h in range(2):
                    turn(("mt", t, h), lambda i: nrm_t[:, t, (4 * h + i) * P:(4 * h + i + 1) * P])
            pe.wait_ge(kd_ready, 6)
            for p in range(2):
                ps = bank("kd", p)
                for t in range(4):
                    last = pe.transpose(ps[:, t * P:(t + 1) * P], kd[:, p, t * P:(t + 1) * P], ident[:, :])
                last.then_inc(fills(("kd", p)), 1)
            for t in range(4):
                evacuated(pe, "v", t)
            for p in range(2):
                evacuated(pe, "kd", p)
                for c in range(2):
                    ps = bank("ds", p, c)
                    for t in range(4):
                        for h in range(2):
                            last = pe.matmul(ps[64 * h:64 * h + 64, t * P:(t + 1) * P],
                                             kd_tok[64 * c:64 * c + 64, p, t, 64 * h:64 * h + 64],
                                             v_sb[64 * c:64 * c + 64, t, (2 * p + h) * P:(2 * p + h + 1) * P],
                                             start=True, stop=True)
                    last.then_inc(fills(("ds", p, c)), 1)
            for t in range(2):
                for h in range(2):
                    evacuated(pe, "mt", t, h)
            pe.wait_ge(w_landed["w_xk"], 16)
            for c in range(4):
                ps = bank("K", c)
                for f in range(2):
                    for k in range(KD):
                        last = pe.matmul(ps[:, f * M:(f + 1) * M], w_xk[:, k, (2 * c + f) * P:(2 * c + f + 1) * P], hmT[:, k, :],
                                         start=(k == 0), stop=(k == KD - 1))
                last.then_inc(fills(("K", c)), 1)
            for h in range(4):
                ps = bank("att", h)
                lo = 64 * (h % 2)
                for t in range(4):
                    last = pe.matmul(ps[:, t * P:(t + 1) * P], ke[lo:lo + 64, h // 2, t * P:(t + 1) * P],
                                     qe[lo:lo + 64, h // 2, t * P:(t + 1) * P], start=True, stop=True)
                last.then_inc(fills(("att", h)), 1)
            for g in range(4):
                pe.wait_ge(pooled, g + 1)
                product(("pool", g), lambda k: w_pool[:, g, :], lambda k: u_sb[:, g, PAD:], 1)
            pe.wait_ge(states, 2)
            for h in range(4):
                evacuated(pe, "att", h)
                ps = bank("o", h)
                lo = 64 * (h % 2)
                for t in range(4):
                    pe.matmul(ps[:, t * P:(t + 1) * P], v_sb[:, t, h * P:(h + 1) * P], att[:, h, t, :], start=True, stop=False)
                    for c in (2 * t, 2 * t + 1):
                        last = pe.matmul(ps[:, c * CHUNK:(c + 1) * CHUNK], S_prev[lo:lo + 64, h // 2, c, :],
                                         qe[lo:lo + 64, h // 2, c * CHUNK:(c + 1) * CHUNK], start=False, stop=(c % 2 == 1))
                last.then_inc(fills(("o", h)), 1)
            pe.wait_ge(w_landed["w_xv"], 16)
            for m in range(2):
                for n in range(2):
                    product(("V", m, n), lambda k: hmT[:, k, m * P:(m + 1) * P], lambda k: w_xv[:, k, n * 512:(n + 1) * 512], KD)
            for h in range(4):
                pe.wait_ge(osq_ready, h + 1)
                product(("ss", h), lambda k: ones[:, :], lambda k: pool_s[:, h % 2, 0:T], 1)
            pe.wait_ge(w_landed["w_out"], 16)
            for g in range(4):
                evacuated(pe, "pool", g)
            pe.wait_ge(mixed, 4)
            for t in range(TT):
                for n in range(2):
                    product(("x1", t, n), lambda k: mixT[:, k, t * P:(t + 1) * P], lambda k: w_out[:, k, n * 512:(n + 1) * 512], KD)
            for t in range(TT):
                pe.wait_ge(normed, NORM["x1", t] + 1)
                for h in range(2):
                    turn(("h2t", t, h), lambda i: nrm_t[:, t, (4 * h + i) * P:(4 * h + i + 1) * P])
            for t in range(TT):
                for h in range(2):
                    evacuated(pe, "h2t", t, h)
            pe.wait_ge(w_landed["w_xq"], 16)
            for f in range(8):
                product(("Q", f), lambda k: w_xq[:, k, f * P:(f + 1) * P], lambda k: hT[:, k, :], KD)
            for h in range(4):
                for f in range(2):
                    evacuated(pe, "Q", 2 * h + f)
                for b in range(2):
                    ps = bank("sc", h, b)
                    for t in (2 * b, 2 * b + 1):
                        for f in range(2):
                            last = pe.matmul(ps[:, (t % 2) * M:(t % 2) * M + M], QT[:, 2 * h + f, t * P:(t + 1) * P],
                                             KT[:, 2 * h + f, :], start=(f == 0), stop=(f == 1))
                    last.then_inc(fills(("sc", h, b)), 1)
            for h in range(4):
                pe.wait_ge(prob_ready, 4 * h + 4)
                for m in range(2):
                    ps = bank("pt", h, m)
                    for t in range(4):
                        last = pe.transpose(ps[:, t * P:(t + 1) * P], prob[:, h, t, m * P:(m + 1) * P], ident[:, :])
                    last.then_inc(fills(("pt", h, m)), 1)
            for h in range(4):
                for m in range(2):
                    evacuated(pe, "pt", h, m)
                for c in range(2):
                    product(("O", h, c), lambda m: V[:, m, (2 * h + c) * P:(2 * h + c + 1) * P], lambda m: pT[:, h, m, :], MT)
            for h in range(4):
                for c in range(2):
                    evacuated(pe, "O", h, c)
            pe.wait_ge(w_landed["w_xo"], 16)
            for t in range(TT):
                for n in range(2):
                    product(("x2", t, n), lambda k: mixT[:, k, t * P:(t + 1) * P], lambda k: w_xo[:, k, n * 512:(n + 1) * 512], KD)
            for t in range(TT):
                pe.wait_ge(normed, NORM["x2", t] + 1)
                for h in range(2):
                    turn(("h3t", t, h), lambda i: nrm_t[:, t, (4 * h + i) * P:(4 * h + i + 1) * P])
            for t in range(TT):
                for h in range(2):
                    evacuated(pe, "h3t", t, h)
            ps = bank("lg")
            for t in range(TT):
                for k in range(KD):
                    last = pe.matmul(ps[:, t * E:(t + 1) * E], hT[:, k, t * P:(t + 1) * P], w_rt[:, k, :],
                                     start=(k == 0), stop=(k == KD - 1))
            last.then_inc(fills(("lg",)), 1)
            pe.wait_ge(mask_ready, 1)
            ps = bank("rank")
            for t in range(TT + 1):
                for s in range(min(t + 1, TT)):
                    last = pe.matmul(ps[:, t * E:(t + 1) * E], before[:, :] if s == t else ones_b[:, :], maskb[:, s, :],
                                     start=(s == 0), stop=(s == min(t, TT - 1)))
            last.then_inc(fills(("rank",)), 1)
            ps = bank("tab")
            for i in range(4 * TT):
                pe.wait_ge(vals_ready, i + 1)
                last = pe.matmul(ps[:, 0:2 * NB], onehot_p[:, i % 4, :], vals[:, i % 4, :, :].rearrange("p c b -> p (c b)"),
                                 start=(i == 0), stop=(i == 4 * TT - 1)).then_inc(vals_used, 1)
            pe.wait_ge(vals_ready, 4 * TT + 1)
            pe.wait_ge(consts, 5)
            ps = bank("meta")
            for s in range(4):
                last = pe.matmul(ps[:, s * 2 * NB:(s + 1) * 2 * NB], spread[:, s, :], tabv.rearrange("p c b -> p (c b)"),
                                 start=True, stop=True)
            last.then_inc(fills(("meta",)), 1)

            def rows_turn(b):
                pe.wait_ge(gathered, 16 * b + 16)
                for i in range(8):
                    last = pe.transpose(PS[i // 4][:, (i % 4) * P:(i % 4 + 1) * P], xg[:, i * P:(i + 1) * P], ident[:, :])
                last.then_inc(xt_full, 1)

            pe.wait_ge(tables_ready, 1)
            pe.wait_ge(bias_ready, 2)
            blocks = pe.value_load(ctl[0:1, 1, 63:64], min_val=E, max_val=NBLK)
            rows_turn(0)
            with pe.Fori(0, NBLK) as b:
                with pe.If(b < blocks):
                    n_sub = pe.value_load(ctl[0:1, 0, bass.ds(b, 1)], min_val=0, max_val=NSUB)
                    pe.wait_ge(xT_ready, 2 * b + 2)
                    pe.wait_ge(sel_ready, b + 1)

                    def gate_up(s, g):
                        for j in range(NCOL):
                            ps = PS[s][SUB * j:SUB * (j + 1), :].rearrange("p (h n) -> p h n", h=2)
                            if g == 0:
                                pe.matmul(ps, sel[:, :], bias3[:, 0:2 * F].rearrange("p (h n) -> p h n", h=2)[:, :, j * FQ:(j + 1) * FQ],
                                          start=True, stop=False)
                        for k in range(GK * g, GK * g + GK):
                            for j in range(NCOL):
                                ps = PS[s][SUB * j:SUB * (j + 1), :].rearrange("p (h n) -> p h n", h=2)
                                last = pe.matmul(ps, xT[:, k, SUB * s:SUB * (s + 1)], wg[:, k, :, j * FQ:(j + 1) * FQ],
                                                 start=False, stop=(k == KD - 1))
                        return last

                    def down(s, g):
                        if g == 0:
                            for j in range(NCOL):
                                pe.matmul(PS[4 + s][SUB * j:SUB * (j + 1), 0:DQ], sel[:, :],
                                          bias3[:, 2 * F + j * DQ:2 * F + (j + 1) * DQ], start=True, stop=False)
                        for k in range(GK * g, GK * g + GK):
                            for j in range(NCOL):
                                last = pe.matmul(PS[4 + s][SUB * j:SUB * (j + 1), 0:DQ],
                                                 aT[:, s, k % 2, SUB * (k // 2):SUB * (k // 2 + 1)],
                                                 wd[:, k, j * DQ:(j + 1) * DQ], start=False, stop=(k == KF - 1))
                        return last

                    for g in range(NG):
                        pe.wait_ge(gu_in[g], 16 * b + 16)
                        for s in range(NSUB - 1, 0, -1):
                            with pe.If(n_sub > s):
                                gate_up(s, g)
                        gate_up(0, g).then_inc(gu_used, 1)
                    for s in range(NSUB):
                        pe.wait_ge(a_ready, 2 * b + s // 2 + 1)
                        pe.wait_ge(y_ready, NSUB * b + NSUB)
                        for c in range(2):
                            last = pe.transpose(PS[4 + s][:, c * P:(c + 1) * P], a_sb[:, s, c * P:(c + 1) * P], ident[:, :])
                        last.then_inc(at_full, 1)
                    with pe.If(b + 1 < blocks):
                        rows_turn(b + 1)
                    pe.wait_ge(aT_ready, NSUB * b + NSUB)
                    for g in range(NG):
                        pe.wait_ge(dn_in[g], 16 * b + 16)
                        for s in range(NSUB - 1, 0, -1):
                            with pe.If(n_sub > s):
                                down(s, g)
                        down(0, g).then_inc(dn_used, 1)

        @block.vector
        def _(dve):
            steps = [0]

            def step(ins):
                steps[0] += 1
                ins.then_inc(dve_step, 1)
                dve.wait_ge(dve_step, steps[0])

            def norm(name, t, src, g):
                n = NORM[name, t]
                dve.wait_ge(sq_sum, n + 1)
                dve.wait_ge(g_in, 16 * (g + 1))
                step(dve.reciprocal(stat[:, 2, n:n + 1], stat[:, 1, n:n + 1]))
                return dve.scalar_tensor_tensor(out=nrm_t[:, t, :], in0=src, scalar=stat[:, 2, n:n + 1], in1=gbc[:, :],
                                                op0=ALU.mult, op1=ALU.mult).then_inc(normed, 1)

            def copy_bank(job, dst, src=None):
                ps = full(dve, *job)
                dve.tensor_copy(dst, ps[:, :] if src is None else src(ps)).then_inc(freed(job), 1)

            def gains_used(n):
                dve.wait_ge(normed, n)
                dve.engine_nop().then_inc(g_used, 1)

            step(dve.memset(pool_s[:, :, 0:PAD], 0.0))
            step(dve.memset(u_sb[:, :, 0:PAD], 0.0))
            for t in range(TT):
                norm("x", t, x_sb[:, t, :], 0)
            gains_used(TT)
            for t in range(TT):
                copy_bank(("xt", t, 0), hT[:, 0:4, t * P:t * P + P], lambda ps: ps[:, :].rearrange("p (k n) -> p k n", k=4))
            for t in range(MT):
                norm("mem", t, V[:, t, :], 1)
            gains_used(TT + MT)
            copy_bank(("k", 0), kg[:, 0, :])
            ps = full(dve, "q", 0)
            dve.tensor_scalar(qg[:, 0, :], ps[:, :], float(CHUNK) ** -0.5, None, ALU.mult).then_inc(freed(("q", 0)), 1)
            copy_bank(("v", 0), v_sb[:, 0, :])
            copy_bank(("v", 2), v_sb[:, 2, :])
            dve.wait_ge(small_in, 16 * 7)
            for p in range(2):
                ps = full(dve, "gate", p)
                dve.wait_ge(consts, 4)
                step(dve.tensor_scalar(gc[:, p, :], ps[:, :], cols[:, 4 + p:5 + p], None, ALU.add))
                dve.scalar_tensor_tensor(out=gtmp[:, p, :], in0=gc[:, p, :], scalar=-1.0, in1=gc[:, p, :],
                                         op0=ALU.mult, op1=ALU.max).then_inc(gd, 1)
                dve.wait_ge(gd, 2 * p + 1)
                dve.tensor_scalar(gc[:, p, :], gc[:, p, :], 0.0, None, ALU.min).then_inc(gd, 1)
                dve.wait_ge(gd, 2 * p + 2)
                dve.engine_nop().then_inc(freed(("gate", p)), 1)
            keep = pool_s[:, 0, PAD:PAD + T]
            step(dve.memset(keep, 1.0))
            step(dve.memset(keep.rearrange("p (c i) -> p c i", i=CHUNK)[:, :, 0:1], 0.0))
            for p in range(2):
                dve.wait_ge(gl, p + 1)
                step(dve.tensor_tensor(gtmp[:, p, :], gc[:, p, :], gtmp[:, p, :], ALU.subtract))
                step(dve.tensor_scalar(gtmp[:, p, :], gtmp[:, p, :], 1.0 / GATE_NORMALIZER, None, ALU.mult))
                dve.tensor_tensor_scan(gc[:, p, :], keep, gtmp[:, p, :], 0.0, ALU.mult, ALU.add).then_inc(gd, 1)
            for p in range(2):
                base = 2 + 10 * p
                evacuated(dve, "q", p)
                evacuated(dve, "k", p)
                dve.wait_ge(gl, base + 10)
                for dst, src in ((qe, qg), (ke, kg), (kd, kg)):
                    if dst is qe:
                        step(dve.tensor_copy(soft[:, 2 + p, 0:8],
                                             qe[:, p, :].rearrange("p (c i) -> p c i", i=CHUNK)[:, :, CHUNK - 1]))
                    dve.tensor_tensor(dst[:, p, :], dst[:, p, :], src[:, p, :], ALU.mult).then_inc(kd_ready, 1)
            for g in (0, 2):
                copy_bank(("u", g), u_sb[:, g, PAD:])
            for t in range(2):
                for m in range(2):
                    evacuated(dve, "xt", 3, m)
                copy_bank(("mt", t, 0), hmT[:, 0:4, t * P:t * P + P], lambda ps: ps[:, :].rearrange("p (k n) -> p k n", k=4))
            copy_bank(("kd", 0), kd_tok[:, 0, :, :].rearrange("p t d -> p (t d)"))
            evacuated(dve, "r", 3)
            step(dve.memset(att.rearrange("p h t i -> p (h t i)"), 0.0))
            for p in range(2):
                even, odd = full(dve, "ds", p, 0), full(dve, "ds", p, 1)
                step(dve.memset(S_prev[:, p, 0, :], 0.0))
                for c in range(7):
                    src = (even, odd)[c % 2][:, (c // 2) * P:(c // 2 + 1) * P]
                    step(dve.scalar_tensor_tensor(out=S_prev[:, p, c + 1, :], in0=S_prev[:, p, c, :],
                                                  scalar=soft[:, 2 + p, c:c + 1], in1=src, op0=ALU.mult, op1=ALU.add))
                dve.engine_nop().then_inc(freed(("ds", p, 0)), 1)
                dve.engine_nop().then_inc(freed(("ds", p, 1)), 1)
                dve.engine_nop().then_inc(states, 1)
            for h in range(4):
                ps = full(dve, "att", h)
                for t in range(4):
                    last = dve.copy_predicated(att[:, h, t, :], causal[:, :].bitcast(U32), ps[:, t * P:(t + 1) * P])
                    if t < 3:
                        step(last)
                last.then_inc(freed(("att", h)), 1)
            for g, w in enumerate(WINDOWS):
                evacuated(dve, "u", g)
                src, n = u_sb[:, g, :], 1
                i = 0
                while n < w:
                    dst = pool_s[:, i % 2, :]
                    step(dve.tensor_tensor(dst[:, PAD:], src[:, PAD:], src[:, PAD - n:PAD + T - n], ALU.add))
                    src, n, i = dst, 2 * n, i + 1
                step(dve.tensor_tensor(soft[:, 1, 0:w], src[:, PAD:PAD + w], inv_cnt[:, 0:w], ALU.mult))
                step(dve.tensor_tensor(soft[:, 1, 0:w], soft[:, 1, 0:w], u_sb[:, g, PAD:PAD + w], ALU.subtract))
                step(dve.scalar_tensor_tensor(out=u_sb[:, g, PAD:], in0=src[:, PAD:], scalar=1.0 / w, in1=u_sb[:, g, PAD:],
                                              op0=ALU.mult, op1=ALU.subtract))
                dve.tensor_copy(u_sb[:, g, PAD:PAD + w], soft[:, 1, 0:w]).then_inc(pooled, 1)
                dve.wait_ge(pooled, g + 1)
            for h in range(4):
                if h == 0:
                    for t in range(2):
                        evacuated(dve, "mt", t, 0)
                        evacuated(dve, "mt", t, 1)
                copy_bank(("o", h), o_sb[:, h, :])
            for m in range(2):
                copy_bank(("V", m, 0), V[:, m, 0:512])
            for h in range(4):
                dve.wait_ge(sig_ready, h + 1)
                step(dve.tensor_tensor(sig_r[:, h, :], sig_r[:, h, :], mixT[:, 4 + h, :], ALU.mult))
                step(dve.scalar_tensor_tensor(out=sig_r[:, h, :], in0=o_sb[:, h, :], scalar=cols[:, 6:7], in1=sig_r[:, h, :],
                                              op0=ALU.mult, op1=ALU.mult))
                evacuated(dve, "ss", h)
                step(dve.reciprocal(gc[:, 1, :], gc[:, 0, :]))
                dve.tensor_tensor(mixT[:, 4 + h, :], sig_r[:, h, :], gc[:, 1, :], ALU.mult).then_inc(mixed, 1)
                dve.wait_ge(mixed, h + 1)

            def residual(job, t, n):
                ps = full(dve, *job)
                dve.tensor_tensor(x_sb[:, t, n * 512:(n + 1) * 512], x_sb[:, t, n * 512:(n + 1) * 512], ps[:, :],
                                  ALU.add).then_inc(freed(job), 1)

            for t in range(TT):
                for n in range(2):
                    residual(("x1", t, n), t, n)
            for t in range(TT):
                norm("x1", t, x_sb[:, t, :], 2)
            gains_used(2 * TT + MT)
            for t in range(TT):
                copy_bank(("h2t", t, 0), hT[:, 0:4, t * P:t * P + P], lambda ps: ps[:, :].rearrange("p (k n) -> p k n", k=4))
            for h in range(4):
                for t in range(4):
                    ps = full(dve, "sc", h, t // 2)
                    dve.tensor_reduce(soft[:, 0, 4 * h + t:4 * h + t + 1], ps[:, (t % 2) * M:(t % 2) * M + M], AX.X, ALU.max,
                                      negate=True).then_inc(maxed, 1)
                for t in range(4):
                    i = 4 * h + t
                    dve.wait_ge(exped, i + 1)
                    step(dve.reciprocal(soft[:, 2, i:i + 1], soft[:, 1, i:i + 1]))
                    dve.tensor_scalar(prob[:, h, t, :], prob[:, h, t, :], soft[:, 2, i:i + 1], None, ALU.mult).then_inc(prob_ready, 1)
                    if t % 2:
                        dve.engine_nop().then_inc(freed(("sc", h, t // 2)), 1)
            for h in range(4):
                copy_bank(("pt", h, 0), pT[:, h, 0, :])
                copy_bank(("O", h, 0), mixT[:, 2 * h, :])
            dve.wait_ge(bias_in, 16 * 6)
            step(dve.tensor_copy(bias3[0:32, :], b_all[0:32, :]))
            step(dve.tensor_copy(bias3[32:64, :], b_all[32:64, :]))
            step(dve.tensor_tensor(b_all[32:64, :], b_all[32:64, :], bias3[32:64, :], ALU.subtract))
            step(dve.tensor_copy(bias3[32:64, :], b_all[32:64, :]))
            dve.engine_nop().then_inc(bias_ready, 1)
            for t in range(TT):
                for n in range(2):
                    residual(("x2", t, n), t, n)
            for t in range(TT):
                norm("x2", t, x_sb[:, t, :], 3)
            gains_used(3 * TT + MT)
            dve.wait_ge(bias_ready, 2)
            for t in range(TT):
                copy_bank(("h3t", t, 0), hT[:, 0:4, t * P:t * P + P], lambda ps: ps[:, :].rearrange("p (k n) -> p k n", k=4))

            ps = full(dve, "lg")
            dve.wait_ge(consts, 5)
            for t in range(TT):
                step(dve.tensor_tensor(logits[:, t, :], ps[:, t * E:(t + 1) * E], b_rt[:, :], ALU.add))
                step(dve.max(top8[:, t, :], logits[:, t, :]))
                step(dve.max_index(idx8[:, t, :], top8[:, t, :], logits[:, t, :]))
                step(dve.tensor_scalar(gsum[:, t:t + 1], top8[:, t, 0:1], -1.0, None, ALU.mult))
            dve.engine_nop().then_inc(top_ready, 1)
            dve.tensor_copy(idxf, idx8[:, :, 0:4]).then_inc(freed(("lg",)), 1)
            evacuated(dve, "lg")
            for k in range(4):
                for t in range(TT):
                    step(dve.tensor_scalar(oh[:, k, t, :], iota_e[:, :], idxf[:, t, k:k + 1], None, ALU.is_equal))
            step(dve.tensor_tensor(maskf, oh[:, 0], oh[:, 1], ALU.add))
            step(dve.tensor_tensor(maskf, maskf, oh[:, 2], ALU.add))
            step(dve.tensor_tensor(maskf, maskf, oh[:, 3], ALU.add))
            dve.tensor_copy(maskb, maskf).then_inc(mask_ready, 1)
            dve.wait_ge(gate_exp, TT)
            step(dve.reciprocal(gsum[:, 4:8], gsum[:, 4:8]))
            for t in range(TT):
                step(dve.tensor_scalar(gate4[:, t, :], gate4[:, t, :], gsum[:, 4 + t:5 + t], None, ALU.mult))
            ps = full(dve, "rank")
            dve.tensor_copy(rank.rearrange("p t e -> p (t e)"), ps[:, 0:5 * E]).then_inc(freed(("rank",)), 1)
            evacuated(dve, "rank")
            cnt = rank[:, 4, :]
            step(dve.tensor_scalar(lvl[:, 0, :], cnt, float(P), None, ALU.is_gt))
            for i in (2, 3):
                step(dve.scalar_tensor_tensor(out=lvl[:, 0, :], in0=cnt, scalar=float(i * P), in1=lvl[:, 0, :], op0=ALU.is_gt, op1=ALU.add))
            step(dve.memset(lvl[:, 1, :], 1.0))
            step(dve.tensor_tensor_scan(xend[:, :], lvl[:, 1, :], lvl[:, 0, :], 0.0, ALU.mult, ALU.add))
            step(dve.tensor_tensor(xoff[:, :], xend[:, :], lvl[:, 0, :], ALU.subtract))
            step(dve.tensor_scalar(xoff[:, :], xoff[:, :], float(E - 1), None, ALU.add))
            for t in range(TT):
                step(dve.tensor_scalar(lvl[:, 1, :], rank[:, t, :], float(P), None, ALU.is_ge))
                step(dve.scalar_tensor_tensor(out=lvl[:, 2, :], in0=rank[:, t, :], scalar=float(2 * P), in1=lvl[:, 1, :], op0=ALU.is_ge, op1=ALU.add))
                step(dve.scalar_tensor_tensor(out=lvl[:, 2, :], in0=rank[:, t, :], scalar=float(3 * P), in1=lvl[:, 2, :], op0=ALU.is_ge, op1=ALU.add))
                step(dve.scalar_tensor_tensor(out=rank[:, t, :], in0=lvl[:, 2, :], scalar=-float(P), in1=rank[:, t, :], op0=ALU.mult, op1=ALU.add))
                step(dve.tensor_tensor(lvl[:, 3, :], xoff[:, :], iota_e[:, :], ALU.subtract))
                step(dve.tensor_tensor(lvl[:, 3, :], lvl[:, 3, :], lvl[:, 1, :], ALU.mult))
                step(dve.tensor_tensor(lvl[:, 3, :], lvl[:, 3, :], lvl[:, 2, :], ALU.add))
                step(dve.tensor_tensor(blk_t[:, t, :], lvl[:, 3, :], iota_e[:, :], ALU.add))
            for k in range(4):
                for t in range(TT):
                    step(dve.tensor_tensor_reduce(junk[:, 0:E], oh[:, k, t, :], rank[:, t, :], 1.0, 0.0, ALU.mult, ALU.add, pos16[:, k, t:t + 1]))
                    step(dve.tensor_tensor_reduce(junk[:, 0:E], oh[:, k, t, :], blk_t[:, t, :], 1.0, 0.0, ALU.mult, ALU.add, blk16[:, k, t:t + 1]))
            for i in range(4 * TT):
                k, t = i // TT, i % TT
                if i >= 4:
                    dve.wait_ge(vals_used, i - 3)
                step(dve.tensor_scalar(onehot_p[:, i % 4, :], iota_p[:, :], pos16[:, k, t:t + 1], None, ALU.is_equal))
                step(dve.tensor_scalar(vals[:, i % 4, 0, :], iota_b[:, :], blk16[:, k, t:t + 1], tokp[:, t:t + 1], ALU.is_equal, ALU.mult))
                dve.tensor_scalar(vals[:, i % 4, 1, :], iota_b[:, :], blk16[:, k, t:t + 1], gate4[:, t, k:k + 1], ALU.is_equal,
                                  ALU.mult).then_inc(vals_ready, 1)
            step(dve.tensor_scalar(nsubf[:, 0:E], cnt, 0.0, None, ALU.is_gt))
            for i in range(1, NSUB):
                step(dve.scalar_tensor_tensor(out=nsubf[:, 0:E], in0=cnt, scalar=float(i * SUB), in1=nsubf[:, 0:E], op0=ALU.is_gt, op1=ALU.add))
            step(dve.memset(nsubf[:, E:NB], float(NSUB)))
            step(dve.tensor_copy(ebc[:, 0:E], iota_e[:, :]))
            for i in range(NB - E):
                step(dve.tensor_scalar(xcmp[:, :], xend[:, :], float(i), None, ALU.is_le))
                step(dve.tensor_reduce(ebc[:, E + i:E + i + 1], xcmp[:, :], AX.X, ALU.add))
            step(dve.tensor_scalar(ebc[:, :], ebc[:, :], float(E - 1), None, ALU.min))
            step(dve.tensor_copy(ctl[0:1, 0, 0:NB], nsubf[0:1, 0:NB]))
            step(dve.tensor_copy(ctl[0:1, 1, 0:NB], ebc[0:1, 0:NB]))
            step(dve.tensor_scalar(ctl[0:1, 1, 63:64], xend[0:1, E - 1:E], float(E), None, ALU.add))
            dve.wait_ge(vals_used, 4 * TT)
            ps = PS[JOB["tab",] % 8]
            dve.tensor_copy(tabv.rearrange("p c b -> p (c b)"), ps[:, 0:2 * NB]).then_inc(vals_ready, 1)
            dve.wait_ge(vals_ready, 4 * TT + 1)
            dve.tensor_scalar(gidx, tabv[:, 0, :], -1.0, 0.0, ALU.add, ALU.max).then_inc(freed(("tab",)), 1)
            evacuated(dve, "tab")
            ps = full(dve, "meta")
            dve.tensor_copy(meta.rearrange("p s c b -> p (s c b)"), ps[:, 0:8 * NB]).then_inc(freed(("meta",)), 1)
            evacuated(dve, "meta")
            for s in range(NSUB):
                row = meta[:, s, 0, :]
                step(dve.tensor_scalar(nsubf[:, 0:NB], row, 0.0, 16384.0, ALU.is_equal, ALU.mult))
                step(dve.scalar_tensor_tensor(out=row, in0=row, scalar=float(NCOL), in1=nsubf[:, 0:NB], op0=ALU.mult, op1=ALU.add))
                step(dve.tensor_scalar(row, row, jcol[:, 0:1], None, ALU.add))
            dve.engine_nop().then_inc(tables_ready, 1)

            blocks = dve.value_load(ctl[0:1, 1, 63:64], min_val=E, max_val=NBLK)

            def pick_row(b):
                dve.tensor_scalar(cur_i[:, 0:1], gidx[:, bass.ds(b, 1)], 0.0, None, ALU.add).then_inc(row_picked, 1)

            def pick_bias(b):
                dve.tensor_scalar(sel[:, :], ebc[:, bass.ds(b, 1)].to_broadcast([P, SUB]), row_e[:, 0:1], None,
                                  ALU.is_equal).then_inc(sel_ready, 1)

            PER = 2 + 2 + 2 * NSUB
            for s in range(NSUB):
                dve.engine_nop().then_inc(y_ready, 1)
            pick_row(0)
            pick_bias(0)
            with dve.Fori(0, NBLK) as b:
                with dve.If(b < blocks):
                    base = b * PER
                    dve.wait_ge(gathered, 16 * b + 16)
                    pick_row(b + 1)
                    dve.wait_ge(gu_used, NG * b + NG)
                    for i in range(2):
                        for s in (2 * i, 2 * i + 1):
                            last = dve.tensor_scalar(gm_sb[:, s, :], PS[s][:, 0:FQ], SWIGLU_LIMIT, None, ALU.min)
                        last.then_inc(gate_min, 1)
                        for s in (2 * i, 2 * i + 1):
                            last = dve.tensor_scalar(up_sb[:, s, :], PS[s][:, FQ:2 * FQ], SWIGLU_LIMIT, -SWIGLU_LIMIT, ALU.min, ALU.max)
                        last.then_inc(moe_step, 1)
                    for i in range(2):
                        h = slice(2 * i, 2 * i + 2)
                        dve.wait_ge(moe_step, base + 2)
                        dve.wait_ge(gate_min, 2 * b + 2)
                        dve.scalar_tensor_tensor(out=up_sb[:, h, :], in0=up_sb[:, h, :], scalar=1.0, in1=gm_sb[:, h, :],
                                                 op0=ALU.add, op1=ALU.mult).then_inc(moe_step, 1)
                    for i in range(2):
                        h = slice(2 * i, 2 * i + 2)
                        dve.wait_ge(moe_step, base + 3 + i)
                        dve.wait_ge(sig_done, 2 * b + i + 1)
                        dve.tensor_tensor(a_sb[:, h, :], up_sb[:, h, :], sg_sb[:, h, :], ALU.mult).then_inc(a_ready, 1)
                    dve.wait_ge(added, 16 * NSUB * b + 16 * TT)
                    for s in range(NSUB):
                        dve.tensor_scalar(cur_i[:, 4 + s:5 + s], meta[:, s, 0, bass.ds(b, 1)], 0.0, None, ALU.add).then_inc(moe_step, 1)
                        dve.tensor_scalar(cur_g[:, s:s + 1], meta[:, s, 1, bass.ds(b, 1)], 0.0, None, ALU.add).then_inc(moe_step, 1)
                    dve.wait_ge(moe_step, base + PER)
                    dve.wait_ge(dn_used, NG * b + NG)
                    pick_bias(b + 1)
                    for s in range(NSUB):
                        dve.tensor_scalar(y_sb[:, s, :], PS[4 + s][:, 0:DQ], cur_g[:, s:s + 1], None, ALU.mult).then_inc(y_ready, 1)
            for t in range(TT):
                norm("out", t, x_sb[:, t, :], 4)

        @block.gpsimd
        def _(pool):
            steps = [0]

            def step(ins, s=pool_step):
                steps[0] += 1
                ins.then_inc(pool_step, 1)
                pool.wait_ge(pool_step, steps[0])

            step(pool.memset(ident[:, :], 0.0))
            pool.affine_select(out=ident[:, :], in_=ident[:, :], compare_op=ALU.not_equal, fill=1.0, base=0,
                               pattern=[[-1, P]], channel_multiplier=1).then_inc(consts, 1)
            step(pool.memset(eps_c[:, :], EPS))
            step(pool.memset(ones[:, :], 1.0 / P))
            step(pool.memset(ones_b[:, :], 1.0))
            step(pool.memset(before[:, :], 1.0))
            pool.affine_select(out=before[:, :], in_=before[:, :], compare_op=ALU.is_gt, fill=0.0, base=0,
                               pattern=[[1, P]], channel_multiplier=-1).then_inc(consts, 1)
            step(pool.memset(causal[:, :], 1.0))
            step(pool.affine_select(out=causal[:, :], in_=causal[:, :], compare_op=ALU.is_ge, fill=0.0, base=0,
                                    pattern=[[1, P]], channel_multiplier=-1))
            pool.memset(causal[0:64, 64:128], 0.0).then_inc(consts, 1)
            for t in range(PAD):
                step(pool.memset(inv_cnt[:, t:t + 1], 1.0 / (t + 1)))
            pool.nop().then_inc(consts, 1)

            for h in range(4):
                evacuated(pool, "sc", h, 1)
            step(pool.iota(iota_e[:, :], pattern=[[1, E]], base=0, channel_multiplier=0, allow_small_or_imprecise_dtypes=True))
            step(pool.iota(iota_b[:, :], pattern=[[1, NB]], base=0, channel_multiplier=0, allow_small_or_imprecise_dtypes=True))
            step(pool.iota(iota_p[:, :], pattern=[[1, P]], base=0, channel_multiplier=0, allow_small_or_imprecise_dtypes=True))
            step(pool.iota(tokp[:, :], pattern=[[P, 4]], base=1, channel_multiplier=1, allow_small_or_imprecise_dtypes=True))
            step(pool.iota(pcol[:, 0:1], pattern=[[0, 1]], base=0, channel_multiplier=1, allow_small_or_imprecise_dtypes=True))
            for j in range(4):
                q = slice(32 * j, 32 * j + 32)
                step(pool.tensor_scalar(row_e[q, 0:1], pcol[q, 0:1], float(-32 * j if j < 3 else 1000), None, ALU.add))
                step(pool.memset(jcol[q, 0:1], float(j - NCOL)))
            step(pool.memset(spread.rearrange("p s q -> p (s q)"), 0.0))
            for s in range(NSUB):
                part = spread[:, s, :].rearrange("p (j r) -> p j r", j=4)
                step(pool.affine_select(out=part, in_=part, compare_op=ALU.not_equal, fill=1.0, base=-SUB * s,
                                        pattern=[[0, 4], [-1, SUB]], channel_multiplier=1))
            pool.nop().then_inc(consts, 1)
            for h in range(4):
                for c in range(2):
                    evacuated(pool, "O", h, c)
            for i in range(3):
                q = slice(32 * i, 32 * i + 32)
                pool.dma_start(b_all[q, 0:2 * F], a["b_gu"][0]).then_inc(bias_in, 16)
                pool.dma_start(b_all[q, 2 * F:2 * F + D], a["b_dn"][0]).then_inc(bias_in, 16)
            step(pool.memset(bias3[96:128, :], 0.0))
            pool.wait_ge(bias_in, 16 * 6)
            q = slice(64, 96)
            step(pool.tensor_copy(bias3[q, :], b_all[q, :]))
            for i in range(2):
                step(pool.tensor_tensor(b_all[q, :], b_all[q, :], bias3[q, :], ALU.subtract))
                step(pool.tensor_copy(bias3[q, :], b_all[q, :]))
            pool.nop().then_inc(bias_ready, 1)
            for t in range(TT):
                pool.wait_ge(normed, NORM["x2", t] + 1)
                pool.dma_start(h3_tok[:, t, :], nrm_t[:, t, :]).then_inc(h3_out, 16)
                pool.dma_start(acc_tok[:, t, :], x_sb[:, t, :]).then_inc(added, 16)

            pool.wait_ge(h3_out, 16 * TT)
            pool.wait_ge(added, 16 * TT)
            gathered_end, added_end = pool.alloc_register("gathered_end"), pool.alloc_register("added_end")
            pool.reg_mov(gathered_end, 16)
            pool.reg_mov(added_end, 16 * TT)

            def gather():
                pool.indirect_dma_start(xg, None, h3_d, bass.IndirectOffsetOnAxis(ap=cur_i[:, 0:1], axis=0)).then_inc(gathered, 16)

            pool.wait_ge(tables_ready, 1)
            blocks = pool.value_load(ctl[0:1, 1, 63:64], min_val=E, max_val=NBLK)
            pool.wait_ge(row_picked, 1)
            gather()
            with pool.Fori(0, NBLK) as b:
                with pool.If(b < blocks):
                    pool.wait_ge(row_picked, b + 2)
                    pool.wait_ge(xt_full, b + 1)
                    pool.reg_add(gathered_end, gathered_end, 16)
                    gather()
                    pool.wait_ge(y_ready, NSUB * b + 2 * NSUB)
                    pool.wait_ge(added, 16 * NSUB * b + 16 * TT)
                    pool.reg_add(added_end, added_end, 16 * NSUB)
                    for s in range(NSUB):
                        pool.indirect_dma_start(acc_d, bass.IndirectOffsetOnAxis(ap=cur_i[:, 4 + s:5 + s], axis=0), y_sb[:, s, :], None,
                                                bounds_check=T * NCOL - 1, oob_is_err=False, compute_op=ALU.add).then_inc(added, 16)
            gathered_all, added_all = pool.snap(gathered_end), pool.snap(added_end)
            pool.wait_ge(gathered, gathered_all)
            pool.tensor_tensor(pool_end[0:1, 0:1], eps_c[0:1, 0:1], eps_c[0:1, 0:1], ALU.add)
            pool.wait_ge(added, added_all)
            pool.tensor_tensor(pool_end[0:1, 1:2], eps_c[0:1, 0:1], eps_c[0:1, 0:1], ALU.add).then_inc(all_added, 1)



_INS = ["x", "mem", "norm_mix_g", "w_in", "w_pool", "pool_scale", "w_gate_up", "b_gate_up", "gla_norm_g", "w_out",
        "norm_xattn_g", "norm_mem_g", "w_xq", "w_xk", "w_xv", "w_xo", "norm_moe_g", "w_router", "b_router",
        "w_gu", "b_gu", "w_dn", "b_dn", "norm_final_g"]


def kernel(**inputs):
    import numpy as _np
    import concourse.bacc as _bacc
    from concourse import mybir as _mybir
    from concourse.bass_utils import run_bass_kernel_spmd as _run

    nc = _bacc.Bacc("TRN2", target_bir_lowering=False, num_devices=1)
    arrays, aps = {}, {}
    for name in _INS:
        arr = _np.ascontiguousarray(inputs[name])
        arrays[f"in_{name}"] = arr
        aps[name] = nc.dram_tensor(f"in_{name}", arr.shape, _mybir.dt.from_np(arr.dtype), kind="ExternalInput").ap()
    out = nc.dram_tensor("out_0", inputs["x"].shape, _mybir.dt.float32, kind="ExternalOutput").ap()
    decoder_layer(nc, aps, out)
    r = _run(nc, [arrays], core_ids=[0])
    return r.results[0]["out_0"]
```

```python
from contextlib import ExitStack

import concourse.bass as bass
from concourse import mybir

F32 = mybir.dt.float32
BF16 = mybir.dt.bfloat16
I32 = mybir.dt.int32
U32 = mybir.dt.uint32
ALU = mybir.AluOpType
ACT = mybir.ActivationFunctionType
AX = mybir.AxisListType

P = 128
EPS = 1e-6
WINDOWS = (2, 4, 8, 16)
PAD = 16
GATE_NORMALIZER = 16.0
SWIGLU_LIMIT = 7.0
SWIGLU_ALPHA = 1.702
CHUNK = 64
SUB = 32
NSUB = P // SUB
NCOL = P // SUB


def lagged(product, turned):
    o = []
    for t in range(5):
        if t < 4:
            o += [(product, t, n) for n in range(2)]
        if t and turned == "h3t" and t > 1:
            o += [("lg", t - 2)]
        if t:
            o += [(turned, t - 1, h) for h in range(2)]
    return o


def job_order():
    o = [("xt", t, h) for t in range(4) for h in range(2)]
    o += [("glr",), ("k", 0), ("k", 1), ("q", 0), ("q", 1)]
    o += [("v", t) for t in range(4)]
    o += [("gate", 0), ("gate", 1)]
    o += [("u", g) for g in range(4)]
    o += [("r", h) for h in range(4)]
    o += [("mt", t, h) for t in range(2) for h in range(2)]
    o += [("kd", 0), ("kd", 1)]
    o += [("ds", p, c) for p in range(2) for c in range(2)]
    o += [("pool", g) for g in range(4)]
    o += [("att", h) for h in range(4)]
    o += [("K", c) for c in range(4)]
    o += [("o", h) for h in range(4)]
    o += [("V", 0, n) for n in range(2)]
    o += [("ss", h) for h in range(4)]
    o += [("V", 1, n) for n in range(2)]
    o += lagged("x1", "h2t")
    o += [("Q", f) for f in range(8)]
    o += [("sc", h, a) for h in range(4) for a in range(2)]
    o += [("pt", h, m) for h in range(4) for m in range(2)]
    o += [("O", h, c) for h in range(4) for c in range(2)]
    o += lagged("x2", "h3t")
    o += [("lg", 3), ("rank",), ("tab",), ("meta",)]
    return o


ORDER = job_order()
JOB = {name: n for n, name in enumerate(ORDER)}


def decoder_layer(nc, a, out):
    T, D = a["x"].shape[1:]
    M = a["mem"].shape[1]
    E = a["w_gu"].shape[1]
    F = a["w_dn"].shape[2]
    TT, KD, KF, MT = T // P, D // P, F // P, M // P
    TOPK = 4
    assert TT == NSUB
    MAX_EXTRA = T * TOPK // (P + 1)
    NBLK = E + MAX_EXTRA
    NB = NBLK + 1
    GK = 2
    NG = KD // GK
    LEAD = 2
    FQ, DQ = F // NCOL, D // NCOL

    x_d = a["x"].rearrange("o (t p) d -> p (o t) d", p=P)
    mem_d = a["mem"].rearrange("o (t p) d -> p (o t) d", p=P)
    out_d = out.rearrange("o (t p) d -> p (o t) d", p=P)
    w_in_d = a["w_in"].rearrange("o (k p) n -> p (o k) n", p=P)
    wsq = {n: a[n].rearrange("o (k p) n -> p (o k) n", p=P) for n in ("w_out", "w_xq", "w_xk", "w_xv", "w_xo")}
    h3_d = nc.dram_tensor("h3_rows", (T, D), F32).ap()
    acc_d = nc.dram_tensor("acc_rows", (T * NCOL, DQ), F32).ap()
    acc_tok = acc_d.rearrange("(t p j) d -> p t (j d)", p=P, j=NCOL)
    h3_tok = h3_d.rearrange("(t p) d -> p t d", p=P)

    with ExitStack() as ctx:
        def sb(name, shape, dt=F32):
            return ctx.enter_context(nc.sbuf_tensor(name, shape, dt))

        def sem(name):
            return ctx.enter_context(nc.semaphore(name))

        big = sb("big", [P, 4 * 8192])
        W = big[:, 0:3 * 8192]
        x_sb = big[:, 3 * 8192:3 * 8192 + 4096].rearrange("p (t d) -> p t d", t=TT)
        mixT = big[:, 3 * 8192 + 4096:4 * 8192].rearrange("p (k n) -> p k n", k=KD)
        nrm = sb("nrm", [P, 4096])
        hT = sb("hT", [P, KD, T])
        qreg = sb("qreg", [P, 4096])
        KT = sb("KT", [P, KD, M])
        V = sb("V", [P, MT, D])
        pool_s = sb("pool_s", [P, 2, PAD + T])
        gbc = sb("gbc", [P, D])

        ident = sb("ident", [P, P])
        ones = sb("ones", [P, P])
        causal = sb("causal", [P, P])
        before = sb("before", [P, P], BF16)
        ones_b = sb("ones_b", [P, P], BF16)
        w_pool = sb("w_pool_sb", [P, 4, P])
        w_gate = sb("w_gate_sb", [16, 256])
        w_rt = sb("w_router_sb", [P, KD, E])
        b_rt = sb("b_router_sb", [P, E])
        cols = sb("cols", [P, 8])
        stat = sb("stat", [P, 3, 24])
        inv_cnt = sb("inv_cnt", [P, PAD])
        eps_c = sb("eps_c", [P, 1])
        pool_end = sb("pool_end", [1, 2])
        soft = sb("soft", [P, 4, 16])
        sel = sb("sel", [P, SUB], BF16)
        ctl = sb("ctl", [1, 3, 64], I32)
        cur_i = sb("cur_i", [P, 8], I32)
        cur_g = sb("cur_g", [P, 4])

        w_in_cols = a["w_in"].shape[2]
        assert w_in_cols == 2064
        R0, R1, R2 = W[:, 0:8192], W[:, 8192:16384], W[:, 16384:24576]
        w_u = R0[:, 0:4096].rearrange("p (k n) -> p k n", k=KD)
        w_qk = R0[:, 4096:8192].rearrange("p (k n) -> p k n", k=KD)
        w_v = R1[:, 0:4096].rearrange("p (k n) -> p k n", k=KD)
        w_r = R1[:, 4096:8192].rearrange("p (k n) -> p k n", k=KD)
        sq = [R[:, :].rearrange("p (k n) -> p k n", k=KD) for R in (R0, R1, R2)]
        w_xk, w_out, w_xo = sq[0], sq[0], sq[0]
        w_xv = sq[1]
        w_xq = sq[2]
        u_sb = R2[:, 0:2112].rearrange("p (g n) -> p g n", g=4)
        qg = R2[:, 2112:3136].rearrange("p (a n) -> p a n", a=2)
        kg = R2[:, 3136:4160].rearrange("p (a n) -> p a n", a=2)
        sig_r = R2[:, 2112:4160].rearrange("p (h n) -> p h n", h=4)
        gc = R2[:, 4160:5184].rearrange("p (a n) -> p a n", a=2)
        v_sb = R2[:, 5184:7232].rearrange("p (t n) -> p t n", t=4)
        glr = R2[0:16, 7232:7744]
        w_lr = R2[:, 7744:7872].rearrange("p (k n) -> p k n", k=KD)
        qe = qreg[:, 0:1024].rearrange("p (a n) -> p a n", a=2)
        ke = qreg[:, 1024:2048].rearrange("p (a n) -> p a n", a=2)
        kd = qreg[:, 2048:3072].rearrange("p (a n) -> p a n", a=2)
        gtmp = qreg[:, 3072:4096].rearrange("p (a n) -> p a n", a=2)
        kd_tok = qreg[:, 3072:4096].rearrange("p (a t d) -> p a t d", a=2, t=4)
        QT = qreg[:, :].rearrange("p (f n) -> p f n", f=8)
        hflat = hT[:, :, :].rearrange("p k n -> p (k n)")
        att = hflat[:, 0:2048].rearrange("p (h t i) -> p h t i", h=4, t=4)
        S_prev = hflat[:, 2048:4096].rearrange("p (a c e) -> p a c e", a=2, c=8)
        pT = hflat.rearrange("p (h m n) -> p h m n", h=4, m=2)
        nrm_t = nrm[:, :].rearrange("p (t d) -> p t d", t=4)
        hmT = nrm[:, 2048:4096].rearrange("p (k m) -> p k m", k=KD)
        o_sb = nrm[:, 0:2048].rearrange("p (h n) -> p h n", h=4)
        prob = nrm[:, :].rearrange("p (h t m) -> p h t m", h=4, t=4)

        def rt(lo, n):
            return qreg[:, lo:lo + n]
        logits = rt(0, 128).rearrange("p (t e) -> p t e", t=4)
        top8 = rt(128, 32).rearrange("p (t k) -> p t k", t=4)
        idx8 = rt(160, 32).bitcast(U32).rearrange("p (t k) -> p t k", t=4)
        idxf = rt(192, 16).rearrange("p (k t) -> p k t", t=4)
        gate4 = rt(208, 16).rearrange("p (t k) -> p t k", t=4)
        gsum = rt(224, 8)
        oh = rt(256, 512).rearrange("p (k t e) -> p k t e", k=4, t=4)
        prod = rt(768, 512).rearrange("p (k t e) -> p k t e", k=4, t=4)
        maskb = rt(1280, 64).bitcast(BF16).rearrange("p (t e) -> p t e", t=4)
        rank = rt(1344, 160).rearrange("p (t e) -> p t e", t=5)
        lvl = rt(1504, 256).rearrange("p (a t e) -> p a t e", a=2, t=4)
        more, xend, xoff = rt(1760, 32), rt(1792, 32), rt(1824, 32)
        pos16 = rt(1856, 16).rearrange("p (k t) -> p k t", k=4)
        blk16 = rt(1872, 16).rearrange("p (k t) -> p k t", k=4)
        inblk = rt(1888, 16 * NB).rearrange("p (k t b) -> p k t b", k=4, t=4)
        onehot_p = V[:, :, :].rearrange("p m d -> p (m d)").rearrange("p (i s) -> p i s", i=16)
        vals = mixT[:, 0:3, :].rearrange("p k n -> p (k n)").rearrange("p (i c b) -> p i c b", i=16, c=2)
        spread = mixT[:, 3, :].rearrange("p (s q) -> p s q", s=4)
        iota_b = rt(2656, NB)
        iota_e = rt(2704, 32)
        iota_p = rt(2736, 128)
        tokp = rt(2864, 4)
        one_e = rt(2868, 32)
        pcol, jcol = rt(2900, 1), rt(2901, 1)
        row_e = rt(2902, 1)
        gidx = rt(2904, NB)
        tabv = rt(2952, 2 * NB).rearrange("p (c b) -> p c b", c=2)
        meta = rt(3048, 8 * NB).rearrange("p (s c b) -> p s c b", s=4, c=2)
        ebc = rt(3432, NB)
        nsubf = rt(3480, NB)
        assert NB == 48 and 2 * F + D == 3072
        bias3 = KT[:, 0:6, :].rearrange("p k n -> p (k n)").bitcast(BF16)
        b_all = hflat[:, 0:3072]
        assert NB == 48 and 2 * F + D == 3072
        xg = nrm[:, 0:1024]
        a_sb = nrm[:, 1024:2048].rearrange("p (s n) -> p s n", s=4)
        y_sb = nrm[:, 2048:3072].rearrange("p (s n) -> p s n", s=4)
        up_sb = nrm[:, 3072:4096].rearrange("p (s n) -> p s n", s=4)
        xT = hflat[:, 0:1024].rearrange("p (k n) -> p k n", k=8)
        aT = hflat[:, 1024:2048].rearrange("p (s c n) -> p s c n", s=4, c=2)
        gm_sb = hflat[:, 2048:3072].rearrange("p (s n) -> p s n", s=4)
        sg_sb = hflat[:, 3072:4096].rearrange("p (s n) -> p s n", s=4)
        wg = W[:, 0:16384].rearrange("p (k h n) -> p k h n", k=KD, h=2)
        wd = big[:, 16384:32768].rearrange("p (a k n) -> p a k n", a=2, k=KF)

        PS = [ctx.enter_context(nc.psum_tensor(f"bank{i}", [P, 512], F32)) for i in range(8)]

        bank_full = [sem(f"bank_full{i}") for i in range(8)]
        bank_free = [sem(f"bank_free{i}") for i in range(8)]
        x_in = [sem("x_in0"), sem("x_in1")]
        mem_in, small_in, g_in, consts = sem("mem_in"), sem("small_in"), sem("g_in"), sem("consts")
        w_landed = {n: sem(f"landed_{n}") for n in ("qk", "lr", "v", "u", "r", "w_xk", "w_xv", "w_out", "w_xq", "w_xo")}
        g_used = sem("g_used")
        sq_sum = sem("sq_sum")
        normed = sem("normed")
        gl = sem("gate_logs")
        gd = sem("gate_dve")
        kd_ready, pooled, states, osq_ready, mixed = sem("kd_ready"), sem("pooled"), sem("states"), sem("osq_ready"), sem("mixed")
        sig_ready = sem("sig_ready")
        maxed, exped, prob_ready = sem("maxed"), sem("exped"), sem("prob_ready")
        act_step, dve_step, pool_step = sem("act_step"), sem("dve_step"), sem("pool_step")
        h3_out = sem("h3_out")
        top_ready, gate_exp, mask_ready, vals_ready, vals_used = sem("top_ready"), sem("gate_exp"), sem("mask_ready"), sem("vals_ready"), sem("vals_used")
        ctl_ready = sem("ctl_ready")
        bias_in, bias_step = sem("bias_in"), sem("bias_step")
        gu_in = [sem(f"gu_in{g}") for g in range(NG)]
        dn_in = [[sem(f"dn_in{i}_{g}") for g in range(NG)] for i in range(2)]
        gu_used, dn_used = sem("gu_used"), sem("dn_used")
        row_picked, sel_ready, gathered, xt_full, xT_ready = sem("row_picked"), sem("sel_ready"), sem("gathered"), sem("xt_full"), sem("xT_ready")
        sub_done, gate_min, sig_done, a_ready = sem("sub_done"), sem("gate_min"), sem("sig_done"), sem("a_ready")
        at_full, aT_ready, y_ready, added = sem("at_full"), sem("aT_ready"), sem("y_ready"), sem("added")
        block_added = sem("block_added")
        moe_step = sem("moe_step")
        all_added, out_done = sem("all_added"), sem("out_done")
        final_in = [sem(f"final_in{t}") for t in range(TT)]

        block = ctx.enter_context(nc.Block())

        def full(eng, *job):
            n = JOB[job]
            eng.wait_ge(bank_full[n % 8], n // 8 + 1)
            return PS[n % 8]

        def freed(job):
            return bank_free[JOB[job] % 8]

        def evacuated(eng, *job):
            n = JOB[job]
            eng.wait_ge(bank_free[n % 8], n // 8 + 1)

        NORMS = [("x", t) for t in range(TT)] + [("mem", t) for t in range(MT)] + [("x1", t) for t in range(TT)] + \
                [("x2", t) for t in range(TT)] + [("out", t) for t in range(TT)]
        NORM = {n: i for i, n in enumerate(NORMS)}

        G_LOADS = ["norm_mix_g", "norm_mem_g", "norm_xattn_g", "norm_moe_g", "norm_final_g"]

        @block.sync
        def _(sp):
            def load_g(i):
                if i:
                    sp.wait_ge(g_used, i)
                src = a[G_LOADS[i]]
                src = src if i < 4 else src.rearrange("(o d) -> o d", o=1)
                sp.dma_start(gbc[:, :], src.to_broadcast([P, D])).then_inc(g_in, 16)

            sp.dma_start(x_sb[:, 0:2, :], x_d[:, 0:2, :]).then_inc(x_in[0], 16)
            load_g(0)
            sp.dma_start(w_lr, w_in_d[:, :, 1536:1552], allow_slow_non_contiguous=True).then_inc(w_landed["lr"], 16)
            sp.dma_start(x_sb[:, 2:4, :], x_d[:, 2:4, :]).then_inc(x_in[1], 16)
            sp.dma_start(w_qk, w_in_d[:, :, 512:1024]).then_inc(w_landed["qk"], 16)
            sp.dma_start(w_v, w_in_d[:, :, 1024:1536]).then_inc(w_landed["v"], 16)
            sp.dma_start(w_u, w_in_d[:, :, 0:512]).then_inc(w_landed["u"], 16)
            sp.dma_start(w_r, w_in_d[:, :, 1552:2064]).then_inc(w_landed["r"], 16)
            for h in range(2):
                evacuated(sp, "xt", 3, h)
            sp.dma_start(V[:, :, :], mem_d).then_inc(mem_in, 16)
            load_g(1)
            full(sp, "u", 3)
            sp.dma_start(w_xk, wsq["w_xk"]).then_inc(w_landed["w_xk"], 16)
            full(sp, "r", 3)
            sp.dma_start(w_xv, wsq["w_xv"]).then_inc(w_landed["w_xv"], 16)
            load_g(2)
            full(sp, "K", 3)
            sp.dma_start(w_out, wsq["w_out"]).then_inc(w_landed["w_out"], 16)
            sp.wait_ge(mixed, 4)
            evacuated(sp, "pool", 3)
            full(sp, "o", 3)
            sp.dma_start(w_xq, wsq["w_xq"]).then_inc(w_landed["w_xq"], 16)
            load_g(3)
            full(sp, "x1", 3, 1)
            sp.dma_start(w_xo, wsq["w_xo"]).then_inc(w_landed["w_xo"], 16)
            full(sp, "Q", 7)
            def expert_rows(name, e, g):
                return a[name][0, e].rearrange("(k p) n -> p k n", p=P)[:, GK * g:GK * g + GK, :]

            def gate_up_tiles(g):
                return wg[:, GK * g:GK * g + GK].rearrange("p k h n -> p k (h n)")

            for g in range(NG):
                sp.dma_start(wd[:, 0, GK * g:GK * g + GK, :], expert_rows("w_dn", 0, g)).then_inc(dn_in[0][g], 16)
            for g in range(NG // 2, NG):
                sp.dma_start(gate_up_tiles(g), expert_rows("w_gu", 0, g)).then_inc(gu_in[g], 16)
            full(sp, "x2", 3, 1)
            for g in range(NG // 2):
                sp.dma_start(gate_up_tiles(g), expert_rows("w_gu", 0, g)).then_inc(gu_in[g], 16)
            load_g(4)
            sp.wait_ge(added, 16 * TT)
            for g in range(NG):
                if g == NG // 2:
                    full(sp, "meta")
                sp.dma_start(wd[:, 1, GK * g:GK * g + GK, :], expert_rows("w_dn", 1, g)).then_inc(dn_in[1][g], 16)
            sp.wait_ge(ctl_ready, 1)
            blocks = sp.value_load(ctl[0:1, 1, 63:64], min_val=E, max_val=NBLK)

            def expert_of(b):
                return sp.value_load(ctl[0:1, 1, bass.ds(b, 1)], min_val=0, max_val=E - 1)

            def gate_up_load(b):
                w = a["w_gu"][0, bass.ds(expert_of(b), 1)].rearrange("o (k p) n -> p (o k) n", p=P)
                for g in range(NG):
                    sp.wait_ge(gu_used, NG * b - NG + g + 1)
                    sp.dma_start(gate_up_tiles(g), w[:, GK * g:GK * g + GK, :]).then_inc(gu_in[g], 16)

            def down_load(b, buffer, groups):
                w = a["w_dn"][0, bass.ds(expert_of(b), 1)].rearrange("o (k p) n -> p (o k) n", p=P)
                for g in groups:
                    sp.wait_ge(dn_used, NG * b - 2 * NG + g + 1)
                    sp.dma_start(wd[:, buffer, GK * g:GK * g + GK, :], w[:, GK * g:GK * g + GK, :]).then_inc(dn_in[buffer][g], 16)

            for g in range(NG):
                sp.wait_ge(gu_used, g + 1)
                sp.dma_start(gate_up_tiles(g), expert_rows("w_gu", 1, g)).then_inc(gu_in[g], 16)
            for g in range(LEAD):
                sp.wait_ge(dn_used, g + 1)
                sp.dma_start(wd[:, 0, GK * g:GK * g + GK, :], expert_rows("w_dn", 2, g)).then_inc(dn_in[0][g], 16)
            with sp.Fori(0, NBLK // 2) as i:
                for odd in range(2):
                    b = 2 * i + 2 + odd
                    with sp.If(b < blocks):
                        gate_up_load(b)
                        down_load(b, odd, range(LEAD, NG))
                    with sp.If(b + 1 < blocks):
                        down_load(b + 1, 1 - odd, range(LEAD))
            sp.wait_ge(all_added, 1)
            for t in range(TT):
                sp.dma_start(x_sb[:, t, :], acc_tok[:, t, :]).then_inc(final_in[t], 16)
            for t in range(TT):
                sp.wait_ge(normed, NORM["out", t] + 1)
                sp.dma_start(out_d[:, t, :], nrm_t[:, t, :]).then_inc(out_done, 16)
            sp.wait_ge(out_done, 16 * TT)

        @block.scalar
        def _(act):
            steps = [0]

            def step(ins):
                steps[0] += 1
                ins.then_inc(act_step, 1)
                act.wait_ge(act_step, steps[0])

            act.dma_start(cols[:, 0:4], a["pool_scale"].rearrange("o (g p) -> p (o g)", p=P),
                          allow_slow_non_contiguous=True).then_inc(small_in, 16)
            act.dma_start(cols[:, 4:6], a["b_gate_up"].rearrange("o (g p) -> p (o g)", p=P),
                          allow_slow_non_contiguous=True).then_inc(small_in, 16)
            act.dma_start(cols[:, 6:7], a["gla_norm_g"].rearrange("o p -> p o"),
                          allow_slow_non_contiguous=True).then_inc(small_in, 16)
            act.dma_start(w_gate[:, :], a["w_gate_up"][0]).then_inc(small_in, 16)
            act.dma_start(w_pool[:, :, :], a["w_pool"][0].rearrange("g c d -> c g d")).then_inc(small_in, 16)
            act.dma_start(w_rt[:, :, :], a["w_router"][0].rearrange("(k p) e -> p k e", p=P)).then_inc(small_in, 16)
            act.dma_start(b_rt[:, :], a["b_router"].to_broadcast([P, E])).then_inc(small_in, 16)

            def squares(name, t, src, dst):
                n = NORM[name, t]
                step(act.activation(dst, src, ACT.Square, scale=float(D) ** -0.5, accum_out=stat[:, 0, n:n + 1]))
                act.activation(stat[:, 1, n:n + 1], stat[:, 0, n:n + 1], ACT.Sqrt, bias=eps_c[:, 0:1]).then_inc(sq_sum, 1)

            def copy_bank(job, dst, src=None, **kw):
                ps = full(act, *job)
                act.activation(dst, ps[:, :] if src is None else src(ps), ACT.Copy, **kw).then_inc(freed(job), 1)

            act.wait_ge(consts, 4)
            for t in range(TT):
                act.wait_ge(x_in[t // 2], 16)
                squares("x", t, x_sb[:, t, :], nrm_t[:, t, :])
            for t in range(TT):
                copy_bank(("xt", t, 1), hT[:, 4:8, t * P:t * P + P], lambda ps: ps[:, :].rearrange("p (k n) -> p k n", k=4))
            act.wait_ge(mem_in, 16)
            copy_bank(("glr",), glr, lambda ps: ps[0:16, :])
            for i in range(2):
                evacuated(act, "xt", 1, 0)
                squares("mem", i, V[:, i, :], nrm_t[:, i, :])
            copy_bank(("k", 1), kg[:, 1, :])
            copy_bank(("q", 1), qg[:, 1, :], scale=float(CHUNK) ** -0.5)
            copy_bank(("v", 1), v_sb[:, 1, :])
            copy_bank(("v", 3), v_sb[:, 3, :])
            for p in range(2):
                act.wait_ge(gd, 2 * p + 1)
                step(act.activation(gtmp[:, p, :], gtmp[:, p, :], ACT.Exp, scale=-1.0))
                act.activation(gtmp[:, p, :], gtmp[:, p, :], ACT.Ln, bias=1.0).then_inc(gl, 1)
            for p in range(2):
                act.wait_ge(gd, 4 + p + 1)
                act.activation(qe[:, p, :], gc[:, p, :], ACT.Exp).then_inc(gl, 1)
                act.activation(ke[:, p, :], gc[:, p, :], ACT.Exp, scale=-1.0).then_inc(gl, 1)
                for c in range(8):
                    last = gc[:, p, c * CHUNK + CHUNK - 1:c * CHUNK + CHUNK]
                    act.activation(kd[:, p, c * CHUNK:(c + 1) * CHUNK], gc[:, p, c * CHUNK:(c + 1) * CHUNK], ACT.Exp,
                                   scale=-1.0, bias=last).then_inc(gl, 1)
            for g in (1, 3):
                copy_bank(("u", g), u_sb[:, g, PAD:])
            for h in range(4):
                copy_bank(("r", h), mixT[:, 4 + h, :])
            for t in range(2):
                evacuated(act, "xt", 3, 1)
                copy_bank(("mt", t, 1), hmT[:, 4:8, t * P:t * P + P], lambda ps: ps[:, :].rearrange("p (k n) -> p k n", k=4))
            copy_bank(("kd", 1), kd_tok[:, 1, :, :].rearrange("p t d -> p (t d)"))
            for h in range(4):
                if h == 0:
                    act.wait_ge(kd_ready, 6)
                evacuated(act, "r", h)
                act.activation(sig_r[:, h, :], mixT[:, 4 + h, :], ACT.Sigmoid).then_inc(sig_ready, 1)
            for g in range(4):
                ps = full(act, "pool", g)
                if g == 0:
                    act.wait_ge(small_in, 16 * 7)
                act.activation(mixT[:, g, :], ps[:, :], ACT.Copy, scale=cols[:, g:g + 1]).then_inc(freed(("pool", g)), 1)
            for c in range(4):
                copy_bank(("K", c), KT[:, 2 * c:2 * c + 2, :], lambda ps: ps[:, :].rearrange("p (a n) -> p a n", a=2))
            for h in range(4):
                evacuated(act, "o", h)
                if h >= 2:
                    full(act, "ss", h - 2)
                elif h == 0:
                    act.wait_ge(pooled, 4)
                act.activation(pool_s[:, h % 2, 0:T], o_sb[:, h, :], ACT.Square).then_inc(osq_ready, 1)
            copy_bank(("V", 0, 1), V[:, 0, 512:1024])
            for h in range(4):
                ps = full(act, "ss", h)
                if h:
                    act.wait_ge(mixed, h)
                act.activation(gc[:, 0, :], ps[:, :], ACT.Sqrt, bias=eps_c[:, 0:1]).then_inc(freed(("ss", h)), 1)
            copy_bank(("V", 1, 1), V[:, 1, 512:1024])
            for t in range(TT + 1):
                if t < TT:
                    evacuated(act, "x1", t, 0)
                    evacuated(act, "x1", t, 1)
                    if t == 0:
                        full(act, "V", 1, 1)
                        act.wait_ge(mixed, 4)
                    squares("x1", t, x_sb[:, t, :], nrm_t[:, t, :])
                if t:
                    copy_bank(("h2t", t - 1, 1), hT[:, 4:8, t * P - P:t * P], lambda ps: ps[:, :].rearrange("p (k n) -> p k n", k=4))
            for f in range(8):
                copy_bank(("Q", f), QT[:, f, :], scale=float(D // 4) ** -0.5)
            for h in range(4):
                for t in range(4):
                    act.wait_ge(maxed, 4 * h + 2 * (t // 2) + 2)
                    ps = full(act, "sc", h, t // 2)
                    if h == t == 0:
                        evacuated(act, "h2t", 3, 0)
                        evacuated(act, "h2t", 3, 1)
                    act.activation(prob[:, h, t, :], ps[:, (t % 2) * M:(t % 2) * M + M], ACT.Exp,
                                   bias=soft[:, 0, 4 * h + t:4 * h + t + 1],
                                   accum_out=soft[:, 1, 4 * h + t:4 * h + t + 1]).then_inc(exped, 1)
            for h in range(4):
                copy_bank(("pt", h, 1), pT[:, h, 1, :])
                copy_bank(("O", h, 1), mixT[:, 2 * h + 1, :])
            act.wait_ge(bias_in, 16 * 6)
            for i, q in enumerate((slice(0, 128), slice(64, 128), slice(96, 128))):
                if i:
                    act.wait_ge(bias_step, 2 * i)
                act.activation(bias3[q, :], b_all[q, :], ACT.Copy).then_inc(bias_step, 1)
            for t in range(TT + 1):
                if t < TT:
                    evacuated(act, "x2", t, 0)
                    evacuated(act, "x2", t, 1)
                    if t == 0:
                        for h in range(4):
                            for m in range(2):
                                evacuated(act, "pt", h, m)
                    squares("x2", t, x_sb[:, t, :], nrm_t[:, t, :])
                if t:
                    copy_bank(("h3t", t - 1, 1), hT[:, 4:8, t * P - P:t * P], lambda ps: ps[:, :].rearrange("p (k n) -> p k n", k=4))
            for t in range(TT):
                act.wait_ge(top_ready, t + 1)
                act.activation(gate4[:, t, :], top8[:, t, 0:4], ACT.Exp, bias=gsum[:, t:t + 1],
                               accum_out=gsum[:, 4 + t:5 + t]).then_inc(gate_exp, 1)

            def x_rows(b):
                act.wait_ge(xt_full, 2 * b + 1)
                act.activation(xT[:, 0:4, :], PS[4][:, :].rearrange("p (k n) -> p k n", k=4), ACT.Copy).then_inc(xT_ready, 1)

            def a_turned(b, s):
                act.wait_ge(at_full, NSUB * b + NSUB - s)
                act.activation(aT[:, s, :, :].rearrange("p c n -> p (c n)"), PS[s][:, 0:256], ACT.Copy).then_inc(aT_ready, 1)

            act.wait_ge(ctl_ready, 1)
            x_rows(0)
            blocks = act.value_load(ctl[0:1, 1, 63:64], min_val=E, max_val=NBLK)
            with act.Fori(0, NBLK) as b:
                with act.If(b < blocks):
                    n_sub = act.value_load(ctl[0:1, 0, bass.ds(b, 1)], min_val=0, max_val=NSUB)
                    with act.If(n_sub > 2):
                        for i, s in enumerate((3, 2)):
                            act.wait_ge(gate_min, NSUB * b + i + 1)
                            act.activation(sg_sb[:, s, :], gm_sb[:, s, :], ACT.Sigmoid, scale=SWIGLU_ALPHA).then_inc(sig_done, 1)
                    with act.Else():
                        for s in (3, 2):
                            act.nop().then_inc(sig_done, 1)
                    for i, s in enumerate((1, 0)):
                        act.wait_ge(gate_min, NSUB * b + i + 3)
                        act.activation(sg_sb[:, s, :], gm_sb[:, s, :], ACT.Sigmoid, scale=SWIGLU_ALPHA).then_inc(sig_done, 1)
                    with act.If(b + 1 < blocks):
                        x_rows(b + 1)
                    with act.If(n_sub > 2):
                        a_turned(b, 3)
                        a_turned(b, 2)
                    with act.Else():
                        for s in (3, 2):
                            act.nop().then_inc(aT_ready, 1)
                    a_turned(b, 1)
                    a_turned(b, 0)
            for t in range(TT):
                act.wait_ge(final_in[t], 16)
                squares("out", t, x_sb[:, t, :], nrm_t[:, t, :])

        @block.tensor
        def _(pe):
            def bank(*job):
                n = JOB[job]
                if n >= 8:
                    pe.wait_ge(bank_free[n % 8], n // 8)
                return PS[n % 8]

            def fills(job):
                return bank_full[JOB[job] % 8]

            def turn(job, src, width=P):
                ps = bank(*job)
                for i in range(4):
                    last = pe.transpose(ps[:, i * P:(i + 1) * P], src(i), ident[:, :])
                last.then_inc(fills(job), 1)

            def product(job, lhsT, rhs, n, width=512, rows=P, finish=True):
                ps = bank(*job)
                for k in range(n):
                    last = pe.matmul(ps[0:rows, 0:width], lhsT(k), rhs(k), start=(k == 0), stop=(k == n - 1))
                return last.then_inc(fills(job), 1)

            pe.wait_ge(consts, 4)
            for t in range(TT):
                pe.wait_ge(normed, NORM["x", t] + 1)
                for h in range(2):
                    turn(("xt", t, h), lambda i: nrm_t[:, t, (4 * h + i) * P:(4 * h + i + 1) * P])
            for t in range(TT):
                for h in range(2):
                    evacuated(pe, "xt", t, h)
            pe.wait_ge(w_landed["lr"], 16)
            product(("glr",), lambda k: w_lr[:, k, :], lambda k: hT[:, k, :], KD, rows=16)
            pe.wait_ge(w_landed["qk"], 16)
            for n in range(2):
                product(("k", n), lambda k: w_qk[:, k, 256 + n * P:256 + (n + 1) * P], lambda k: hT[:, k, :], KD)
            for n in range(2):
                product(("q", n), lambda k: w_qk[:, k, n * P:(n + 1) * P], lambda k: hT[:, k, :], KD)
            pe.wait_ge(w_landed["v"], 16)
            for t in range(TT):
                product(("v", t), lambda k: hT[:, k, t * P:(t + 1) * P], lambda k: w_v[:, k, :], KD)
            evacuated(pe, "glr")
            pe.wait_ge(small_in, 16 * 7)
            for n in range(2):
                product(("gate", n), lambda k: w_gate[:, n * P:(n + 1) * P], lambda k: glr, 1)
            pe.wait_ge(w_landed["u"], 16)
            for g in range(4):
                product(("u", g), lambda k: w_u[:, k, g * P:(g + 1) * P], lambda k: hT[:, k, :], KD)
            pe.wait_ge(w_landed["r"], 16)
            for h in range(4):
                product(("r", h), lambda k: w_r[:, k, h * P:(h + 1) * P], lambda k: hT[:, k, :], KD)
            for t in range(2):
                pe.wait_ge(normed, NORM["mem", t] + 1)
                for h in range(2):
                    turn(("mt", t, h), lambda i: nrm_t[:, t, (4 * h + i) * P:(4 * h + i + 1) * P])
            pe.wait_ge(kd_ready, 6)
            for p in range(2):
                ps = bank("kd", p)
                for t in range(4):
                    last = pe.transpose(ps[:, t * P:(t + 1) * P], kd[:, p, t * P:(t + 1) * P], ident[:, :])
                last.then_inc(fills(("kd", p)), 1)
            for t in range(4):
                evacuated(pe, "v", t)
            for p in range(2):
                evacuated(pe, "kd", p)
                for c in range(2):
                    ps = bank("ds", p, c)
                    for t in range(4):
                        for h in range(2):
                            last = pe.matmul(ps[64 * h:64 * h + 64, t * P:(t + 1) * P],
                                             kd_tok[64 * c:64 * c + 64, p, t, 64 * h:64 * h + 64],
                                             v_sb[64 * c:64 * c + 64, t, (2 * p + h) * P:(2 * p + h + 1) * P],
                                             start=True, stop=True)
                    last.then_inc(fills(("ds", p, c)), 1)
            for g in range(4):
                pe.wait_ge(pooled, g + 1)
                product(("pool", g), lambda k: w_pool[:, g, :], lambda k: u_sb[:, g, PAD:], 1)
            for h in range(4):
                ps = bank("att", h)
                lo = 64 * (h % 2)
                for t in range(4):
                    last = pe.matmul(ps[:, t * P:(t + 1) * P], ke[lo:lo + 64, h // 2, t * P:(t + 1) * P],
                                     qe[lo:lo + 64, h // 2, t * P:(t + 1) * P], start=True, stop=True)
                last.then_inc(fills(("att", h)), 1)
            for t in range(2):
                for h in range(2):
                    evacuated(pe, "mt", t, h)
            pe.wait_ge(w_landed["w_xk"], 16)
            for c in range(4):
                ps = bank("K", c)
                for f in range(2):
                    for k in range(KD):
                        last = pe.matmul(ps[:, f * M:(f + 1) * M], w_xk[:, k, (2 * c + f) * P:(2 * c + f + 1) * P], hmT[:, k, :],
                                         start=(k == 0), stop=(k == KD - 1))
                last.then_inc(fills(("K", c)), 1)
            pe.wait_ge(states, 2)
            for h in range(4):
                evacuated(pe, "att", h)
                ps = bank("o", h)
                lo = 64 * (h % 2)
                for t in range(4):
                    pe.matmul(ps[:, t * P:(t + 1) * P], v_sb[:, t, h * P:(h + 1) * P], att[:, h, t, :], start=True, stop=False)
                    for c in (2 * t, 2 * t + 1):
                        last = pe.matmul(ps[:, c * CHUNK:(c + 1) * CHUNK], S_prev[lo:lo + 64, h // 2, c, :],
                                         qe[lo:lo + 64, h // 2, c * CHUNK:(c + 1) * CHUNK], start=False, stop=(c % 2 == 1))
                last.then_inc(fills(("o", h)), 1)
            pe.wait_ge(w_landed["w_xv"], 16)

            def values(m):
                for n in range(2):
                    product(("V", m, n), lambda k: hmT[:, k, m * P:(m + 1) * P], lambda k: w_xv[:, k, n * 512:(n + 1) * 512], KD)

            values(0)
            for h in range(4):
                pe.wait_ge(osq_ready, h + 1)
                product(("ss", h), lambda k: ones[:, :], lambda k: pool_s[:, h % 2, 0:T], 1)
            values(1)

            def residual_and_turn(product_name, turn_name, norm_name, w, behind=None):
                for t in range(TT + 1):
                    if t < TT:
                        for n in range(2):
                            product((product_name, t, n), lambda k: mixT[:, k, t * P:(t + 1) * P],
                                    lambda k: w[:, k, n * 512:(n + 1) * 512], KD)
                    if behind and t > 1:
                        behind(t - 2)
                    if t:
                        pe.wait_ge(normed, NORM[norm_name, t - 1] + 1)
                        for h in range(2):
                            turn((turn_name, t - 1, h), lambda i: nrm_t[:, t - 1, (4 * h + i) * P:(4 * h + i + 1) * P])

            pe.wait_ge(w_landed["w_out"], 16)
            for g in range(4):
                evacuated(pe, "pool", g)
            pe.wait_ge(mixed, 4)
            residual_and_turn("x1", "h2t", "x1", w_out)
            for t in range(TT):
                for h in range(2):
                    evacuated(pe, "h2t", t, h)
            pe.wait_ge(w_landed["w_xq"], 16)
            for f in range(8):
                product(("Q", f), lambda k: w_xq[:, k, f * P:(f + 1) * P], lambda k: hT[:, k, :], KD)
            for h in range(4):
                for f in range(2):
                    evacuated(pe, "Q", 2 * h + f)
                for b in range(2):
                    ps = bank("sc", h, b)
                    for t in (2 * b, 2 * b + 1):
                        for f in range(2):
                            last = pe.matmul(ps[:, (t % 2) * M:(t % 2) * M + M], QT[:, 2 * h + f, t * P:(t + 1) * P],
                                             KT[:, 2 * h + f, :], start=(f == 0), stop=(f == 1))
                    last.then_inc(fills(("sc", h, b)), 1)
            for h in range(4):
                pe.wait_ge(prob_ready, 4 * h + 4)
                for m in range(2):
                    ps = bank("pt", h, m)
                    for t in range(4):
                        last = pe.transpose(ps[:, t * P:(t + 1) * P], prob[:, h, t, m * P:(m + 1) * P], ident[:, :])
                    last.then_inc(fills(("pt", h, m)), 1)
            for h in range(4):
                for m in range(2):
                    evacuated(pe, "pt", h, m)
                for c in range(2):
                    product(("O", h, c), lambda m: V[:, m, (2 * h + c) * P:(2 * h + c + 1) * P], lambda m: pT[:, h, m, :], MT)
            for h in range(4):
                for c in range(2):
                    evacuated(pe, "O", h, c)
            pe.wait_ge(w_landed["w_xo"], 16)

            def router(t):
                for h in range(2):
                    evacuated(pe, "h3t", t, h)
                product(("lg", t), lambda k: hT[:, k, t * P:(t + 1) * P], lambda k: w_rt[:, k, :], KD, width=E)

            residual_and_turn("x2", "h3t", "x2", w_xo, behind=router)
            router(TT - 1)
            pe.wait_ge(mask_ready, 1)
            ps = bank("rank")
            for t in range(TT + 1):
                for s in range(min(t + 1, TT)):
                    last = pe.matmul(ps[:, t * E:(t + 1) * E], before[:, :] if s == t else ones_b[:, :], maskb[:, s, :],
                                     start=(s == 0), stop=(s == min(t, TT - 1)))
            last.then_inc(fills(("rank",)), 1)
            ps = bank("tab")
            for i in range(4 * TT):
                if i % 4 == 0:
                    pe.wait_ge(vals_ready, i // 4 + 1)
                last = pe.matmul(ps[:, 0:2 * NB], onehot_p[:, i, :], vals[:, i, :, :].rearrange("p c b -> p (c b)"),
                                 start=(i == 0), stop=(i == 4 * TT - 1))
            last.then_inc(fills(("tab",)), 1)
            pe.wait_ge(vals_ready, 5)
            pe.wait_ge(consts, 6)
            ps = bank("meta")
            for s in range(4):
                last = pe.matmul(ps[:, s * 2 * NB:(s + 1) * 2 * NB], spread[:, s, :], tabv.rearrange("p c b -> p (c b)"),
                                 start=True, stop=True)
            last.then_inc(fills(("meta",)), 1)

            def rows_turn(b):
                pe.wait_ge(gathered, 16 * b + 16)
                for h in range(2):
                    for i in range(4):
                        last = pe.transpose(PS[4 + h][:, i * P:(i + 1) * P], xg[:, (4 * h + i) * P:(4 * h + i + 1) * P], ident[:, :])
                    last.then_inc(xt_full, 1)

            def a_turn(b, s):
                pe.wait_ge(a_ready, NSUB * b + NSUB - s)
                for c in range(2):
                    last = pe.transpose(PS[s][:, c * P:(c + 1) * P], a_sb[:, s, c * P:(c + 1) * P], ident[:, :])
                last.then_inc(at_full, 1)

            pe.wait_ge(ctl_ready, 1)
            pe.wait_ge(bias_step, 5)
            blocks = pe.value_load(ctl[0:1, 1, 63:64], min_val=E, max_val=NBLK)
            rows_turn(0)
            evacuated(pe, "meta")
            with pe.Fori(0, NBLK) as b:
                with pe.If(b < blocks):
                    n_sub = pe.value_load(ctl[0:1, 0, bass.ds(b, 1)], min_val=0, max_val=NSUB)
                    pe.wait_ge(xT_ready, 2 * b + 2)
                    pe.wait_ge(sel_ready, b + 1)

                    def gate_up(s, g):
                        for j in range(NCOL):
                            ps = PS[s][SUB * j:SUB * (j + 1), :].rearrange("p (h n) -> p h n", h=2)
                            if g == 0:
                                pe.matmul(ps, sel[:, :], bias3[:, 0:2 * F].rearrange("p (h n) -> p h n", h=2)[:, :, j * FQ:(j + 1) * FQ],
                                          start=True, stop=False)
                        for k in range(GK * g, GK * g + GK):
                            for j in range(NCOL):
                                ps = PS[s][SUB * j:SUB * (j + 1), :].rearrange("p (h n) -> p h n", h=2)
                                last = pe.matmul(ps, xT[:, k, SUB * s:SUB * (s + 1)], wg[:, k, :, j * FQ:(j + 1) * FQ],
                                                 start=False, stop=(k == KD - 1))
                        return last

                    def down(s, g, buffer):
                        if g == 0:
                            for j in range(NCOL):
                                pe.matmul(PS[4 + s][SUB * j:SUB * (j + 1), 0:DQ], sel[:, :],
                                          bias3[:, 2 * F + j * DQ:2 * F + (j + 1) * DQ], start=True, stop=False)
                        for k in range(GK * g, GK * g + GK):
                            for j in range(NCOL):
                                last = pe.matmul(PS[4 + s][SUB * j:SUB * (j + 1), 0:DQ],
                                                 aT[:, s, k % 2, SUB * (k // 2):SUB * (k // 2 + 1)],
                                                 wd[:, buffer, k, j * DQ:(j + 1) * DQ], start=False, stop=(k == KF - 1))
                        return last

                    for g in range(NG - 1):
                        pe.wait_ge(gu_in[g], 16 * b + 16)
                        for s in range(NSUB - 1, 0, -1):
                            with pe.If(n_sub > s):
                                gate_up(s, g)
                        gate_up(0, g).then_inc(gu_used, 1)
                    pe.wait_ge(gu_in[NG - 1], 16 * b + 16)
                    for s in range(NSUB - 1, 0, -1):
                        with pe.If(n_sub > s):
                            gate_up(s, NG - 1).then_inc(sub_done, 1)
                        with pe.Else():
                            pe.nop().then_inc(sub_done, 1)
                    gate_up(0, NG - 1).then_inc(gu_used, 1)
                    with pe.If(b + 1 < blocks):
                        pe.wait_ge(y_ready, NSUB * b + NSUB)
                        rows_turn(b + 1)
                    with pe.If(n_sub > 2):
                        a_turn(b, 3)
                        a_turn(b, 2)
                    with pe.Else():
                        for s in (3, 2):
                            pe.nop().then_inc(at_full, 1)
                    a_turn(b, 1)
                    a_turn(b, 0)
                    with pe.If(b + 1 < blocks):
                        pe.wait_ge(xT_ready, 2 * b + 4)
                    pe.wait_ge(y_ready, NSUB * b + NSUB)
                    pe.wait_ge(aT_ready, NSUB * b + NSUB)

                    def down_all(buffer):
                        for g in range(NG):
                            pe.wait_ge(dn_in[buffer][g], 8 * b + 16 - 8 * buffer)
                            for s in range(NSUB - 1, 0, -1):
                                with pe.If(n_sub > s):
                                    down(s, g, buffer)
                            down(0, g, buffer).then_inc(dn_used, 1)

                    parity = pe.value_load(ctl[0:1, 2, bass.ds(b, 1)], min_val=0, max_val=1)
                    with pe.If(parity > 0):
                        down_all(1)
                    with pe.Else():
                        down_all(0)

        @block.vector
        def _(dve):
            steps = [0]

            def step(ins):
                steps[0] += 1
                ins.then_inc(dve_step, 1)
                dve.wait_ge(dve_step, steps[0])

            def norm(name, t, src, g):
                n = NORM[name, t]
                dve.wait_ge(sq_sum, n + 1)
                dve.wait_ge(g_in, 16 * (g + 1))
                step(dve.reciprocal(stat[:, 2, n:n + 1], stat[:, 1, n:n + 1]))
                return dve.scalar_tensor_tensor(out=nrm_t[:, t, :], in0=src, scalar=stat[:, 2, n:n + 1], in1=gbc[:, :],
                                                op0=ALU.mult, op1=ALU.mult).then_inc(normed, 1)

            def copy_bank(job, dst, src=None):
                ps = full(dve, *job)
                dve.tensor_copy(dst, ps[:, :] if src is None else src(ps)).then_inc(freed(job), 1)

            def gains_used(n):
                dve.wait_ge(normed, n)
                dve.engine_nop().then_inc(g_used, 1)

            step(dve.memset(pool_s[:, :, 0:PAD], 0.0))
            step(dve.memset(u_sb[:, :, 0:PAD], 0.0))
            for t in range(TT):
                norm("x", t, x_sb[:, t, :], 0)
            gains_used(TT)
            for t in range(TT):
                copy_bank(("xt", t, 0), hT[:, 0:4, t * P:t * P + P], lambda ps: ps[:, :].rearrange("p (k n) -> p k n", k=4))
            for t in range(MT):
                norm("mem", t, V[:, t, :], 1)
            gains_used(TT + MT)
            copy_bank(("k", 0), kg[:, 0, :])
            ps = full(dve, "q", 0)
            dve.tensor_scalar(qg[:, 0, :], ps[:, :], float(CHUNK) ** -0.5, None, ALU.mult).then_inc(freed(("q", 0)), 1)
            copy_bank(("v", 0), v_sb[:, 0, :])
            copy_bank(("v", 2), v_sb[:, 2, :])
            dve.wait_ge(small_in, 16 * 7)
            for p in range(2):
                ps = full(dve, "gate", p)
                dve.wait_ge(consts, 4)
                step(dve.tensor_scalar(gc[:, p, :], ps[:, :], cols[:, 4 + p:5 + p], None, ALU.add))
                dve.scalar_tensor_tensor(out=gtmp[:, p, :], in0=gc[:, p, :], scalar=-1.0, in1=gc[:, p, :],
                                         op0=ALU.mult, op1=ALU.max).then_inc(gd, 1)
                dve.wait_ge(gd, 2 * p + 1)
                dve.tensor_scalar(gc[:, p, :], gc[:, p, :], 0.0, None, ALU.min).then_inc(gd, 1)
                dve.wait_ge(gd, 2 * p + 2)
                dve.engine_nop().then_inc(freed(("gate", p)), 1)
            keep = pool_s[:, 0, PAD:PAD + T]
            step(dve.memset(keep, 1.0))
            step(dve.memset(keep.rearrange("p (c i) -> p c i", i=CHUNK)[:, :, 0:1], 0.0))
            for p in range(2):
                dve.wait_ge(gl, p + 1)
                step(dve.tensor_tensor(gtmp[:, p, :], gc[:, p, :], gtmp[:, p, :], ALU.subtract))
                step(dve.tensor_scalar(gtmp[:, p, :], gtmp[:, p, :], 1.0 / GATE_NORMALIZER, None, ALU.mult))
                dve.tensor_tensor_scan(gc[:, p, :], keep, gtmp[:, p, :], 0.0, ALU.mult, ALU.add).then_inc(gd, 1)
            for p in range(2):
                base = 2 + 10 * p
                evacuated(dve, "q", p)
                evacuated(dve, "k", p)
                dve.wait_ge(gl, base + 10)
                for dst, src in ((qe, qg), (ke, kg), (kd, kg)):
                    if dst is qe:
                        step(dve.tensor_copy(soft[:, 2 + p, 0:8],
                                             qe[:, p, :].rearrange("p (c i) -> p c i", i=CHUNK)[:, :, CHUNK - 1]))
                    dve.tensor_tensor(dst[:, p, :], dst[:, p, :], src[:, p, :], ALU.mult).then_inc(kd_ready, 1)
            for g in (0, 2):
                copy_bank(("u", g), u_sb[:, g, PAD:])
            for g, w in enumerate(WINDOWS):
                evacuated(dve, "u", g)
                src, n = u_sb[:, g, :], 1
                i = 0
                while n < w:
                    dst = pool_s[:, i % 2, :]
                    step(dve.tensor_tensor(dst[:, PAD:], src[:, PAD:], src[:, PAD - n:PAD + T - n], ALU.add))
                    src, n, i = dst, 2 * n, i + 1
                step(dve.tensor_tensor(soft[:, 1, 0:w], src[:, PAD:PAD + w], inv_cnt[:, 0:w], ALU.mult))
                step(dve.tensor_tensor(soft[:, 1, 0:w], soft[:, 1, 0:w], u_sb[:, g, PAD:PAD + w], ALU.subtract))
                step(dve.scalar_tensor_tensor(out=u_sb[:, g, PAD:], in0=src[:, PAD:], scalar=1.0 / w, in1=u_sb[:, g, PAD:],
                                              op0=ALU.mult, op1=ALU.subtract))
                dve.tensor_copy(u_sb[:, g, PAD:PAD + w], soft[:, 1, 0:w]).then_inc(pooled, 1)
                dve.wait_ge(pooled, g + 1)
            for t in range(2):
                for m in range(2):
                    evacuated(dve, "xt", 3, m)
                copy_bank(("mt", t, 0), hmT[:, 0:4, t * P:t * P + P], lambda ps: ps[:, :].rearrange("p (k n) -> p k n", k=4))
            copy_bank(("kd", 0), kd_tok[:, 0, :, :].rearrange("p t d -> p (t d)"))
            evacuated(dve, "r", 3)
            step(dve.memset(att.rearrange("p h t i -> p (h t i)"), 0.0))
            for p in range(2):
                even, odd = full(dve, "ds", p, 0), full(dve, "ds", p, 1)
                step(dve.memset(S_prev[:, p, 0, :], 0.0))
                for c in range(7):
                    src = (even, odd)[c % 2][:, (c // 2) * P:(c // 2 + 1) * P]
                    step(dve.scalar_tensor_tensor(out=S_prev[:, p, c + 1, :], in0=S_prev[:, p, c, :],
                                                  scalar=soft[:, 2 + p, c:c + 1], in1=src, op0=ALU.mult, op1=ALU.add))
                dve.engine_nop().then_inc(freed(("ds", p, 0)), 1)
                dve.engine_nop().then_inc(freed(("ds", p, 1)), 1)
                dve.engine_nop().then_inc(states, 1)
            for h in range(4):
                ps = full(dve, "att", h)
                for t in range(4):
                    last = dve.copy_predicated(att[:, h, t, :], causal[:, :].bitcast(U32), ps[:, t * P:(t + 1) * P])
                    if t < 3:
                        step(last)
                last.then_inc(freed(("att", h)), 1)
            for h in range(4):
                if h == 0:
                    for t in range(2):
                        evacuated(dve, "mt", t, 0)
                        evacuated(dve, "mt", t, 1)
                copy_bank(("o", h), o_sb[:, h, :])
            copy_bank(("V", 0, 0), V[:, 0, 0:512])
            for h in range(4):
                dve.wait_ge(sig_ready, h + 1)
                step(dve.tensor_tensor(sig_r[:, h, :], sig_r[:, h, :], mixT[:, 4 + h, :], ALU.mult))
                step(dve.scalar_tensor_tensor(out=sig_r[:, h, :], in0=o_sb[:, h, :], scalar=cols[:, 6:7], in1=sig_r[:, h, :],
                                              op0=ALU.mult, op1=ALU.mult))
                evacuated(dve, "ss", h)
                step(dve.reciprocal(gc[:, 1, :], gc[:, 0, :]))
                dve.tensor_tensor(mixT[:, 4 + h, :], sig_r[:, h, :], gc[:, 1, :], ALU.mult).then_inc(mixed, 1)
                dve.wait_ge(mixed, h + 1)

            def residual(job, t, n):
                ps = full(dve, *job)
                dve.tensor_tensor(x_sb[:, t, n * 512:(n + 1) * 512], x_sb[:, t, n * 512:(n + 1) * 512], ps[:, :],
                                  ALU.add).then_inc(freed(job), 1)

            copy_bank(("V", 1, 0), V[:, 1, 0:512])

            def residual_and_norm(product_name, turn_name, norm_name, g, behind=None):
                for t in range(TT + 1):
                    if t < TT:
                        for n in range(2):
                            residual((product_name, t, n), t, n)
                    if t:
                        copy_bank((turn_name, t - 1, 0), hT[:, 0:4, t * P - P:t * P], lambda ps: ps[:, :].rearrange("p (k n) -> p k n", k=4))
                    if t < TT:
                        norm(norm_name, t, x_sb[:, t, :], g)
                    if behind and t > 1:
                        behind(t - 2)

            residual_and_norm("x1", "h2t", "x1", 2)
            gains_used(2 * TT + MT)
            for h in range(4):
                for t in range(4):
                    ps = full(dve, "sc", h, t // 2)
                    dve.tensor_reduce(soft[:, 0, 4 * h + t:4 * h + t + 1], ps[:, (t % 2) * M:(t % 2) * M + M], AX.X, ALU.max,
                                      negate=True).then_inc(maxed, 1)
                for t in range(4):
                    i = 4 * h + t
                    dve.wait_ge(exped, i + 1)
                    step(dve.reciprocal(soft[:, 2, i:i + 1], soft[:, 1, i:i + 1]))
                    dve.tensor_scalar(prob[:, h, t, :], prob[:, h, t, :], soft[:, 2, i:i + 1], None, ALU.mult).then_inc(prob_ready, 1)
                    if t % 2:
                        dve.engine_nop().then_inc(freed(("sc", h, t // 2)), 1)
            for h in range(4):
                copy_bank(("pt", h, 0), pT[:, h, 0, :])
                copy_bank(("O", h, 0), mixT[:, 2 * h, :])
            def top_four(t):
                ps = full(dve, "lg", t)
                dve.wait_ge(consts, 5)
                dve.tensor_tensor(logits[:, t, :], ps[:, 0:E], b_rt[:, :], ALU.add).then_inc(freed(("lg", t)), 1)
                evacuated(dve, "lg", t)
                step(dve.max(top8[:, t, :], logits[:, t, :]))
                dve.tensor_scalar(gsum[:, t:t + 1], top8[:, t, 0:1], -1.0, None, ALU.mult).then_inc(top_ready, 1)
                step(dve.max_index(idx8[:, t, :], top8[:, t, :], logits[:, t, :]))

            for i, q in enumerate((slice(64, 128), slice(96, 128))):
                dve.wait_ge(bias_step, 2 * i + 1)
                dve.tensor_tensor(b_all[q, :], b_all[q, :], bias3[q, :], ALU.subtract).then_inc(bias_step, 1)
            dve.wait_ge(bias_step, 5)
            residual_and_norm("x2", "h3t", "x2", 3, behind=top_four)
            gains_used(3 * TT + MT)
            top_four(TT - 1)

            step(dve.tensor_copy(idxf, idx8[:, :, 0:4].rearrange("p t k -> p k t")))
            iota_kte = iota_e.rearrange("p (k t e) -> p k t e", k=1, t=1).to_broadcast([P, 4, TT, E])
            step(dve.tensor_tensor(oh, iota_kte, idxf.rearrange("p k (t o) -> p k t o", o=1).to_broadcast([P, 4, TT, E]), ALU.is_equal))
            step(dve.tensor_tensor(prod[:, 0:2], oh[:, 0:2], oh[:, 2:4], ALU.add))
            dve.tensor_tensor(maskb, prod[:, 0], prod[:, 1], ALU.add).then_inc(mask_ready, 1)
            dve.wait_ge(gate_exp, TT)
            step(dve.reciprocal(gsum[:, 4:8], gsum[:, 4:8]))
            step(dve.tensor_tensor(gate4, gate4, gsum[:, 4:8].rearrange("p (t o) -> p t o", o=1).to_broadcast([P, TT, 4]), ALU.mult))
            ps = full(dve, "rank")
            dve.tensor_copy(rank.rearrange("p t e -> p (t e)"), ps[:, 0:5 * E]).then_inc(freed(("rank",)), 1)
            evacuated(dve, "rank")
            cnt, rk = rank[:, 4, :], rank[:, 0:4, :]
            step(dve.tensor_scalar(more[:, :], cnt, float(P), None, ALU.is_gt))
            for i in (2, 3):
                step(dve.scalar_tensor_tensor(out=more[:, :], in0=cnt, scalar=float(i * P), in1=more[:, :], op0=ALU.is_gt, op1=ALU.add))
            step(dve.tensor_tensor_scan(xend[:, :], one_e[:, :], more[:, :], 0.0, ALU.mult, ALU.add))
            step(dve.tensor_tensor(xoff[:, :], xend[:, :], more[:, :], ALU.subtract))
            step(dve.scalar_tensor_tensor(out=xoff[:, :], in0=xoff[:, :], scalar=float(E - 1), in1=iota_e, op0=ALU.add, op1=ALU.subtract))
            step(dve.tensor_scalar(lvl[:, 0], rk, float(P), None, ALU.is_ge))
            step(dve.scalar_tensor_tensor(out=lvl[:, 1], in0=rk, scalar=float(2 * P), in1=lvl[:, 0], op0=ALU.is_ge, op1=ALU.add))
            step(dve.scalar_tensor_tensor(out=lvl[:, 1], in0=rk, scalar=float(3 * P), in1=lvl[:, 1], op0=ALU.is_ge, op1=ALU.add))
            step(dve.scalar_tensor_tensor(out=rk, in0=lvl[:, 1], scalar=-float(P), in1=rk, op0=ALU.mult, op1=ALU.add))
            step(dve.tensor_tensor(lvl[:, 0], lvl[:, 0], xoff.rearrange("p (o e) -> p o e", o=1).to_broadcast([P, TT, E]), ALU.mult))
            step(dve.tensor_tensor(lvl[:, 0], lvl[:, 0], lvl[:, 1], ALU.add))
            step(dve.tensor_tensor(lvl[:, 0], lvl[:, 0], iota_e.rearrange("p (o e) -> p o e", o=1).to_broadcast([P, TT, E]), ALU.add))
            for dst, src in ((pos16, rk), (blk16, lvl[:, 0])):
                step(dve.tensor_tensor(prod, oh, src.rearrange("p (o t) e -> p o t e", o=1).to_broadcast([P, 4, TT, E]), ALU.mult))
                step(dve.tensor_reduce(dst, prod, AX.X, ALU.add))
            step(dve.tensor_tensor(inblk, iota_b.rearrange("p (k t b) -> p k t b", k=1, t=1).to_broadcast([P, 4, TT, NB]),
                                   blk16.rearrange("p k (t o) -> p k t o", o=1).to_broadcast([P, 4, TT, NB]), ALU.is_equal))
            vals4 = vals.rearrange("p (k t) c b -> p k t c b", k=4)
            step(dve.tensor_tensor(vals4[:, :, :, 0, :], inblk, tokp.rearrange("p (k t b) -> p k t b", k=1, b=1).to_broadcast([P, 4, TT, NB]), ALU.mult))
            step(dve.tensor_tensor(vals4[:, :, :, 1, :], inblk,
                                   gate4.rearrange("p t (k b) -> p k t b", b=1).to_broadcast([P, 4, TT, NB]), ALU.mult))
            for k in range(4):
                dve.tensor_tensor(onehot_p[:, TT * k:TT * k + TT, :], iota_p.rearrange("p (t s) -> p t s", t=1).to_broadcast([P, TT, P]),
                                  pos16[:, k, :].rearrange("p (t s) -> p t s", s=1).to_broadcast([P, TT, P]), ALU.is_equal).then_inc(vals_ready, 1)
            step(dve.tensor_scalar(nsubf[:, 0:E], cnt, 0.0, None, ALU.is_gt))
            for i in range(1, NSUB):
                step(dve.scalar_tensor_tensor(out=nsubf[:, 0:E], in0=cnt, scalar=float(i * SUB), in1=nsubf[:, 0:E], op0=ALU.is_gt, op1=ALU.add))
            step(dve.memset(nsubf[:, E:NB], float(NSUB)))
            step(dve.tensor_copy(ebc[:, 0:E], iota_e[:, :]))
            xsum = inblk.rearrange("p k t b -> p (k t b)")[:, 0:(NB - E) * E].rearrange("p (i e) -> p i e", e=E)
            step(dve.tensor_tensor(xsum, xend.rearrange("p (i e) -> p i e", i=1).to_broadcast([P, NB - E, E]),
                                   iota_b[:, 0:NB - E].rearrange("p (i e) -> p i e", e=1).to_broadcast([P, NB - E, E]), ALU.is_le))
            step(dve.tensor_reduce(ebc[:, E:NB], xsum, AX.X, ALU.add))
            step(dve.tensor_scalar(ebc[:, :], ebc[:, :], float(E - 1), None, ALU.min))
            step(dve.tensor_copy(ctl[0:1, 0, 0:NB], nsubf[0:1, 0:NB]))
            step(dve.tensor_copy(ctl[0:1, 1, 0:NB], ebc[0:1, 0:NB]))
            parities = ctl[0:1, 2, :].rearrange("o (i a) -> o i a", a=2)
            for i in range(2):
                step(dve.memset(parities[:, :, i], i))
            step(dve.tensor_scalar(ctl[0:1, 1, 63:64], xend[0:1, E - 1:E], float(E), None, ALU.add))
            dve.engine_nop().then_inc(ctl_ready, 1)
            ps = full(dve, "tab")
            dve.tensor_copy(tabv.rearrange("p c b -> p (c b)"), ps[:, 0:2 * NB]).then_inc(vals_ready, 1)
            dve.wait_ge(vals_ready, 5)
            dve.tensor_scalar(gidx, tabv[:, 0, :], -1.0, 0.0, ALU.add, ALU.max).then_inc(freed(("tab",)), 1)
            evacuated(dve, "tab")

            def pick_row(b):
                dve.tensor_scalar(cur_i[:, 0:1], gidx[:, bass.ds(b, 1)], 0.0, None, ALU.add).then_inc(row_picked, 1)

            def pick_bias(b):
                dve.tensor_scalar(sel[:, :], ebc[:, bass.ds(b, 1)].to_broadcast([P, SUB]), row_e[:, 0:1], None,
                                  ALU.is_equal).then_inc(sel_ready, 1)

            pick_row(0)
            pick_bias(0)
            ps = full(dve, "meta")
            dve.tensor_copy(meta.rearrange("p s c b -> p (s c b)"), ps[:, 0:8 * NB]).then_inc(freed(("meta",)), 1)
            evacuated(dve, "meta")
            row = meta[:, :, 0, :]
            empty = inblk.rearrange("p k t b -> p (k t) b")[:, 0:NSUB, :]
            step(dve.tensor_scalar(empty, row, 0.0, 16384.0, ALU.is_equal, ALU.mult))
            step(dve.scalar_tensor_tensor(out=row, in0=row, scalar=float(NCOL), in1=empty, op0=ALU.mult, op1=ALU.add))
            step(dve.tensor_scalar(row, row, jcol[:, 0:1], None, ALU.add))

            blocks = dve.value_load(ctl[0:1, 1, 63:64], min_val=E, max_val=NBLK)

            def swiglu(b, s, i):
                dve.tensor_scalar(gm_sb[:, s, :], PS[s][:, 0:FQ], SWIGLU_LIMIT, None, ALU.min).then_inc(gate_min, 1)
                dve.tensor_scalar(up_sb[:, s, :], PS[s][:, FQ:2 * FQ], SWIGLU_LIMIT, -SWIGLU_LIMIT, ALU.min, ALU.max).then_inc(moe_step, 1)
                dve.wait_ge(gate_min, NSUB * b + i + 1)
                dve.wait_ge(moe_step, PER * b + 2 * i + 1)
                dve.scalar_tensor_tensor(out=up_sb[:, s, :], in0=up_sb[:, s, :], scalar=1.0, in1=gm_sb[:, s, :],
                                         op0=ALU.add, op1=ALU.mult).then_inc(moe_step, 1)
                dve.wait_ge(moe_step, PER * b + 2 * i + 2)
                dve.wait_ge(sig_done, NSUB * b + i + 1)
                dve.tensor_tensor(a_sb[:, s, :], up_sb[:, s, :], sg_sb[:, s, :], ALU.mult).then_inc(a_ready, 1)

            def x_rows(b):
                dve.wait_ge(xt_full, 2 * b + 2)
                dve.tensor_copy(xT[:, 4:8, :], PS[5][:, :].rearrange("p (k n) -> p k n", k=4)).then_inc(xT_ready, 1)

            def scale(s):
                dve.tensor_scalar(y_sb[:, s, :], PS[4 + s][:, 0:DQ], cur_g[:, s:s + 1], None, ALU.mult).then_inc(y_ready, 1)

            PER = 2 * NSUB + 2
            for s in range(NSUB):
                dve.engine_nop().then_inc(y_ready, 1)
            x_rows(0)
            with dve.Fori(0, NBLK) as b:
                with dve.If(b < blocks):
                    n_sub = dve.value_load(ctl[0:1, 0, bass.ds(b, 1)], min_val=0, max_val=NSUB)
                    dve.wait_ge(gathered, 16 * b + 16)
                    pick_row(b + 1)
                    with dve.If(n_sub > 2):
                        dve.wait_ge(sub_done, 3 * b + 1)
                        swiglu(b, 3, 0)
                        dve.wait_ge(sub_done, 3 * b + 2)
                        swiglu(b, 2, 1)
                    with dve.Else():
                        for s in (3, 2):
                            dve.engine_nop().then_inc(gate_min, 1)
                            dve.engine_nop().then_inc(moe_step, 1)
                            dve.engine_nop().then_inc(moe_step, 1)
                            dve.engine_nop().then_inc(a_ready, 1)
                    dve.wait_ge(sub_done, 3 * b + 3)
                    swiglu(b, 1, 2)
                    dve.wait_ge(gu_used, NG * b + NG)
                    swiglu(b, 0, 3)
                    with dve.If(b + 1 < blocks):
                        x_rows(b + 1)
                    dve.wait_ge(block_added, b + 1)
                    dve.tensor_scalar(cur_i[:, 4:4 + NSUB], meta[:, :, 0, bass.ds(b, 1)].rearrange("p s o -> p (s o)"),
                                      0.0, None, ALU.add).then_inc(moe_step, 1)
                    dve.tensor_scalar(cur_g[:, :], meta[:, :, 1, bass.ds(b, 1)].rearrange("p s o -> p (s o)"),
                                      0.0, None, ALU.add).then_inc(moe_step, 1)
                    dve.wait_ge(dn_used, NG * b + 1)
                    pick_bias(b + 1)
                    dve.wait_ge(moe_step, PER * b + PER)
                    dve.wait_ge(dn_used, NG * b + NG)
                    scale(0)
                    scale(1)
                    with dve.If(n_sub > 2):
                        scale(2)
                        scale(3)
                    with dve.Else():
                        for s in (2, 3):
                            dve.engine_nop().then_inc(y_ready, 1)
            for t in range(TT):
                norm("out", t, x_sb[:, t, :], 4)

        @block.gpsimd
        def _(pool):
            steps = [0]

            def step(ins, s=pool_step):
                steps[0] += 1
                ins.then_inc(pool_step, 1)
                pool.wait_ge(pool_step, steps[0])

            step(pool.memset(ident[:, :], 0.0))
            pool.affine_select(out=ident[:, :], in_=ident[:, :], compare_op=ALU.not_equal, fill=1.0, base=0,
                               pattern=[[-1, P]], channel_multiplier=1).then_inc(consts, 1)
            step(pool.memset(eps_c[:, :], EPS))
            step(pool.memset(ones[:, :], 1.0 / P))
            step(pool.memset(ones_b[:, :], 1.0))
            step(pool.memset(before[:, :], 1.0))
            pool.affine_select(out=before[:, :], in_=before[:, :], compare_op=ALU.is_gt, fill=0.0, base=0,
                               pattern=[[1, P]], channel_multiplier=-1).then_inc(consts, 1)
            step(pool.memset(causal[:, :], 1.0))
            step(pool.affine_select(out=causal[:, :], in_=causal[:, :], compare_op=ALU.is_ge, fill=0.0, base=0,
                                    pattern=[[1, P]], channel_multiplier=-1))
            pool.memset(causal[0:64, 64:128], 0.0).then_inc(consts, 1)
            for t in range(PAD):
                step(pool.memset(inv_cnt[:, t:t + 1], 1.0 / (t + 1)))
            pool.nop().then_inc(consts, 1)

            for h in range(4):
                evacuated(pool, "sc", h, 1)
            step(pool.iota(iota_e[:, :], pattern=[[1, E]], base=0, channel_multiplier=0, allow_small_or_imprecise_dtypes=True))
            step(pool.iota(iota_b[:, :], pattern=[[1, NB]], base=0, channel_multiplier=0, allow_small_or_imprecise_dtypes=True))
            step(pool.iota(iota_p[:, :], pattern=[[1, P]], base=0, channel_multiplier=0, allow_small_or_imprecise_dtypes=True))
            step(pool.iota(tokp[:, :], pattern=[[P, 4]], base=1, channel_multiplier=1, allow_small_or_imprecise_dtypes=True))
            step(pool.iota(pcol[:, 0:1], pattern=[[0, 1]], base=0, channel_multiplier=1, allow_small_or_imprecise_dtypes=True))
            for j in range(4):
                q = slice(32 * j, 32 * j + 32)
                step(pool.tensor_scalar(row_e[q, 0:1], pcol[q, 0:1], float(-32 * j), None, ALU.add))
                step(pool.memset(jcol[q, 0:1], float(j - NCOL)))
            step(pool.memset(one_e[:, :], 1.0))
            pool.nop().then_inc(consts, 1)
            for h in range(4):
                for c in range(2):
                    evacuated(pool, "O", h, c)
            step(pool.memset(b_all[32:64, :], 0.0))
            for i in (0, 2, 3):
                q = slice(32 * i, 32 * i + 32)
                pool.dma_start(b_all[q, 0:2 * F], a["b_gu"][0]).then_inc(bias_in, 16)
                pool.dma_start(b_all[q, 2 * F:2 * F + D], a["b_dn"][0]).then_inc(bias_in, 16)
            for t in range(TT):
                pool.wait_ge(normed, NORM["x2", t] + 1)
                pool.dma_start(h3_tok[:, t, :], nrm_t[:, t, :]).then_inc(h3_out, 16)
                pool.dma_start(acc_tok[:, t, :], x_sb[:, t, :]).then_inc(added, 16)
            full(pool, "x2", 3, 1)
            step(pool.memset(spread.rearrange("p s q -> p (s q)"), 0.0))
            for s in range(NSUB):
                part = spread[:, s, :].rearrange("p (j r) -> p j r", j=4)
                step(pool.affine_select(out=part, in_=part, compare_op=ALU.not_equal, fill=1.0, base=-SUB * s,
                                        pattern=[[0, 4], [-1, SUB]], channel_multiplier=1))
            pool.nop().then_inc(consts, 1)

            pool.wait_ge(h3_out, 16 * TT)
            pool.wait_ge(added, 16 * TT)
            gathered_end, added_end = pool.alloc_register("gathered_end"), pool.alloc_register("added_end")
            pool.reg_mov(gathered_end, 16)
            pool.reg_mov(added_end, 16 * TT)

            def gather():
                pool.indirect_dma_start(xg, None, h3_d, bass.IndirectOffsetOnAxis(ap=cur_i[:, 0:1], axis=0)).then_inc(gathered, 16)

            pool.wait_ge(ctl_ready, 1)
            blocks = pool.value_load(ctl[0:1, 1, 63:64], min_val=E, max_val=NBLK)
            pool.wait_ge(row_picked, 1)
            gather()
            with pool.Fori(0, NBLK) as b:
                with pool.If(b < blocks):
                    pool.wait_ge(row_picked, b + 2)
                    n_sub = pool.value_load(ctl[0:1, 0, bass.ds(b, 1)], min_val=0, max_val=NSUB)
                    pool.wait_ge(xt_full, 2 * b + 2)
                    pool.reg_add(gathered_end, gathered_end, 16)
                    gather()
                    pool.wait_ge(added, pool.snap(added_end))
                    pool.nop().then_inc(block_added, 1)
                    for s in range(NSUB):
                        with pool.If(n_sub > s):
                            pool.wait_ge(y_ready, NSUB * b + NSUB + s + 1)
                            pool.reg_add(added_end, added_end, 16)
                            pool.indirect_dma_start(acc_d, bass.IndirectOffsetOnAxis(ap=cur_i[:, 4 + s:5 + s], axis=0), y_sb[:, s, :], None,
                                                    bounds_check=T * NCOL - 1, oob_is_err=False, compute_op=ALU.add).then_inc(added, 16)
            gathered_all, added_all = pool.snap(gathered_end), pool.snap(added_end)
            pool.wait_ge(gathered, gathered_all)
            pool.tensor_tensor(pool_end[0:1, 0:1], eps_c[0:1, 0:1], eps_c[0:1, 0:1], ALU.add)
            pool.wait_ge(added, added_all)
            pool.tensor_tensor(pool_end[0:1, 1:2], eps_c[0:1, 0:1], eps_c[0:1, 0:1], ALU.add).then_inc(all_added, 1)



_INS = ["x", "mem", "norm_mix_g", "w_in", "w_pool", "pool_scale", "w_gate_up", "b_gate_up", "gla_norm_g", "w_out",
        "norm_xattn_g", "norm_mem_g", "w_xq", "w_xk", "w_xv", "w_xo", "norm_moe_g", "w_router", "b_router",
        "w_gu", "b_gu", "w_dn", "b_dn", "norm_final_g"]


def kernel(**inputs):
    import numpy as _np
    import concourse.bacc as _bacc
    from concourse import mybir as _mybir
    from concourse.bass_utils import run_bass_kernel_spmd as _run

    nc = _bacc.Bacc("TRN2", target_bir_lowering=False, num_devices=1)
    arrays, aps = {}, {}
    for name in _INS:
        arr = _np.ascontiguousarray(inputs[name])
        arrays[f"in_{name}"] = arr
        aps[name] = nc.dram_tensor(f"in_{name}", arr.shape, _mybir.dt.from_np(arr.dtype), kind="ExternalInput").ap()
    out = nc.dram_tensor("out_0", inputs["x"].shape, _mybir.dt.float32, kind="ExternalOutput").ap()
    decoder_layer(nc, aps, out)
    r = _run(nc, [arrays], core_ids=[0])
    return r.results[0]["out_0"]
```

```python
from contextlib import ExitStack

import concourse.bass as bass
from concourse import mybir

F32 = mybir.dt.float32
BF16 = mybir.dt.bfloat16
I32 = mybir.dt.int32
U32 = mybir.dt.uint32
ALU = mybir.AluOpType
ACT = mybir.ActivationFunctionType
AX = mybir.AxisListType

P = 128
EPS = 1e-6
WINDOWS = (2, 4, 8, 16)
PAD = 16
GATE_NORMALIZER = 16.0
SWIGLU_LIMIT = 7.0
SWIGLU_ALPHA = 1.702
CHUNK = 64
SUB = 32
NSUB = P // SUB
NCOL = P // SUB


def lagged(product, turned):
    o = []
    for t in range(5):
        if t < 4:
            o += [(product, t, n) for n in range(2)]
        if t and turned == "h3t" and t > 1:
            o += [("lg", t - 2)]
        if t:
            o += [(turned, t - 1, h) for h in range(2)]
    return o


def job_order():
    o = [("xt", t, h) for t in range(4) for h in range(2)]
    o += [("glr",), ("k", 0), ("k", 1), ("q", 0), ("q", 1)]
    o += [("v", t) for t in range(4)]
    o += [("gate", 0), ("gate", 1)]
    o += [("u", g) for g in range(4)]
    o += [("r", h) for h in range(4)]
    o += [("mt", t, h) for t in range(2) for h in range(2)]
    o += [("kd", 0), ("kd", 1)]
    o += [("ds", p, c) for p in range(2) for c in range(2)]
    o += [("pool", g) for g in range(4)]
    o += [("att", h) for h in range(4)]
    o += [("K", c) for c in range(3)]
    o += [("o", h) for h in range(4)]
    o += [("K", 3)]
    o += [("ss", h) for h in range(4)]
    o += [("V", m, n) for m in range(2) for n in range(2)]
    o += lagged("x1", "h2t")
    o += [("Q", f) for f in range(8)]
    o += [("sc", h, a) for h in range(4) for a in range(2)]
    o += [("pt", h, m) for h in range(4) for m in range(2)]
    o += [("O", h, c) for h in range(4) for c in range(2)]
    o += lagged("x2", "h3t")
    o += [("lg", 3), ("rank",), ("tab",), ("meta",)]
    return o


ORDER = job_order()
JOB = {name: n for n, name in enumerate(ORDER)}


def decoder_layer(nc, a, out):
    T, D = a["x"].shape[1:]
    M = a["mem"].shape[1]
    E = a["w_gu"].shape[1]
    F = a["w_dn"].shape[2]
    TT, KD, KF, MT = T // P, D // P, F // P, M // P
    TOPK = 4
    assert TT == NSUB
    MAX_EXTRA = T * TOPK // (P + 1)
    NBLK = E + MAX_EXTRA
    NB = NBLK + 1
    BEYOND = float(32 * T)
    STRETCH = 16
    STRETCHES = NB // STRETCH
    GK = 2
    NG = KD // GK
    LEAD = 2
    FQ, DQ = F // NCOL, D // NCOL

    x_d = a["x"].rearrange("o (t p) d -> p (o t) d", p=P)
    mem_d = a["mem"].rearrange("o (t p) d -> p (o t) d", p=P)
    out_d = out.rearrange("o (t p) d -> p (o t) d", p=P)
    w_in_d = a["w_in"].rearrange("o (k p) n -> p (o k) n", p=P)
    wsq = {n: a[n].rearrange("o (k p) n -> p (o k) n", p=P) for n in ("w_out", "w_xq", "w_xk", "w_xv", "w_xo")}
    h3_d = nc.dram_tensor("h3_rows", (T, D), F32).ap()
    acc_d = nc.dram_tensor("acc_rows", (T * NCOL, DQ), F32).ap()
    acc_tok = acc_d.rearrange("(t p j) d -> p t (j d)", p=P, j=NCOL)
    h3_tok = h3_d.rearrange("(t p) d -> p t d", p=P)

    with ExitStack() as ctx:
        def sb(name, shape, dt=F32):
            return ctx.enter_context(nc.sbuf_tensor(name, shape, dt))

        def sem(name):
            return ctx.enter_context(nc.semaphore(name))

        big = sb("big", [P, 4 * 8192])
        W = big[:, 0:3 * 8192]
        x_sb = big[:, 3 * 8192:3 * 8192 + 4096].rearrange("p (t d) -> p t d", t=TT)
        mixT = big[:, 3 * 8192 + 4096:4 * 8192].rearrange("p (k n) -> p k n", k=KD)
        nrm = sb("nrm", [P, 4096])
        hT = sb("hT", [P, KD, T])
        qreg = sb("qreg", [P, 4096])
        KT = sb("KT", [P, KD, M])
        V = sb("V", [P, MT, D])
        pool_s = sb("pool_s", [P, 2, PAD + T])
        gbc = sb("gbc", [P, D])

        ident = sb("ident", [P, P])
        ones = sb("ones", [P, P])
        causal = sb("causal", [P, P])
        before = sb("before", [P, P], BF16)
        ones_b = sb("ones_b", [P, P], BF16)
        w_pool = sb("w_pool_sb", [P, 4, P])
        w_gate = sb("w_gate_sb", [P, 256])
        w_rt = sb("w_router_sb", [P, KD, E])
        b_rt = sb("b_router_sb", [P, E])
        cols = sb("cols", [P, 8])
        stat = sb("stat", [P, 3, 24])
        inv_cnt = sb("inv_cnt", [P, PAD])
        eps_c = sb("eps_c", [P, 1])
        pool_end = sb("pool_end", [1, 2])
        soft = sb("soft", [P, 4, 16])
        sel = sb("sel", [P, SUB], BF16)
        ctl = sb("ctl", [1, 3, 64], I32)
        cur_i = sb("cur_i", [P, 8], I32)
        cur_g = sb("cur_g", [P, 4])

        w_in_cols = a["w_in"].shape[2]
        assert w_in_cols == 2064
        R0, R1, R2 = W[:, 0:8192], W[:, 8192:16384], W[:, 16384:24576]
        w_u = R0[:, 0:4096].rearrange("p (k n) -> p k n", k=KD)
        w_qk = R0[:, 4096:8192].rearrange("p (k n) -> p k n", k=KD)
        w_v = R1[:, 0:4096].rearrange("p (k n) -> p k n", k=KD)
        w_r = R1[:, 4096:8192].rearrange("p (k n) -> p k n", k=KD)
        sq = [R[:, :].rearrange("p (k n) -> p k n", k=KD) for R in (R0, R1, R2)]
        w_xk, w_out, w_xo = sq[0], sq[0], sq[0]
        w_xv = sq[1]
        w_xq = sq[2]
        u_sb = R2[:, 0:2112].rearrange("p (g n) -> p g n", g=4)
        qg = R2[:, 2112:3136].rearrange("p (a n) -> p a n", a=2)
        kg = R2[:, 3136:4160].rearrange("p (a n) -> p a n", a=2)
        sig_r = R2[:, 2112:4160].rearrange("p (h n) -> p h n", h=4)
        gc = R2[:, 4160:5184].rearrange("p (a n) -> p a n", a=2)
        v_sb = R2[:, 5184:7232].rearrange("p (t n) -> p t n", t=4)
        lg_part_sb = causal[:, :]
        stack = w_pool[:, 0, 0:E]
        glr = R2[:, 7232:7744]
        w_lr = R2[:, 7744:8000].rearrange("p (k n) -> p k n", k=KD)
        qe = qreg[:, 0:1024].rearrange("p (a n) -> p a n", a=2)
        ke = qreg[:, 1024:2048].rearrange("p (a n) -> p a n", a=2)
        kd = qreg[:, 2048:3072].rearrange("p (a n) -> p a n", a=2)
        gtmp = qreg[:, 3072:4096].rearrange("p (a n) -> p a n", a=2)
        kd_tok = qreg[:, 3072:4096].rearrange("p (a t d) -> p a t d", a=2, t=4)
        QT = qreg[:, :].rearrange("p (f n) -> p f n", f=8)
        hflat = hT[:, :, :].rearrange("p k n -> p (k n)")
        att = hflat[:, 0:2048].rearrange("p (h t i) -> p h t i", h=4, t=4)
        S_prev = hflat[:, 2048:4096].rearrange("p (a c e) -> p a c e", a=2, c=8)
        pT = hflat.rearrange("p (h m n) -> p h m n", h=4, m=2)
        nrm_t = nrm[:, :].rearrange("p (t d) -> p t d", t=4)
        hmT = nrm[:, 2048:4096].rearrange("p (k m) -> p k m", k=KD)
        o_sb = nrm[:, 0:2048].rearrange("p (h n) -> p h n", h=4)
        prob = nrm[:, :].rearrange("p (h t m) -> p h t m", h=4, t=4)

        def rt(lo, n):
            return qreg[:, lo:lo + n]
        logits = rt(0, 128).rearrange("p (t e) -> p t e", t=4)
        top8 = rt(128, 32).rearrange("p (t k) -> p t k", t=4)
        idx8 = rt(160, 32).bitcast(U32).rearrange("p (t k) -> p t k", t=4)
        idxf = rt(192, 16).rearrange("p (k t) -> p k t", t=4)
        gate4 = rt(208, 16).rearrange("p (t k) -> p t k", t=4)
        gsum = rt(224, 8)
        oh = rt(256, 512).rearrange("p (k t e) -> p k t e", k=4, t=4)
        prod = rt(768, 512).rearrange("p (k t e) -> p k t e", k=4, t=4)
        maskb = rt(1280, 64).bitcast(BF16).rearrange("p (t e) -> p t e", t=4)
        rank = rt(1344, 160).rearrange("p (t e) -> p t e", t=5)
        full1, level = (rt(1504 + 16 * i, 16).rearrange("p (k t) -> p k t", k=4) for i in range(2))
        more, xend, xoff = rt(1760, 32), rt(1792, 32), rt(1824, 32)
        pos16 = rt(1856, 16).rearrange("p (k t) -> p k t", k=4)
        blk16 = rt(1872, 16).rearrange("p (k t) -> p k t", k=4)
        inblk = rt(1888, 16 * NB).rearrange("p (k t b) -> p k t b", k=4, t=4)
        onehot_p = V[:, :, :].rearrange("p m d -> p (m d)").rearrange("p (i s) -> p i s", i=16)
        vals = mixT[:, 0:3, :].rearrange("p k n -> p (k n)").rearrange("p (i c b) -> p i c b", i=16, c=2)
        spread = mixT[:, 3, :].rearrange("p (s q) -> p s q", s=4)
        iota_b = rt(2656, NB)
        iota_e = rt(2704, 32)
        iota_p = rt(2736, 128)
        tokp = rt(2864, 4)
        one_e = rt(2868, 32)
        pcol, jcol = rt(2900, 1), rt(2901, 1)
        row_e = rt(2902, 1)
        gidx_next = rt(3528, NB + 1)
        gidx = gidx_next[:, 0:NB]
        tabv = rt(2952, 2 * NB).rearrange("p (c b) -> p c b", c=2)
        meta = rt(3048, 8 * NB).rearrange("p (s c b) -> p s c b", s=4, c=2)
        ebc_next = rt(3584, NB + 1)
        ebc = ebc_next[:, 0:NB]
        nsubf = rt(3480, NB)
        assert NB == 48 and 2 * F + D == 3072
        bias3 = KT[:, 0:6, :].rearrange("p k n -> p (k n)").bitcast(BF16)
        b_all = R1[:, 4096:4096 + 3072]
        xg = nrm[:, 0:1024]
        a_sb = nrm[:, 1024:2048].rearrange("p (s n) -> p s n", s=4)
        y_sb = nrm[:, 2048:3072].rearrange("p (s n) -> p s n", s=4)
        up_sb = nrm[:, 3072:4096].rearrange("p (s n) -> p s n", s=4)
        xT = hflat[:, 0:1024].rearrange("p (k n) -> p k n", k=8)
        aT = hflat[:, 1024:2048].rearrange("p (s c n) -> p s c n", s=4, c=2)
        gm_sb = hflat[:, 2048:3072].rearrange("p (s n) -> p s n", s=4)
        sg_sb = hflat[:, 3072:4096].rearrange("p (s n) -> p s n", s=4)
        wg = W[:, 0:16384].rearrange("p (k h n) -> p k h n", k=KD, h=2)
        wd = big[:, 16384:32768].rearrange("p (a k n) -> p a k n", a=2, k=KF)

        PS = [ctx.enter_context(nc.psum_tensor(f"bank{i}", [P, 512], F32)) for i in range(8)]

        bank_full = [sem(f"bank_full{i}") for i in range(8)]
        bank_free = [sem(f"bank_free{i}") for i in range(8)]
        x_in = [sem(f"x_in{t}") for t in range(TT)]
        mem_in, small_in, g_in, consts = sem("mem_in"), sem("small_in"), sem("g_in"), sem("consts")
        w_landed = {n: sem(f"landed_{n}") for n in ("qk", "lr", "v", "u", "r", "w_xk", "w_xv", "w_out", "w_xq", "w_xo")}
        g_used, cleared = sem("g_used"), sem("cleared")
        lg_parts, lg_copied, stack_ready = sem("lg_parts"), sem("lg_copied"), sem("stack_ready")
        sq_sum = sem("sq_sum")
        normed = sem("normed")
        gate_logs = sem("gate_logs")
        gate_dve = sem("gate_dve")
        kd_ready, pooled, states, osq_ready, mixed = sem("kd_ready"), sem("pooled"), sem("states"), sem("osq_ready"), sem("mixed")
        sig_ready = sem("sig_ready")
        maxed, exped, prob_ready = sem("maxed"), sem("exped"), sem("prob_ready")
        act_step, dve_step, pool_step = sem("act_step"), sem("dve_step"), sem("pool_step")
        h3_out = sem("h3_out")
        top_ready, gate_exp, mask_ready, vals_ready = sem("top_ready"), sem("gate_exp"), sem("mask_ready"), sem("vals_ready")
        ctl_ready = sem("ctl_ready")
        bias_in, bias_step = sem("bias_in"), sem("bias_step")
        gu_in = [sem(f"gu_in{g}") for g in range(NG)]
        dn_in = [[sem(f"dn_in{i}_{g}") for g in range(NG)] for i in range(2)]
        gu_used, dn_used = sem("gu_used"), sem("dn_used")
        row_picked, sel_ready, gathered, xt_full, xT_ready = sem("row_picked"), sem("sel_ready"), sem("gathered"), sem("xt_full"), sem("xT_ready")
        sub_done, gate_min, sig_done, a_ready = sem("sub_done"), sem("gate_min"), sem("sig_done"), sem("a_ready")
        at_full, aT_ready, y_ready, added = sem("at_full"), sem("aT_ready"), sem("y_ready"), sem("added")
        block_added = sem("block_added")
        moe_step = sem("moe_step")
        all_added, out_done = sem("all_added"), sem("out_done")
        final_in = [sem(f"final_in{t}") for t in range(TT)]

        block = ctx.enter_context(nc.Block())

        def full(eng, *job):
            n = JOB[job]
            eng.wait_ge(bank_full[n % 8], n // 8 + 1)
            return PS[n % 8]

        def freed(job):
            return bank_free[JOB[job] % 8]

        def evacuated(eng, *job):
            n = JOB[job]
            eng.wait_ge(bank_free[n % 8], n // 8 + 1)

        NORMS = [("x", t) for t in range(TT)] + [("mem", t) for t in range(MT)] + [("x1", t) for t in range(TT)] + \
                [("x2", t) for t in range(TT)] + [("out", t) for t in range(TT)]
        NORM = {n: i for i, n in enumerate(NORMS)}

        G_LOADS = ["norm_mix_g", "norm_mem_g", "norm_xattn_g", "norm_moe_g", "norm_final_g"]

        @block.sync
        def _(sp):
            def load_g(i):
                if i:
                    sp.wait_ge(g_used, i)
                src = a[G_LOADS[i]]
                src = src if i < 4 else src.rearrange("(o d) -> o d", o=1)
                sp.dma_start(gbc[:, :], src.to_broadcast([P, D])).then_inc(g_in, 16)

            sp.dma_start(x_sb[:, 0, :], x_d[:, 0, :]).then_inc(x_in[0], 16)
            load_g(0)
            for t in range(1, TT):
                sp.dma_start(x_sb[:, t, :], x_d[:, t, :]).then_inc(x_in[t], 16)
            sp.wait_ge(cleared, 2)
            sp.dma_start(w_lr[:, :, 0:16], w_in_d[:, :, 1536:1552], allow_slow_non_contiguous=True).then_inc(w_landed["lr"], 16)
            sp.dma_start(w_qk, w_in_d[:, :, 512:1024]).then_inc(w_landed["qk"], 16)
            sp.dma_start(w_v, w_in_d[:, :, 1024:1536]).then_inc(w_landed["v"], 16)
            sp.dma_start(cols[:, 0:4], a["pool_scale"].rearrange("o (g p) -> p (o g)", p=P),
                         allow_slow_non_contiguous=True).then_inc(small_in, 16)
            sp.dma_start(cols[:, 4:6], a["b_gate_up"].rearrange("o (g p) -> p (o g)", p=P),
                         allow_slow_non_contiguous=True).then_inc(small_in, 16)
            sp.dma_start(cols[:, 6:7], a["gla_norm_g"].rearrange("o p -> p o"),
                         allow_slow_non_contiguous=True).then_inc(small_in, 16)
            for j in range(4):
                sp.dma_start(w_gate[32 * j:32 * j + 16, :], a["w_gate_up"][0]).then_inc(small_in, 16)
            sp.dma_start(w_pool[:, :, :], a["w_pool"][0].rearrange("g c d -> c g d")).then_inc(small_in, 16)
            sp.dma_start(w_rt[:, :, :], a["w_router"][0].rearrange("(k p) e -> p k e", p=P)).then_inc(small_in, 16)
            sp.dma_start(b_rt[:, :], a["b_router"].to_broadcast([P, E])).then_inc(small_in, 16)
            sp.dma_start(w_u, w_in_d[:, :, 0:512]).then_inc(w_landed["u"], 16)
            sp.dma_start(w_r, w_in_d[:, :, 1552:2064]).then_inc(w_landed["r"], 16)
            for h in range(2):
                evacuated(sp, "xt", 3, h)
            sp.dma_start(V[:, :, :], mem_d).then_inc(mem_in, 16)
            load_g(1)
            full(sp, "u", 3)
            sp.dma_start(w_xk, wsq["w_xk"]).then_inc(w_landed["w_xk"], 16)
            full(sp, "r", 3)
            sp.dma_start(w_xv, wsq["w_xv"]).then_inc(w_landed["w_xv"], 16)
            load_g(2)
            full(sp, "K", 3)
            sp.dma_start(w_out, wsq["w_out"]).then_inc(w_landed["w_out"], 16)
            sp.wait_ge(mixed, 4)
            evacuated(sp, "pool", 3)
            full(sp, "o", 3)
            sp.dma_start(w_xq, wsq["w_xq"]).then_inc(w_landed["w_xq"], 16)
            load_g(3)
            full(sp, "x1", 3, 1)
            sp.dma_start(w_xo, wsq["w_xo"]).then_inc(w_landed["w_xo"], 16)
            full(sp, "Q", 7)
            def expert_rows(name, e, g):
                return a[name][0, e].rearrange("(k p) n -> p k n", p=P)[:, GK * g:GK * g + GK, :]

            def gate_up_tiles(g):
                return wg[:, GK * g:GK * g + GK].rearrange("p k h n -> p k (h n)")

            for g in range(NG):
                sp.dma_start(wd[:, 0, GK * g:GK * g + GK, :], expert_rows("w_dn", 0, g)).then_inc(dn_in[0][g], 16)
            for g in range(NG // 2, NG):
                if g == NG - 1:
                    sp.wait_ge(bias_step, 5)
                sp.dma_start(gate_up_tiles(g), expert_rows("w_gu", 0, g)).then_inc(gu_in[g], 16)
            full(sp, "x2", 3, 1)
            for g in range(NG // 2):
                sp.dma_start(gate_up_tiles(g), expert_rows("w_gu", 0, g)).then_inc(gu_in[g], 16)
            load_g(4)
            sp.wait_ge(added, 16 * TT)
            for g in range(NG):
                if g == NG // 2:
                    full(sp, "meta")
                sp.dma_start(wd[:, 1, GK * g:GK * g + GK, :], expert_rows("w_dn", 1, g)).then_inc(dn_in[1][g], 16)
            sp.wait_ge(ctl_ready, 1)
            blocks = sp.value_load(ctl[0:1, 1, 63:64], min_val=E, max_val=NBLK)

            def expert_of(b):
                return sp.value_load(ctl[0:1, 1, bass.ds(b, 1)], min_val=0, max_val=E - 1)

            def gate_up_load(b):
                w = a["w_gu"][0, bass.ds(expert_of(b), 1)].rearrange("o (k p) n -> p (o k) n", p=P)
                for g in range(NG):
                    sp.wait_ge(gu_used, NG * b - NG + g + 1)
                    sp.dma_start(gate_up_tiles(g), w[:, GK * g:GK * g + GK, :]).then_inc(gu_in[g], 16)

            def down_load(b, buffer, groups):
                w = a["w_dn"][0, bass.ds(expert_of(b), 1)].rearrange("o (k p) n -> p (o k) n", p=P)
                for g in groups:
                    sp.wait_ge(dn_used, NG * b - 2 * NG + g + 1)
                    sp.dma_start(wd[:, buffer, GK * g:GK * g + GK, :], w[:, GK * g:GK * g + GK, :]).then_inc(dn_in[buffer][g], 16)

            for g in range(NG):
                sp.wait_ge(gu_used, g + 1)
                sp.dma_start(gate_up_tiles(g), expert_rows("w_gu", 1, g)).then_inc(gu_in[g], 16)
            for g in range(LEAD):
                sp.wait_ge(dn_used, g + 1)
                sp.dma_start(wd[:, 0, GK * g:GK * g + GK, :], expert_rows("w_dn", 2, g)).then_inc(dn_in[0][g], 16)
            with sp.Fori(0, STRETCHES) as o:
                with sp.If(STRETCH * o + 2 < blocks):
                    with sp.Fori(0, STRETCH // 2) as i:
                        for odd in range(2):
                            b = STRETCH * o + 2 * i + 2 + odd
                            with sp.If(b < blocks):
                                gate_up_load(b)
                                down_load(b, odd, range(LEAD, NG))
                            with sp.If(b + 1 < blocks):
                                down_load(b + 1, 1 - odd, range(LEAD))
            sp.wait_ge(all_added, 1)
            for t in range(TT):
                sp.dma_start(x_sb[:, t, :], acc_tok[:, t, :]).then_inc(final_in[t], 16)
            for t in range(TT):
                sp.wait_ge(normed, NORM["out", t] + 1)
                sp.dma_start(out_d[:, t, :], nrm_t[:, t, :]).then_inc(out_done, 16)
            sp.wait_ge(out_done, 16 * TT)

        @block.scalar
        def _(act):
            steps = [0]

            def step(ins):
                steps[0] += 1
                ins.then_inc(act_step, 1)
                act.wait_ge(act_step, steps[0])

            def squares(name, t, src, dst):
                n = NORM[name, t]
                step(act.activation(dst, src, ACT.Square, scale=float(D) ** -0.5, accum_out=stat[:, 0, n:n + 1]))
                act.activation(stat[:, 1, n:n + 1], stat[:, 0, n:n + 1], ACT.Sqrt, bias=eps_c[:, 0:1]).then_inc(sq_sum, 1)

            def copy_bank(job, dst, src=None, **kw):
                ps = full(act, *job)
                act.activation(dst, ps[:, :] if src is None else src(ps), ACT.Copy, **kw).then_inc(freed(job), 1)

            def keys(c):
                copy_bank(("K", c), KT[:, 2 * c:2 * c + 2, :], lambda ps: ps[:, :].rearrange("p (a n) -> p a n", a=2))

            def sqrt_table(i):
                act.activation(stat[:, 1, 22 + i:23 + i], eps_c[:, 0:1], ACT.Sqrt)

            act.wait_ge(consts, 1)
            sqrt_table(0)
            for t in range(TT):
                act.wait_ge(x_in[t], 16)
                squares("x", t, x_sb[:, t, :], nrm_t[:, t, :])
            for t in range(TT):
                copy_bank(("xt", t, 1), hT[:, 4:8, t * P:t * P + P], lambda ps: ps[:, :].rearrange("p (k n) -> p k n", k=4))
            act.wait_ge(mem_in, 16)
            copy_bank(("glr",), glr)
            for i in range(2):
                evacuated(act, "xt", 1, 0)
                squares("mem", i, V[:, i, :], nrm_t[:, i, :])
            copy_bank(("k", 1), kg[:, 1, :])
            copy_bank(("q", 1), qg[:, 1, :], scale=float(CHUNK) ** -0.5)
            copy_bank(("v", 1), v_sb[:, 1, :])
            copy_bank(("v", 3), v_sb[:, 3, :])
            for p in range(2):
                act.wait_ge(gate_dve, 2 * p + 1)
                step(act.activation(gtmp[:, p, :], gtmp[:, p, :], ACT.Exp, scale=-1.0))
                act.activation(gtmp[:, p, :], gtmp[:, p, :], ACT.Ln, bias=1.0).then_inc(gate_logs, 1)
            for p in range(2):
                act.wait_ge(gate_dve, 4 + p + 1)
                act.activation(qe[:, p, :], gc[:, p, :], ACT.Exp).then_inc(gate_logs, 1)
                act.activation(ke[:, p, :], gc[:, p, :], ACT.Exp, scale=-1.0).then_inc(gate_logs, 1)
                for c in range(8):
                    last = gc[:, p, c * CHUNK + CHUNK - 1:c * CHUNK + CHUNK]
                    act.activation(kd[:, p, c * CHUNK:(c + 1) * CHUNK], gc[:, p, c * CHUNK:(c + 1) * CHUNK], ACT.Exp,
                                   scale=-1.0, bias=last).then_inc(gate_logs, 1)
            for g in (1, 3):
                copy_bank(("u", g), u_sb[:, g, PAD:])
            for h in range(4):
                copy_bank(("r", h), mixT[:, 4 + h, :])
            for t in range(2):
                evacuated(act, "xt", 3, 1)
                copy_bank(("mt", t, 1), hmT[:, 4:8, t * P:t * P + P], lambda ps: ps[:, :].rearrange("p (k n) -> p k n", k=4))
            copy_bank(("kd", 1), kd_tok[:, 1, :, :].rearrange("p t d -> p (t d)"))
            for h in range(4):
                if h == 0:
                    act.wait_ge(kd_ready, 6)
                evacuated(act, "r", h)
                act.activation(sig_r[:, h, :], mixT[:, 4 + h, :], ACT.Sigmoid).then_inc(sig_ready, 1)
            for g in range(4):
                ps = full(act, "pool", g)
                if g == 0:
                    act.wait_ge(small_in, 16 * 10)
                act.activation(mixT[:, g, :], ps[:, :], ACT.Copy, scale=cols[:, g:g + 1]).then_inc(freed(("pool", g)), 1)
            for c in range(3):
                keys(c)
            for h in range(4):
                evacuated(act, "o", h)
                if h >= 2:
                    full(act, "ss", h - 2)
                elif h == 0:
                    act.wait_ge(pooled, 4)
                act.activation(pool_s[:, h % 2, 0:T], o_sb[:, h, :], ACT.Square).then_inc(osq_ready, 1)
                if h == 1:
                    keys(3)
            for h in range(4):
                ps = full(act, "ss", h)
                if h:
                    act.wait_ge(mixed, h)
                act.activation(gc[:, 0, :], ps[:, :], ACT.Sqrt, bias=eps_c[:, 0:1]).then_inc(freed(("ss", h)), 1)
            for m in range(2):
                copy_bank(("V", m, 1), V[:, m, 512:1024])
            for t in range(TT + 1):
                if t < TT:
                    evacuated(act, "x1", t, 0)
                    evacuated(act, "x1", t, 1)
                    if t == 0:
                        full(act, "V", 1, 1)
                        act.wait_ge(mixed, 4)
                    squares("x1", t, x_sb[:, t, :], nrm_t[:, t, :])
                if t:
                    copy_bank(("h2t", t - 1, 1), hT[:, 4:8, t * P - P:t * P], lambda ps: ps[:, :].rearrange("p (k n) -> p k n", k=4))
            for f in range(8):
                copy_bank(("Q", f), QT[:, f, :], scale=float(D // 4) ** -0.5)

            def bias_part(i):
                q = slice((0, 64, 96)[i], P)
                if i:
                    act.wait_ge(bias_step, 2 * i)
                act.activation(bias3[q, :], b_all[q, :], ACT.Copy).then_inc(bias_step, 1)

            for h in range(4):
                for t in range(4):
                    act.wait_ge(maxed, 4 * h + 2 * (t // 2) + 2)
                    ps = full(act, "sc", h, t // 2)
                    if h == t == 0:
                        evacuated(act, "h2t", 3, 0)
                        evacuated(act, "h2t", 3, 1)
                    act.activation(prob[:, h, t, :], ps[:, (t % 2) * M:(t % 2) * M + M], ACT.Exp,
                                   bias=soft[:, 0, 4 * h + t:4 * h + t + 1],
                                   accum_out=soft[:, 1, 4 * h + t:4 * h + t + 1]).then_inc(exped, 1)
            full(act, "sc", 3, 1)
            act.wait_ge(bias_in, 16 * 6)
            bias_part(0)
            for h in range(4):
                copy_bank(("pt", h, 1), pT[:, h, 1, :])
            bias_part(1)
            for h in range(4):
                copy_bank(("O", h, 1), mixT[:, 2 * h + 1, :])
            bias_part(2)
            for t in range(TT + 1):
                if t < TT:
                    evacuated(act, "x2", t, 0)
                    evacuated(act, "x2", t, 1)
                    if t == 0:
                        for h in range(4):
                            for m in range(2):
                                evacuated(act, "pt", h, m)
                    squares("x2", t, x_sb[:, t, :], nrm_t[:, t, :])
                if t:
                    copy_bank(("h3t", t - 1, 1), hT[:, 4:8, t * P - P:t * P], lambda ps: ps[:, :].rearrange("p (k n) -> p k n", k=4))
            for t in range(TT):
                act.wait_ge(top_ready, t + 1)
                act.activation(gate4[:, t, :], top8[:, t, 0:4], ACT.Exp, bias=gsum[:, t:t + 1],
                               accum_out=gsum[:, 4 + t:5 + t]).then_inc(gate_exp, 1)

            def x_rows(b):
                act.wait_ge(xt_full, 2 * b + 1)
                act.activation(xT[:, 0:4, :], PS[4][:, :].rearrange("p (k n) -> p k n", k=4), ACT.Copy).then_inc(xT_ready, 1)

            def a_turned(b, s):
                act.wait_ge(at_full, NSUB * b + NSUB - s)
                act.activation(aT[:, s, :, :].rearrange("p c n -> p (c n)"), PS[s][:, 0:256], ACT.Copy).then_inc(aT_ready, 1)

            x_rows(0)
            act.wait_ge(ctl_ready, 1)
            blocks = act.value_load(ctl[0:1, 1, 63:64], min_val=E, max_val=NBLK)
            with act.Fori(0, STRETCHES) as o:
                with act.If(STRETCH * o < blocks):
                    with act.Fori(0, STRETCH) as i:
                        b = STRETCH * o + i
                        with act.If(b < blocks):
                            n_sub = act.value_load(ctl[0:1, 0, bass.ds(b, 1)], min_val=0, max_val=NSUB)
                            with act.If(n_sub > 2):
                                for i, s in enumerate((3, 2)):
                                    act.wait_ge(gate_min, NSUB * b + i + 1)
                                    act.activation(sg_sb[:, s, :], gm_sb[:, s, :], ACT.Sigmoid, scale=SWIGLU_ALPHA).then_inc(sig_done, 1)
                            with act.Else():
                                for s in (3, 2):
                                    act.nop().then_inc(sig_done, 1)
                            for i, s in enumerate((1, 0)):
                                act.wait_ge(gate_min, NSUB * b + i + 3)
                                act.activation(sg_sb[:, s, :], gm_sb[:, s, :], ACT.Sigmoid, scale=SWIGLU_ALPHA).then_inc(sig_done, 1)
                            with act.If(b + 1 < blocks):
                                x_rows(b + 1)
                            with act.If(n_sub > 2):
                                a_turned(b, 3)
                                a_turned(b, 2)
                            with act.Else():
                                for s in (3, 2):
                                    act.nop().then_inc(aT_ready, 1)
                            a_turned(b, 1)
                            a_turned(b, 0)
            sqrt_table(1)
            for t in range(TT):
                act.wait_ge(final_in[t], 16)
                squares("out", t, x_sb[:, t, :], nrm_t[:, t, :])

        @block.tensor
        def _(pe):
            def bank(*job):
                n = JOB[job]
                if n >= 8:
                    pe.wait_ge(bank_free[n % 8], n // 8)
                return PS[n % 8]

            def fills(job):
                return bank_full[JOB[job] % 8]

            def turn(job, src):
                ps = bank(*job)
                for i in range(4):
                    last = pe.transpose(ps[:, i * P:(i + 1) * P], src(i), ident[:, :])
                last.then_inc(fills(job), 1)

            def product(job, lhsT, rhs, n):
                ps = bank(*job)
                for k in range(n):
                    last = pe.matmul(ps[:, :], lhsT(k), rhs(k), start=(k == 0), stop=(k == n - 1))
                return last.then_inc(fills(job), 1)

            pe.wait_ge(consts, 4)
            for t in range(TT):
                pe.wait_ge(normed, NORM["x", t] + 1)
                for h in range(2):
                    turn(("xt", t, h), lambda i: nrm_t[:, t, (4 * h + i) * P:(4 * h + i + 1) * P])
            for t in range(TT):
                for h in range(2):
                    evacuated(pe, "xt", t, h)
            pe.wait_ge(w_landed["lr"], 16)
            ps = bank("glr")
            for i in range(2):
                for j in range(4):
                    last = pe.matmul(ps[32 * j:32 * j + 32, :], w_lr[:, 4 * i + j, :], hT[:, 4 * i + j, :], start=(i == 0), stop=(i == 1))
            last.then_inc(fills(("glr",)), 1)
            pe.wait_ge(w_landed["qk"], 16)
            for n in range(2):
                product(("k", n), lambda k: w_qk[:, k, 256 + n * P:256 + (n + 1) * P], lambda k: hT[:, k, :], KD)
            for n in range(2):
                product(("q", n), lambda k: w_qk[:, k, n * P:(n + 1) * P], lambda k: hT[:, k, :], KD)
            pe.wait_ge(w_landed["v"], 16)
            for t in range(TT):
                product(("v", t), lambda k: hT[:, k, t * P:(t + 1) * P], lambda k: w_v[:, k, :], KD)
            evacuated(pe, "glr")
            pe.wait_ge(small_in, 16 * 10)
            for n in range(2):
                product(("gate", n), lambda k: w_gate[:, n * P:(n + 1) * P], lambda k: glr, 1)
            pe.wait_ge(w_landed["u"], 16)
            for g in range(4):
                product(("u", g), lambda k: w_u[:, k, g * P:(g + 1) * P], lambda k: hT[:, k, :], KD)
            pe.wait_ge(w_landed["r"], 16)
            for h in range(4):
                product(("r", h), lambda k: w_r[:, k, h * P:(h + 1) * P], lambda k: hT[:, k, :], KD)
            for t in range(2):
                pe.wait_ge(normed, NORM["mem", t] + 1)
                for h in range(2):
                    turn(("mt", t, h), lambda i: nrm_t[:, t, (4 * h + i) * P:(4 * h + i + 1) * P])
            pe.wait_ge(kd_ready, 6)
            for p in range(2):
                ps = bank("kd", p)
                for t in range(4):
                    last = pe.transpose(ps[:, t * P:(t + 1) * P], kd[:, p, t * P:(t + 1) * P], ident[:, :])
                last.then_inc(fills(("kd", p)), 1)
            for t in range(4):
                evacuated(pe, "v", t)
            for p in range(2):
                evacuated(pe, "kd", p)
                for c in range(2):
                    ps = bank("ds", p, c)
                    for t in range(4):
                        for h in range(2):
                            last = pe.matmul(ps[64 * h:64 * h + 64, t * P:(t + 1) * P],
                                             kd_tok[64 * c:64 * c + 64, p, t, 64 * h:64 * h + 64],
                                             v_sb[64 * c:64 * c + 64, t, (2 * p + h) * P:(2 * p + h + 1) * P],
                                             start=True, stop=True)
                    last.then_inc(fills(("ds", p, c)), 1)
            for g in range(4):
                pe.wait_ge(pooled, g + 1)
                product(("pool", g), lambda k: w_pool[:, g, :], lambda k: u_sb[:, g, PAD:], 1)
            for h in range(4):
                ps = bank("att", h)
                lo = 64 * (h % 2)
                for t in range(4):
                    last = pe.matmul(ps[:, t * P:(t + 1) * P], ke[lo:lo + 64, h // 2, t * P:(t + 1) * P],
                                     qe[lo:lo + 64, h // 2, t * P:(t + 1) * P], start=True, stop=True)
                last.then_inc(fills(("att", h)), 1)
            for t in range(2):
                for h in range(2):
                    evacuated(pe, "mt", t, h)
            pe.wait_ge(w_landed["w_xk"], 16)

            def keys(c):
                ps = bank("K", c)
                for f in range(2):
                    for k in range(KD):
                        last = pe.matmul(ps[:, f * M:(f + 1) * M], w_xk[:, k, (2 * c + f) * P:(2 * c + f + 1) * P], hmT[:, k, :],
                                         start=(k == 0), stop=(k == KD - 1))
                last.then_inc(fills(("K", c)), 1)

            for c in range(3):
                keys(c)
            pe.wait_ge(states, 2)
            for h in range(4):
                evacuated(pe, "att", h)
                ps = bank("o", h)
                lo = 64 * (h % 2)
                for t in range(4):
                    pe.matmul(ps[:, t * P:(t + 1) * P], v_sb[:, t, h * P:(h + 1) * P], att[:, h, t, :], start=True, stop=False)
                    for c in (2 * t, 2 * t + 1):
                        last = pe.matmul(ps[:, c * CHUNK:(c + 1) * CHUNK], S_prev[lo:lo + 64, h // 2, c, :],
                                         qe[lo:lo + 64, h // 2, c * CHUNK:(c + 1) * CHUNK], start=False, stop=(c % 2 == 1))
                last.then_inc(fills(("o", h)), 1)
            keys(3)
            for h in range(4):
                pe.wait_ge(osq_ready, h + 1)
                product(("ss", h), lambda k: ones[:, :], lambda k: pool_s[:, h % 2, 0:T], 1)
            pe.wait_ge(w_landed["w_xv"], 16)
            for m in range(2):
                for n in range(2):
                    product(("V", m, n), lambda k: hmT[:, k, m * P:(m + 1) * P], lambda k: w_xv[:, k, n * 512:(n + 1) * 512], KD)

            def residual_and_turn(product_name, turn_name, norm_name, w, behind=None):
                for t in range(TT + 1):
                    if t < TT:
                        for n in range(2):
                            product((product_name, t, n), lambda k: mixT[:, k, t * P:(t + 1) * P],
                                    lambda k: w[:, k, n * 512:(n + 1) * 512], KD)
                    if behind and 1 < t < TT:
                        behind(t - 2)
                    if t:
                        pe.wait_ge(normed, NORM[norm_name, t - 1] + 1)
                        for h in range(2):
                            turn((turn_name, t - 1, h), lambda i: nrm_t[:, t - 1, (4 * h + i) * P:(4 * h + i + 1) * P])
                if behind:
                    behind(TT - 2)

            pe.wait_ge(w_landed["w_out"], 16)
            for g in range(4):
                evacuated(pe, "pool", g)
            pe.wait_ge(mixed, 4)
            residual_and_turn("x1", "h2t", "x1", w_out)
            for t in range(TT):
                for h in range(2):
                    evacuated(pe, "h2t", t, h)
            pe.wait_ge(w_landed["w_xq"], 16)
            for f in range(8):
                product(("Q", f), lambda k: w_xq[:, k, f * P:(f + 1) * P], lambda k: hT[:, k, :], KD)
            for h in range(4):
                for f in range(2):
                    evacuated(pe, "Q", 2 * h + f)
                for b in range(2):
                    ps = bank("sc", h, b)
                    for t in (2 * b, 2 * b + 1):
                        for f in range(2):
                            last = pe.matmul(ps[:, (t % 2) * M:(t % 2) * M + M], QT[:, 2 * h + f, t * P:(t + 1) * P],
                                             KT[:, 2 * h + f, :], start=(f == 0), stop=(f == 1))
                    last.then_inc(fills(("sc", h, b)), 1)
            for h in range(4):
                pe.wait_ge(prob_ready, 4 * h + 4)
                for m in range(2):
                    ps = bank("pt", h, m)
                    for t in range(4):
                        last = pe.transpose(ps[:, t * P:(t + 1) * P], prob[:, h, t, m * P:(m + 1) * P], ident[:, :])
                    last.then_inc(fills(("pt", h, m)), 1)
            for h in range(4):
                for m in range(2):
                    evacuated(pe, "pt", h, m)
                for c in range(2):
                    product(("O", h, c), lambda m: V[:, m, (2 * h + c) * P:(2 * h + c + 1) * P], lambda m: pT[:, h, m, :], MT)
            for h in range(4):
                for c in range(2):
                    evacuated(pe, "O", h, c)
            pe.wait_ge(w_landed["w_xo"], 16)

            def router_parts(t):
                for h in range(2):
                    evacuated(pe, "h3t", t, h)
                ps = bank("lg", t)
                for i in range(2):
                    for j in range(4):
                        last = pe.matmul(ps[32 * j:32 * j + 32, 0:P], w_rt[:, 4 * i + j, :], hT[:, 4 * i + j, t * P:(t + 1) * P],
                                         start=(i == 0), stop=(i == 1))
                last.then_inc(lg_parts, 1)

            def router_sum(t):
                pe.wait_ge(lg_copied, t + 1)
                pe.matmul(PS[JOB["lg", t] % 8][:, P:P + E], lg_part_sb, stack, start=True, stop=True).then_inc(fills(("lg", t)), 1)

            def router(t):
                if t:
                    router_sum(t - 1)
                router_parts(t)

            pe.wait_ge(stack_ready, 1)
            residual_and_turn("x2", "h3t", "x2", w_xo, behind=router)
            router(TT - 1)
            router_sum(TT - 1)
            pe.wait_ge(mask_ready, 1)
            ps = bank("rank")
            for t in range(TT + 1):
                for s in range(min(t + 1, TT)):
                    last = pe.matmul(ps[:, t * E:(t + 1) * E], before[:, :] if s == t else ones_b[:, :], maskb[:, s, :],
                                     start=(s == 0), stop=(s == min(t, TT - 1)))
            last.then_inc(fills(("rank",)), 1)
            ps = bank("tab")
            for i in range(4 * TT):
                if i % 4 == 0:
                    pe.wait_ge(vals_ready, i // 4 + 1)
                last = pe.matmul(ps[:, 0:2 * NB], onehot_p[:, i, :], vals[:, i, :, :].rearrange("p c b -> p (c b)"),
                                 start=(i == 0), stop=(i == 4 * TT - 1))
            last.then_inc(fills(("tab",)), 1)
            pe.wait_ge(vals_ready, 5)
            pe.wait_ge(consts, 6)
            ps = bank("meta")
            for s in range(4):
                last = pe.matmul(ps[:, s * 2 * NB:(s + 1) * 2 * NB], spread[:, s, :], tabv.rearrange("p c b -> p (c b)"),
                                 start=True, stop=True)
            last.then_inc(fills(("meta",)), 1)

            def rows_turn(b):
                pe.wait_ge(gathered, 16 * b + 16)
                for h in range(2):
                    for i in range(4):
                        last = pe.transpose(PS[4 + h][:, i * P:(i + 1) * P], xg[:, (4 * h + i) * P:(4 * h + i + 1) * P], ident[:, :])
                    last.then_inc(xt_full, 1)

            def a_turn(b, s):
                pe.wait_ge(a_ready, NSUB * b + NSUB - s)
                for c in range(2):
                    last = pe.transpose(PS[s][:, c * P:(c + 1) * P], a_sb[:, s, c * P:(c + 1) * P], ident[:, :])
                last.then_inc(at_full, 1)

            rows_turn(0)
            pe.wait_ge(bias_step, 5)
            pe.wait_ge(ctl_ready, 1)
            blocks = pe.value_load(ctl[0:1, 1, 63:64], min_val=E, max_val=NBLK)
            evacuated(pe, "meta")
            with pe.Fori(0, STRETCHES) as o:
                with pe.If(STRETCH * o < blocks):
                    with pe.Fori(0, STRETCH) as i:
                        b = STRETCH * o + i
                        with pe.If(b < blocks):
                            n_sub = pe.value_load(ctl[0:1, 0, bass.ds(b, 1)], min_val=0, max_val=NSUB)
                            pe.wait_ge(xT_ready, 2 * b + 2)
                            pe.wait_ge(sel_ready, b + 1)

                            def gate_up(s, g):
                                for j in range(NCOL):
                                    ps = PS[s][SUB * j:SUB * (j + 1), :].rearrange("p (h n) -> p h n", h=2)
                                    if g == 0:
                                        pe.matmul(ps, sel[:, :], bias3[:, 0:2 * F].rearrange("p (h n) -> p h n", h=2)[:, :, j * FQ:(j + 1) * FQ],
                                                  start=True, stop=False)
                                for k in range(GK * g, GK * g + GK):
                                    for j in range(NCOL):
                                        ps = PS[s][SUB * j:SUB * (j + 1), :].rearrange("p (h n) -> p h n", h=2)
                                        last = pe.matmul(ps, xT[:, k, SUB * s:SUB * (s + 1)], wg[:, k, :, j * FQ:(j + 1) * FQ],
                                                         start=False, stop=(k == KD - 1))
                                return last

                            def down(s, g, buffer):
                                if g == 0:
                                    for j in range(NCOL):
                                        pe.matmul(PS[4 + s][SUB * j:SUB * (j + 1), 0:DQ], sel[:, :],
                                                  bias3[:, 2 * F + j * DQ:2 * F + (j + 1) * DQ], start=True, stop=False)
                                for k in range(GK * g, GK * g + GK):
                                    for j in range(NCOL):
                                        last = pe.matmul(PS[4 + s][SUB * j:SUB * (j + 1), 0:DQ],
                                                         aT[:, s, k % 2, SUB * (k // 2):SUB * (k // 2 + 1)],
                                                         wd[:, buffer, k, j * DQ:(j + 1) * DQ], start=False, stop=(k == KF - 1))
                                return last

                            for g in range(NG - 1):
                                pe.wait_ge(gu_in[g], 16 * b + 16)
                                for s in range(NSUB - 1, 0, -1):
                                    with pe.If(n_sub > s):
                                        gate_up(s, g)
                                gate_up(0, g).then_inc(gu_used, 1)
                            pe.wait_ge(gu_in[NG - 1], 16 * b + 16)
                            for s in range(NSUB - 1, 0, -1):
                                with pe.If(n_sub > s):
                                    gate_up(s, NG - 1).then_inc(sub_done, 1)
                                with pe.Else():
                                    pe.nop().then_inc(sub_done, 1)
                            gate_up(0, NG - 1).then_inc(gu_used, 1)
                            with pe.If(b + 1 < blocks):
                                pe.wait_ge(y_ready, NSUB * b + NSUB)
                                rows_turn(b + 1)
                            with pe.If(n_sub > 2):
                                a_turn(b, 3)
                                a_turn(b, 2)
                            with pe.Else():
                                for s in (3, 2):
                                    pe.nop().then_inc(at_full, 1)
                            a_turn(b, 1)
                            a_turn(b, 0)
                            with pe.If(b + 1 < blocks):
                                pe.wait_ge(xT_ready, 2 * b + 4)
                            pe.wait_ge(y_ready, NSUB * b + NSUB)
                            pe.wait_ge(aT_ready, NSUB * b + NSUB)

                            def down_all(buffer):
                                for g in range(NG):
                                    pe.wait_ge(dn_in[buffer][g], 8 * b + 16 - 8 * buffer)
                                    for s in range(NSUB - 1, 0, -1):
                                        with pe.If(n_sub > s):
                                            down(s, g, buffer)
                                    down(0, g, buffer).then_inc(dn_used, 1)

                            parity = pe.value_load(ctl[0:1, 2, bass.ds(b, 1)], min_val=0, max_val=1)
                            with pe.If(parity > 0):
                                down_all(1)
                            with pe.Else():
                                down_all(0)

        @block.vector
        def _(dve):
            steps = [0]

            def step(ins):
                steps[0] += 1
                ins.then_inc(dve_step, 1)
                dve.wait_ge(dve_step, steps[0])

            def norm(name, t, src, g):
                n = NORM[name, t]
                dve.wait_ge(sq_sum, n + 1)
                dve.wait_ge(g_in, 16 * (g + 1))
                step(dve.reciprocal(stat[:, 2, n:n + 1], stat[:, 1, n:n + 1]))
                return dve.scalar_tensor_tensor(out=nrm_t[:, t, :], in0=src, scalar=stat[:, 2, n:n + 1], in1=gbc[:, :],
                                                op0=ALU.mult, op1=ALU.mult).then_inc(normed, 1)

            def copy_bank(job, dst, src=None):
                ps = full(dve, *job)
                dve.tensor_copy(dst, ps[:, :] if src is None else src(ps)).then_inc(freed(job), 1)

            def gains_used(n):
                dve.wait_ge(normed, n)
                dve.engine_nop().then_inc(g_used, 1)

            step(dve.memset(pool_s[:, :, 0:PAD], 0.0))
            step(dve.memset(u_sb[:, :, 0:PAD], 0.0))
            dve.memset(w_lr[:, :, 16:32], 0.0).then_inc(cleared, 1)
            dve.memset(w_gate[:, :], 0.0).then_inc(cleared, 1)
            for t in range(TT):
                norm("x", t, x_sb[:, t, :], 0)
            gains_used(TT)
            for t in range(TT):
                copy_bank(("xt", t, 0), hT[:, 0:4, t * P:t * P + P], lambda ps: ps[:, :].rearrange("p (k n) -> p k n", k=4))
            for t in range(MT):
                norm("mem", t, V[:, t, :], 1)
            gains_used(TT + MT)
            copy_bank(("k", 0), kg[:, 0, :])
            ps = full(dve, "q", 0)
            dve.tensor_scalar(qg[:, 0, :], ps[:, :], float(CHUNK) ** -0.5, None, ALU.mult).then_inc(freed(("q", 0)), 1)
            copy_bank(("v", 0), v_sb[:, 0, :])
            copy_bank(("v", 2), v_sb[:, 2, :])
            dve.wait_ge(small_in, 16 * 10)
            for p in range(2):
                ps = full(dve, "gate", p)
                dve.wait_ge(consts, 4)
                step(dve.tensor_scalar(gc[:, p, :], ps[:, :], cols[:, 4 + p:5 + p], None, ALU.add))
                dve.scalar_tensor_tensor(out=gtmp[:, p, :], in0=gc[:, p, :], scalar=-1.0, in1=gc[:, p, :],
                                         op0=ALU.mult, op1=ALU.max).then_inc(gate_dve, 1)
                dve.wait_ge(gate_dve, 2 * p + 1)
                dve.tensor_scalar(gc[:, p, :], gc[:, p, :], 0.0, None, ALU.min).then_inc(gate_dve, 1)
                dve.wait_ge(gate_dve, 2 * p + 2)
                dve.engine_nop().then_inc(freed(("gate", p)), 1)
            keep = pool_s[:, 0, PAD:PAD + T]
            step(dve.memset(keep, 1.0))
            step(dve.memset(keep.rearrange("p (c i) -> p c i", i=CHUNK)[:, :, 0:1], 0.0))
            for p in range(2):
                dve.wait_ge(gate_logs, p + 1)
                step(dve.tensor_tensor(gtmp[:, p, :], gc[:, p, :], gtmp[:, p, :], ALU.subtract))
                step(dve.tensor_scalar(gtmp[:, p, :], gtmp[:, p, :], 1.0 / GATE_NORMALIZER, None, ALU.mult))
                dve.tensor_tensor_scan(gc[:, p, :], keep, gtmp[:, p, :], 0.0, ALU.mult, ALU.add).then_inc(gate_dve, 1)
            for p in range(2):
                base = 2 + 10 * p
                evacuated(dve, "q", p)
                evacuated(dve, "k", p)
                dve.wait_ge(gate_logs, base + 10)
                for dst, src in ((qe, qg), (ke, kg), (kd, kg)):
                    if dst is qe:
                        step(dve.tensor_copy(soft[:, 2 + p, 0:8],
                                             qe[:, p, :].rearrange("p (c i) -> p c i", i=CHUNK)[:, :, CHUNK - 1]))
                    dve.tensor_tensor(dst[:, p, :], dst[:, p, :], src[:, p, :], ALU.mult).then_inc(kd_ready, 1)
            for g in (0, 2):
                copy_bank(("u", g), u_sb[:, g, PAD:])
            for g, w in enumerate(WINDOWS):
                evacuated(dve, "u", g)
                src, n = u_sb[:, g, :], 1
                i = 0
                while n < w:
                    dst = pool_s[:, i % 2, :]
                    step(dve.tensor_tensor(dst[:, PAD:], src[:, PAD:], src[:, PAD - n:PAD + T - n], ALU.add))
                    src, n, i = dst, 2 * n, i + 1
                step(dve.tensor_tensor(soft[:, 1, 0:w], src[:, PAD:PAD + w], inv_cnt[:, 0:w], ALU.mult))
                step(dve.tensor_tensor(soft[:, 1, 0:w], soft[:, 1, 0:w], u_sb[:, g, PAD:PAD + w], ALU.subtract))
                step(dve.scalar_tensor_tensor(out=u_sb[:, g, PAD:], in0=src[:, PAD:], scalar=1.0 / w, in1=u_sb[:, g, PAD:],
                                              op0=ALU.mult, op1=ALU.subtract))
                dve.tensor_copy(u_sb[:, g, PAD:PAD + w], soft[:, 1, 0:w]).then_inc(pooled, 1)
                dve.wait_ge(pooled, g + 1)
            for t in range(2):
                for m in range(2):
                    evacuated(dve, "xt", 3, m)
                copy_bank(("mt", t, 0), hmT[:, 0:4, t * P:t * P + P], lambda ps: ps[:, :].rearrange("p (k n) -> p k n", k=4))
            copy_bank(("kd", 0), kd_tok[:, 0, :, :].rearrange("p t d -> p (t d)"))
            evacuated(dve, "r", 3)
            step(dve.memset(att.rearrange("p h t i -> p (h t i)"), 0.0))
            for p in range(2):
                even, odd = full(dve, "ds", p, 0), full(dve, "ds", p, 1)
                step(dve.memset(S_prev[:, p, 0, :], 0.0))
                for c in range(7):
                    src = (even, odd)[c % 2][:, (c // 2) * P:(c // 2 + 1) * P]
                    step(dve.scalar_tensor_tensor(out=S_prev[:, p, c + 1, :], in0=S_prev[:, p, c, :],
                                                  scalar=soft[:, 2 + p, c:c + 1], in1=src, op0=ALU.mult, op1=ALU.add))
                dve.engine_nop().then_inc(freed(("ds", p, 0)), 1)
                dve.engine_nop().then_inc(freed(("ds", p, 1)), 1)
                dve.engine_nop().then_inc(states, 1)
            for h in range(4):
                ps = full(dve, "att", h)
                for t in range(4):
                    last = dve.copy_predicated(att[:, h, t, :], causal[:, :].bitcast(U32), ps[:, t * P:(t + 1) * P])
                    if t < 3:
                        step(last)
                last.then_inc(freed(("att", h)), 1)
            for h in range(4):
                if h == 0:
                    for t in range(2):
                        evacuated(dve, "mt", t, 0)
                        evacuated(dve, "mt", t, 1)
                copy_bank(("o", h), o_sb[:, h, :])
            for h in range(4):
                dve.wait_ge(sig_ready, h + 1)
                step(dve.tensor_tensor(sig_r[:, h, :], sig_r[:, h, :], mixT[:, 4 + h, :], ALU.mult))
                step(dve.scalar_tensor_tensor(out=sig_r[:, h, :], in0=o_sb[:, h, :], scalar=cols[:, 6:7], in1=sig_r[:, h, :],
                                              op0=ALU.mult, op1=ALU.mult))
                evacuated(dve, "ss", h)
                step(dve.reciprocal(gc[:, 1, :], gc[:, 0, :]))
                dve.tensor_tensor(mixT[:, 4 + h, :], sig_r[:, h, :], gc[:, 1, :], ALU.mult).then_inc(mixed, 1)
                dve.wait_ge(mixed, h + 1)

            def residual(job, t, n):
                ps = full(dve, *job)
                dve.tensor_tensor(x_sb[:, t, n * 512:(n + 1) * 512], x_sb[:, t, n * 512:(n + 1) * 512], ps[:, :],
                                  ALU.add).then_inc(freed(job), 1)

            for m in range(2):
                copy_bank(("V", m, 0), V[:, m, 0:512])

            def residual_and_norm(product_name, turn_name, norm_name, g, behind=None):
                for t in range(TT + 1):
                    if t < TT:
                        for n in range(2):
                            residual((product_name, t, n), t, n)
                    if t:
                        copy_bank((turn_name, t - 1, 0), hT[:, 0:4, t * P - P:t * P], lambda ps: ps[:, :].rearrange("p (k n) -> p k n", k=4))
                    if t < TT:
                        norm(norm_name, t, x_sb[:, t, :], g)
                    if behind and t > 1:
                        behind(t - 2)

            residual_and_norm("x1", "h2t", "x1", 2)
            gains_used(2 * TT + MT)
            for h in range(4):
                for t in range(4):
                    ps = full(dve, "sc", h, t // 2)
                    dve.tensor_reduce(soft[:, 0, 4 * h + t:4 * h + t + 1], ps[:, (t % 2) * M:(t % 2) * M + M], AX.X, ALU.max,
                                      negate=True).then_inc(maxed, 1)
                for t in range(4):
                    i = 4 * h + t
                    dve.wait_ge(exped, i + 1)
                    step(dve.reciprocal(soft[:, 2, i:i + 1], soft[:, 1, i:i + 1]))
                    dve.tensor_scalar(prob[:, h, t, :], prob[:, h, t, :], soft[:, 2, i:i + 1], None, ALU.mult).then_inc(prob_ready, 1)
                    if t % 2:
                        dve.engine_nop().then_inc(freed(("sc", h, t // 2)), 1)

            def bias_rest(i):
                q = slice((64, 96)[i], P)
                dve.wait_ge(bias_step, 2 * i + 1)
                dve.tensor_tensor(b_all[q, :], b_all[q, :], bias3[q, :], ALU.subtract).then_inc(bias_step, 1)

            for h in range(4):
                copy_bank(("pt", h, 0), pT[:, h, 0, :])
            bias_rest(0)
            for h in range(4):
                copy_bank(("O", h, 0), mixT[:, 2 * h, :])
            dve.wait_ge(consts, 5)
            dve.tensor_scalar(stack, iota_e, row_e[:, 0:1], None, ALU.is_equal).then_inc(stack_ready, 1)
            bias_rest(1)
            def top_four(t):
                ps = full(dve, "lg", t)
                dve.tensor_tensor(logits[:, t, :], ps[:, P:P + E], b_rt[:, :], ALU.add).then_inc(freed(("lg", t)), 1)
                evacuated(dve, "lg", t)
                step(dve.max(top8[:, t, :], logits[:, t, :]))
                dve.tensor_scalar(gsum[:, t:t + 1], top8[:, t, 0:1], -1.0, None, ALU.mult).then_inc(top_ready, 1)
                step(dve.max_index(idx8[:, t, :], top8[:, t, :], logits[:, t, :]))

            def router(t):
                if t:
                    top_four(t - 1)
                dve.wait_ge(lg_parts, t + 1)
                dve.tensor_copy(lg_part_sb, PS[JOB["lg", t] % 8][:, 0:P]).then_inc(lg_copied, 1)

            residual_and_norm("x2", "h3t", "x2", 3, behind=router)
            gains_used(3 * TT + MT)
            router(TT - 1)
            top_four(TT - 1)

            step(dve.tensor_copy(idxf, idx8[:, :, 0:4].rearrange("p t k -> p k t")))
            iota_kte = iota_e.rearrange("p (k t e) -> p k t e", k=1, t=1).to_broadcast([P, 4, TT, E])
            step(dve.tensor_tensor(oh, iota_kte, idxf.rearrange("p k (t o) -> p k t o", o=1).to_broadcast([P, 4, TT, E]), ALU.is_equal))
            step(dve.tensor_tensor(prod[:, 0:2], oh[:, 0:2], oh[:, 2:4], ALU.add))
            dve.tensor_tensor(maskb, prod[:, 0], prod[:, 1], ALU.add).then_inc(mask_ready, 1)
            dve.wait_ge(gate_exp, TT)
            step(dve.reciprocal(gsum[:, 4:8], gsum[:, 4:8]))
            step(dve.tensor_tensor(gate4, gate4, gsum[:, 4:8].rearrange("p (t o) -> p t o", o=1).to_broadcast([P, TT, 4]), ALU.mult))
            ps = full(dve, "rank")
            dve.tensor_copy(rank.rearrange("p t e -> p (t e)"), ps[:, 0:5 * E]).then_inc(freed(("rank",)), 1)
            evacuated(dve, "rank")
            cnt, rk = rank[:, 4, :], rank[:, 0:4, :]
            step(dve.tensor_scalar(more[:, :], cnt, float(P), None, ALU.is_gt))
            for i in (2, 3):
                step(dve.scalar_tensor_tensor(out=more[:, :], in0=cnt, scalar=float(i * P), in1=more[:, :], op0=ALU.is_gt, op1=ALU.add))
            step(dve.tensor_tensor_scan(xend[:, :], one_e[:, :], more[:, :], 0.0, ALU.mult, ALU.add))
            step(dve.tensor_tensor(xoff[:, :], xend[:, :], more[:, :], ALU.subtract))
            step(dve.scalar_tensor_tensor(out=xoff[:, :], in0=xoff[:, :], scalar=float(E - 1), in1=iota_e, op0=ALU.add, op1=ALU.subtract))
            for dst, src in ((pos16, rk.rearrange("p (o t) e -> p o t e", o=1)),
                             (blk16, xoff.rearrange("p (o t e) -> p o t e", o=1, t=1))):
                step(dve.tensor_tensor(prod, oh, src.to_broadcast([P, 4, TT, E]), ALU.mult))
                step(dve.tensor_reduce(dst, prod, AX.X, ALU.add))
            step(dve.tensor_scalar(full1, pos16, float(P), None, ALU.is_ge))
            step(dve.scalar_tensor_tensor(out=level, in0=pos16, scalar=float(2 * P), in1=full1, op0=ALU.is_ge, op1=ALU.add))
            step(dve.scalar_tensor_tensor(out=level, in0=pos16, scalar=float(3 * P), in1=level, op0=ALU.is_ge, op1=ALU.add))
            step(dve.tensor_tensor(blk16, blk16, full1, ALU.mult))
            step(dve.tensor_tensor(blk16, blk16, idxf, ALU.add))
            step(dve.tensor_tensor(blk16, blk16, level, ALU.add))
            step(dve.scalar_tensor_tensor(out=pos16, in0=level, scalar=-float(P), in1=pos16, op0=ALU.mult, op1=ALU.add))
            vals4 = vals.rearrange("p (k t) c b -> p k t c b", k=4)
            for k in range(4):
                step(dve.tensor_tensor(inblk[:, k], iota_b.rearrange("p (t b) -> p t b", t=1).to_broadcast([P, TT, NB]),
                                       blk16[:, k, :].rearrange("p (t o) -> p t o", o=1).to_broadcast([P, TT, NB]), ALU.is_equal))
                step(dve.tensor_tensor(vals4[:, k, :, 0, :], inblk[:, k], tokp.rearrange("p (t b) -> p t b", b=1).to_broadcast([P, TT, NB]), ALU.mult))
                step(dve.tensor_tensor(vals4[:, k, :, 1, :], inblk[:, k],
                                       gate4[:, :, k].rearrange("p (t b) -> p t b", b=1).to_broadcast([P, TT, NB]), ALU.mult))
                dve.tensor_tensor(onehot_p[:, TT * k:TT * k + TT, :], iota_p.rearrange("p (t s) -> p t s", t=1).to_broadcast([P, TT, P]),
                                  pos16[:, k, :].rearrange("p (t s) -> p t s", s=1).to_broadcast([P, TT, P]), ALU.is_equal).then_inc(vals_ready, 1)
            step(dve.tensor_scalar(nsubf[:, 0:E], cnt, 0.0, None, ALU.is_gt))
            for i in range(1, NSUB):
                step(dve.scalar_tensor_tensor(out=nsubf[:, 0:E], in0=cnt, scalar=float(i * SUB), in1=nsubf[:, 0:E], op0=ALU.is_gt, op1=ALU.add))
            step(dve.memset(nsubf[:, E:NB], float(NSUB)))
            ps = full(dve, "tab")
            dve.tensor_copy(tabv.rearrange("p c b -> p (c b)"), ps[:, 0:2 * NB]).then_inc(vals_ready, 1)
            dve.wait_ge(vals_ready, 5)
            step(dve.tensor_scalar(gidx, tabv[:, 0, :], 0.0, BEYOND, ALU.is_equal, ALU.mult))
            dve.scalar_tensor_tensor(out=gidx, in0=tabv[:, 0, :], scalar=-1.0, in1=gidx, op0=ALU.add, op1=ALU.add).then_inc(freed(("tab",)), 1)
            evacuated(dve, "tab")

            def pick_row(b):
                dve.tensor_scalar(cur_i[:, 0:1], gidx_next[:, bass.ds(b, 1)], 0.0, None, ALU.add).then_inc(row_picked, 1)

            def pick_bias(b):
                dve.tensor_scalar(sel[:, :], ebc_next[:, bass.ds(b, 1)].to_broadcast([P, SUB]), row_e[:, 0:1], None,
                                  ALU.is_equal).then_inc(sel_ready, 1)

            pick_row(0)
            step(dve.tensor_copy(ebc[:, 0:E], iota_e[:, :]))
            xsum = inblk.rearrange("p k t b -> p (k t b)")[:, 0:(NB - E) * E].rearrange("p (i e) -> p i e", e=E)
            step(dve.tensor_tensor(xsum, xend.rearrange("p (i e) -> p i e", i=1).to_broadcast([P, NB - E, E]),
                                   iota_b[:, 0:NB - E].rearrange("p (i e) -> p i e", e=1).to_broadcast([P, NB - E, E]), ALU.is_le))
            step(dve.tensor_reduce(ebc[:, E:NB], xsum, AX.X, ALU.add))
            step(dve.tensor_scalar(ebc[:, :], ebc[:, :], float(E - 1), None, ALU.min))
            step(dve.tensor_copy(ctl[0:1, 0, 0:NB], nsubf[0:1, 0:NB]))
            step(dve.tensor_copy(ctl[0:1, 1, 0:NB], ebc[0:1, 0:NB]))
            parities = ctl[0:1, 2, :].rearrange("o (i a) -> o i a", a=2)
            for i in range(2):
                step(dve.memset(parities[:, :, i], i))
            step(dve.tensor_scalar(ctl[0:1, 1, 63:64], xend[0:1, E - 1:E], float(E), None, ALU.add))
            dve.engine_nop().then_inc(ctl_ready, 1)
            pick_bias(0)
            ps = full(dve, "meta")
            dve.tensor_copy(meta.rearrange("p s c b -> p (s c b)"), ps[:, 0:8 * NB]).then_inc(freed(("meta",)), 1)
            evacuated(dve, "meta")
            row = meta[:, :, 0, :]
            empty = inblk.rearrange("p k t b -> p (k t) b")[:, 0:NSUB, :]
            step(dve.tensor_scalar(empty, row, 0.0, BEYOND, ALU.is_equal, ALU.mult))
            step(dve.scalar_tensor_tensor(out=row, in0=row, scalar=float(NCOL), in1=empty, op0=ALU.mult, op1=ALU.add))
            step(dve.tensor_scalar(row, row, jcol[:, 0:1], None, ALU.add))

            blocks = dve.value_load(ctl[0:1, 1, 63:64], min_val=E, max_val=NBLK)

            def swiglu(b, s, i):
                dve.tensor_scalar(gm_sb[:, s, :], PS[s][:, 0:FQ], SWIGLU_LIMIT, None, ALU.min).then_inc(gate_min, 1)
                dve.tensor_scalar(up_sb[:, s, :], PS[s][:, FQ:2 * FQ], SWIGLU_LIMIT, -SWIGLU_LIMIT, ALU.min, ALU.max).then_inc(moe_step, 1)
                dve.wait_ge(gate_min, NSUB * b + i + 1)
                dve.wait_ge(moe_step, PER * b + 2 * i + 1)
                dve.scalar_tensor_tensor(out=up_sb[:, s, :], in0=up_sb[:, s, :], scalar=1.0, in1=gm_sb[:, s, :],
                                         op0=ALU.add, op1=ALU.mult).then_inc(moe_step, 1)
                dve.wait_ge(moe_step, PER * b + 2 * i + 2)
                dve.wait_ge(sig_done, NSUB * b + i + 1)
                dve.tensor_tensor(a_sb[:, s, :], up_sb[:, s, :], sg_sb[:, s, :], ALU.mult).then_inc(a_ready, 1)

            def x_rows(b):
                dve.wait_ge(xt_full, 2 * b + 2)
                dve.tensor_copy(xT[:, 4:8, :], PS[5][:, :].rearrange("p (k n) -> p k n", k=4)).then_inc(xT_ready, 1)

            def scale(s):
                dve.tensor_scalar(y_sb[:, s, :], PS[4 + s][:, 0:DQ], cur_g[:, s:s + 1], None, ALU.mult).then_inc(y_ready, 1)

            PER = 2 * NSUB + 2
            for s in range(NSUB):
                dve.engine_nop().then_inc(y_ready, 1)
            x_rows(0)
            with dve.Fori(0, STRETCHES) as o:
                with dve.If(STRETCH * o < blocks):
                    with dve.Fori(0, STRETCH) as i:
                        b = STRETCH * o + i
                        with dve.If(b < blocks):
                            n_sub = dve.value_load(ctl[0:1, 0, bass.ds(b, 1)], min_val=0, max_val=NSUB)
                            dve.wait_ge(gathered, 16 * b + 16)
                            pick_row(b + 1)
                            with dve.If(n_sub > 2):
                                dve.wait_ge(sub_done, 3 * b + 1)
                                swiglu(b, 3, 0)
                                dve.wait_ge(sub_done, 3 * b + 2)
                                swiglu(b, 2, 1)
                            with dve.Else():
                                for s in (3, 2):
                                    dve.engine_nop().then_inc(gate_min, 1)
                                    dve.engine_nop().then_inc(moe_step, 1)
                                    dve.engine_nop().then_inc(moe_step, 1)
                                    dve.engine_nop().then_inc(a_ready, 1)
                            dve.wait_ge(sub_done, 3 * b + 3)
                            swiglu(b, 1, 2)
                            dve.wait_ge(gu_used, NG * b + NG)
                            swiglu(b, 0, 3)
                            with dve.If(b + 1 < blocks):
                                x_rows(b + 1)
                            dve.wait_ge(block_added, b + 1)
                            dve.tensor_scalar(cur_i[:, 4:4 + NSUB], meta[:, :, 0, bass.ds(b, 1)].rearrange("p s o -> p (s o)"),
                                              0.0, None, ALU.add).then_inc(moe_step, 1)
                            dve.tensor_scalar(cur_g[:, :], meta[:, :, 1, bass.ds(b, 1)].rearrange("p s o -> p (s o)"),
                                              0.0, None, ALU.add).then_inc(moe_step, 1)
                            dve.wait_ge(dn_used, NG * b + 1)
                            pick_bias(b + 1)
                            dve.wait_ge(moe_step, PER * b + PER)
                            dve.wait_ge(dn_used, NG * b + NG)
                            scale(0)
                            scale(1)
                            with dve.If(n_sub > 2):
                                scale(2)
                                scale(3)
                            with dve.Else():
                                for s in (2, 3):
                                    dve.engine_nop().then_inc(y_ready, 1)
            for t in range(TT):
                norm("out", t, x_sb[:, t, :], 4)

        @block.gpsimd
        def _(pool):
            steps = [0]

            def step(ins, s=pool_step):
                steps[0] += 1
                ins.then_inc(pool_step, 1)
                pool.wait_ge(pool_step, steps[0])

            step(pool.memset(eps_c[:, :], EPS))
            step(pool.memset(ident[:, :], 0.0))
            pool.affine_select(out=ident[:, :], in_=ident[:, :], compare_op=ALU.not_equal, fill=1.0, base=0,
                               pattern=[[-1, P]], channel_multiplier=1).then_inc(consts, 1)
            step(pool.memset(ones[:, :], 1.0 / P))
            step(pool.memset(ones_b[:, :], 1.0))
            step(pool.memset(before[:, :], 1.0))
            pool.affine_select(out=before[:, :], in_=before[:, :], compare_op=ALU.is_gt, fill=0.0, base=0,
                               pattern=[[1, P]], channel_multiplier=-1).then_inc(consts, 1)
            step(pool.memset(causal[:, :], 1.0))
            step(pool.affine_select(out=causal[:, :], in_=causal[:, :], compare_op=ALU.is_ge, fill=0.0, base=0,
                                    pattern=[[1, P]], channel_multiplier=-1))
            pool.memset(causal[0:64, 64:128], 0.0).then_inc(consts, 1)
            for t in range(PAD):
                step(pool.memset(inv_cnt[:, t:t + 1], 1.0 / (t + 1)))
            pool.nop().then_inc(consts, 1)

            full(pool, "V", 1, 1)
            step(pool.memset(b_all[32:64, :], 0.0))
            for i in (0, 2, 3):
                q = slice(32 * i, 32 * i + 32)
                pool.dma_start(b_all[q, 0:2 * F], a["b_gu"][0]).then_inc(bias_in, 16)
                pool.dma_start(b_all[q, 2 * F:2 * F + D], a["b_dn"][0]).then_inc(bias_in, 16)

            for h in range(4):
                evacuated(pool, "sc", h, 1)
            step(pool.iota(iota_e[:, :], pattern=[[1, E]], base=0, channel_multiplier=0, allow_small_or_imprecise_dtypes=True))
            step(pool.iota(iota_b[:, :], pattern=[[1, NB]], base=0, channel_multiplier=0, allow_small_or_imprecise_dtypes=True))
            step(pool.iota(iota_p[:, :], pattern=[[1, P]], base=0, channel_multiplier=0, allow_small_or_imprecise_dtypes=True))
            step(pool.iota(tokp[:, :], pattern=[[P, 4]], base=1, channel_multiplier=1, allow_small_or_imprecise_dtypes=True))
            step(pool.iota(pcol[:, 0:1], pattern=[[0, 1]], base=0, channel_multiplier=1, allow_small_or_imprecise_dtypes=True))
            for j in range(4):
                q = slice(32 * j, 32 * j + 32)
                step(pool.tensor_scalar(row_e[q, 0:1], pcol[q, 0:1], float(-32 * j), None, ALU.add))
                step(pool.memset(jcol[q, 0:1], float(j - NCOL)))
            step(pool.memset(one_e[:, :], 1.0))
            pool.nop().then_inc(consts, 1)
            for t in range(TT):
                pool.wait_ge(normed, NORM["x2", t] + 1)
                pool.dma_start(h3_tok[:, t, :], nrm_t[:, t, :]).then_inc(h3_out, 16)
                pool.dma_start(acc_tok[:, t, :], x_sb[:, t, :]).then_inc(added, 16)
            full(pool, "x2", 3, 1)
            step(pool.memset(spread.rearrange("p s q -> p (s q)"), 0.0))
            for s in range(NSUB):
                part = spread[:, s, :].rearrange("p (j r) -> p j r", j=4)
                step(pool.affine_select(out=part, in_=part, compare_op=ALU.not_equal, fill=1.0, base=-SUB * s,
                                        pattern=[[0, 4], [-1, SUB]], channel_multiplier=1))
            pool.nop().then_inc(consts, 1)

            pool.wait_ge(h3_out, 16 * TT)
            pool.wait_ge(added, 16 * TT)
            gathered_end, added_end = pool.alloc_register("gathered_end"), pool.alloc_register("added_end")
            pool.reg_mov(gathered_end, 16)
            pool.reg_mov(added_end, 16 * TT)

            def gather(rows):
                pool.indirect_dma_start(xg[0:rows], None, h3_d, bass.IndirectOffsetOnAxis(ap=cur_i[0:rows, 0:1], axis=0),
                                        bounds_check=T - 1, oob_is_err=False).then_inc(gathered, 16)

            def gather_next(b, rows):
                pool.wait_ge(row_picked, b + 2)
                pool.wait_ge(xt_full, 2 * b + 2)
                pool.reg_add(gathered_end, gathered_end, 16)
                gather(rows)

            pool.wait_ge(row_picked, 1)
            gather(P)
            pool.wait_ge(ctl_ready, 1)
            blocks = pool.value_load(ctl[0:1, 1, 63:64], min_val=E, max_val=NBLK)
            with pool.Fori(0, STRETCHES) as o:
                with pool.If(STRETCH * o < blocks):
                    with pool.Fori(0, STRETCH) as i:
                        b = STRETCH * o + i
                        with pool.If(b < blocks):
                            n_sub = pool.value_load(ctl[0:1, 0, bass.ds(b, 1)], min_val=0, max_val=NSUB)
                            n_next = pool.value_load(ctl[0:1, 0, bass.ds(b + 1, 1)], min_val=0, max_val=NSUB)
                            with pool.If(n_next > 3):
                                gather_next(b, P)
                            with pool.Else():
                                with pool.If(n_next > 2):
                                    gather_next(b, 3 * SUB)
                                with pool.Else():
                                    gather_next(b, 2 * SUB)
                            pool.wait_ge(added, pool.snap(added_end))
                            pool.nop().then_inc(block_added, 1)
                            for s in range(NSUB):
                                with pool.If(n_sub > s):
                                    pool.wait_ge(y_ready, NSUB * b + NSUB + s + 1)
                                    pool.reg_add(added_end, added_end, 16)
                                    pool.indirect_dma_start(acc_d, bass.IndirectOffsetOnAxis(ap=cur_i[:, 4 + s:5 + s], axis=0), y_sb[:, s, :], None,
                                                            bounds_check=T * NCOL - 1, oob_is_err=False, compute_op=ALU.add).then_inc(added, 16)
            gathered_all, added_all = pool.snap(gathered_end), pool.snap(added_end)
            pool.wait_ge(gathered, gathered_all)
            pool.tensor_tensor(pool_end[0:1, 0:1], eps_c[0:1, 0:1], eps_c[0:1, 0:1], ALU.add)
            pool.wait_ge(added, added_all)
            pool.tensor_tensor(pool_end[0:1, 1:2], eps_c[0:1, 0:1], eps_c[0:1, 0:1], ALU.add).then_inc(all_added, 1)



_INS = ["x", "mem", "norm_mix_g", "w_in", "w_pool", "pool_scale", "w_gate_up", "b_gate_up", "gla_norm_g", "w_out",
        "norm_xattn_g", "norm_mem_g", "w_xq", "w_xk", "w_xv", "w_xo", "norm_moe_g", "w_router", "b_router",
        "w_gu", "b_gu", "w_dn", "b_dn", "norm_final_g"]


def kernel(**inputs):
    import numpy as _np
    import concourse.bacc as _bacc
    from concourse import mybir as _mybir
    from concourse.bass_utils import run_bass_kernel_spmd as _run

    nc = _bacc.Bacc("TRN2", target_bir_lowering=False, num_devices=1)
    arrays, aps = {}, {}
    for name in _INS:
        arr = _np.ascontiguousarray(inputs[name])
        arrays[f"in_{name}"] = arr
        aps[name] = nc.dram_tensor(f"in_{name}", arr.shape, _mybir.dt.from_np(arr.dtype), kind="ExternalInput").ap()
    out = nc.dram_tensor("out_0", inputs["x"].shape, _mybir.dt.float32, kind="ExternalOutput").ap()
    decoder_layer(nc, aps, out)
    r = _run(nc, [arrays], core_ids=[0])
    return r.results[0]["out_0"]
```
